# Optimizing a Trainium2 kernel written in Bass

```python
import math
import jax, jax.numpy as jnp
from jax import lax
import numpy as np

D_MODEL = 1024
BATCH = 1
SEQ = 512
DEPTH = 1

CHUNK = 64
N_MEM = 256
MIX_WIDTH = D_MODEL
M_WIDTH = MIX_WIDTH // 2
M_HEADS = 4
M_HDIM = M_WIDTH // M_HEADS
M_CONV = 4
F_BIAS_LO = 3.0
F_BIAS_HI = 6.0
R_WIDTH = MIX_WIDTH - M_WIDTH
R_HDIM = 64
R_HEADS = R_WIDTH // R_HDIM
R_DECAY_LORA = 64
R_AAA_LORA = 64
R_GATE_LORA = 160
DECAY_SCALE = math.exp(-0.5)
X_HEADS = 4
X_HDIM = D_MODEL // X_HEADS
D_FF = 2816
FFN_CONV = 3
NORM_EPS = 1e-6
GN_EPS = 64e-5
M_COLS = 4 * M_WIDTH + 2 * M_HEADS
R_COLS = 3 * R_WIDTH + R_DECAY_LORA + R_AAA_LORA + R_GATE_LORA
IN_COLS = M_COLS + R_COLS


def rmsnorm(x, g, eps=NORM_EPS):
    xf = x.astype(jnp.float32)
    y = xf * lax.rsqrt(jnp.mean(xf * xf, -1, keepdims=True) + eps)
    return (y * g.astype(jnp.float32)).astype(x.dtype)

def standardize_heads(y, eps):
    yf = y.astype(jnp.float32)
    mu = jnp.mean(yf, -1, keepdims=True)
    var = jnp.mean(jnp.square(yf - mu), -1, keepdims=True)
    return (yf - mu) * lax.rsqrt(var + eps)

def causal_dwconv(x, w, b):
    width = w.shape[0]
    seq = x.shape[1]
    xp = jnp.pad(x, ((0, 0), (width - 1, 0), (0, 0)))
    y = b
    for j in range(width):
        y = y + xp[:, j:j + seq] * w[j]
    return y

def token_shift(p, mu):
    prev = jnp.pad(p, ((0, 0), (1, 0), (0, 0)))[:, :-1]
    return p + (prev - p) * mu

def mlstm_chunkwise(q, k, v, i_pre, f_pre):
    B, H, S, dh = q.shape
    nc = S // CHUNK
    f32 = jnp.float32
    q = q.astype(f32).reshape(B, H, nc, CHUNK, dh) * (dh ** -0.5)
    k = k.astype(f32).reshape(B, H, nc, CHUNK, dh)
    v = v.astype(f32).reshape(B, H, nc, CHUNK, dh)
    logi = i_pre.astype(f32).reshape(B, H, nc, CHUNK)
    logf = jax.nn.log_sigmoid(f_pre.astype(f32)).reshape(B, H, nc, CHUNK)
    b = jnp.cumsum(logf, -1)
    g = b[..., -1]
    a = g[..., None] - b + logi
    m_loc = jnp.max(a, -1)
    wa = jnp.exp(a - m_loc[..., None])
    c_loc = jnp.einsum('bhclv,bhclk->bhcvk', v * wa[..., None], k)
    n_loc = jnp.einsum('bhcl,bhclk->bhck', wa, k)

    def step(carry, inp):
        c, n, m = carry
        g_c, m_l, c_l, n_l = inp
        m_new = jnp.maximum(g_c + m, m_l)
        s_old = jnp.exp(g_c + m - m_new)
        s_loc = jnp.exp(m_l - m_new)
        c_new = s_old[..., None, None] * c + s_loc[..., None, None] * c_l
        n_new = s_old[..., None] * n + s_loc[..., None] * n_l
        return (c_new, n_new, m_new), (c, n, m)

    init = (jnp.zeros((B, H, dh, dh), f32), jnp.zeros((B, H, dh), f32), jnp.zeros((B, H), f32))
    xs = (jnp.moveaxis(g, 2, 0), jnp.moveaxis(m_loc, 2, 0),
          jnp.moveaxis(c_loc, 2, 0), jnp.moveaxis(n_loc, 2, 0))
    _, (c_prev, n_prev, m_prev) = lax.scan(step, init, xs)
    c_prev = jnp.moveaxis(c_prev, 0, 2)
    n_prev = jnp.moveaxis(n_prev, 0, 2)
    m_prev = jnp.moveaxis(m_prev, 0, 2)

    inter = b + m_prev[..., None]
    causal = jnp.tril(jnp.ones((CHUNK, CHUNK), dtype=bool))
    d = jnp.where(causal, b[..., :, None] - b[..., None, :] + logi[..., None, :], -jnp.inf)
    m_t = jnp.maximum(inter, jnp.max(d, -1))
    s_int = jnp.exp(inter - m_t)
    p = jnp.exp(d - m_t[..., None]) * jnp.einsum('bhctd,bhcsd->bhcts', q, k)
    num = (s_int[..., None] * jnp.einsum('bhcvk,bhctk->bhctv', c_prev, q)
           + jnp.einsum('bhcts,bhcsv->bhctv', p, v))
    den = s_int * jnp.einsum('bhck,bhctk->bhct', n_prev, q) + jnp.sum(p, -1)
    h = num / jnp.maximum(jnp.abs(den), jnp.exp(-m_t))[..., None]
    return h.reshape(B, H, S, dh)

def rwkv7_scan(r, w, k, v, kk, a):
    B, S, H, N = r.shape

    def step(state, inp):
        r_t, w_t, k_t, v_t, kk_t, a_t = inp
        sk = jnp.einsum('bhvk,bhk->bhv', state, kk_t)
        state = (state * w_t[:, :, None, :]
                 - sk[..., None] * (kk_t * a_t)[:, :, None, :]
                 + v_t[..., None] * k_t[:, :, None, :])
        y = jnp.einsum('bhvk,bhk->bhv', state, r_t)
        return state, y

    xs = (jnp.moveaxis(r, 1, 0), jnp.moveaxis(w, 1, 0), jnp.moveaxis(k, 1, 0),
          jnp.moveaxis(v, 1, 0), jnp.moveaxis(kk, 1, 0), jnp.moveaxis(a, 1, 0))
    _, y = lax.scan(step, jnp.zeros((B, H, N, N), jnp.float32), xs)
    return jnp.moveaxis(y, 0, 1)

def hybrid_token_mixer(h, w_in, m_conv_w, m_conv_b, m_gate_b, m_norm_g, r_mu, r_w0, r_w_up,
                       r_a0, r_a_up, r_g_up, r_kk, r_ka, r_rk, r_gn_g, r_gn_b, w_out):
    B, S, _ = h.shape
    f32 = jnp.float32
    p = h @ w_in
    pm, pr = p[..., :M_COLS], p[..., M_COLS:]

    qk = jax.nn.silu(causal_dwconv(pm[..., :2 * M_WIDTH], m_conv_w, m_conv_b))
    q, k = qk[..., :M_WIDTH], qk[..., M_WIDTH:]
    v = pm[..., 2 * M_WIDTH:3 * M_WIDTH]
    o = pm[..., 3 * M_WIDTH:4 * M_WIDTH]
    gates = pm[..., 4 * M_WIDTH:] + m_gate_b
    i_pre, f_pre = gates[..., :M_HEADS], gates[..., M_HEADS:]

    def to_heads(t):
        return t.reshape(B, S, M_HEADS, M_HDIM).transpose(0, 2, 1, 3)

    hm = mlstm_chunkwise(to_heads(q), to_heads(k), to_heads(v),
                         i_pre.transpose(0, 2, 1), f_pre.transpose(0, 2, 1))
    hm = standardize_heads(hm.transpose(0, 2, 1, 3), NORM_EPS).reshape(B, S, M_WIDTH)
    y_m = (jax.nn.sigmoid(o.astype(f32)) * hm * m_norm_g.astype(f32)).astype(h.dtype)

    pr = token_shift(pr, r_mu)
    rr = pr[..., :R_WIDTH]
    kr = pr[..., R_WIDTH:2 * R_WIDTH]
    vr = pr[..., 2 * R_WIDTH:3 * R_WIDTH]
    off = 3 * R_WIDTH
    wd = pr[..., off:off + R_DECAY_LORA]
    off = off + R_DECAY_LORA
    ad = pr[..., off:off + R_AAA_LORA]
    off = off + R_AAA_LORA
    gd = pr[..., off:off + R_GATE_LORA]
    w = jnp.exp(-DECAY_SCALE * jax.nn.sigmoid((r_w0 + jnp.tanh(wd) @ r_w_up).astype(f32)))
    a = jax.nn.sigmoid((r_a0 + ad @ r_a_up).astype(f32))
    g = jax.nn.sigmoid(gd) @ r_g_up

    def rh(t):
        return t.astype(f32).reshape(B, S, R_HEADS, R_HDIM)

    kk = rh(kr * r_kk)
    kk = kk / jnp.maximum(jnp.sqrt(jnp.sum(kk * kk, -1, keepdims=True)), 1e-12)
    kr = kr.astype(f32) * (1.0 + (a - 1.0) * r_ka.astype(f32))
    rr, kr, vr, w, a = rh(rr), rh(kr), rh(vr), rh(w), rh(a)
    yr = rwkv7_scan(rr, w, kr, vr, kk, a)
    yr = (standardize_heads(yr, GN_EPS) * r_gn_g.astype(f32).reshape(R_HEADS, R_HDIM)
          + r_gn_b.astype(f32).reshape(R_HEADS, R_HDIM))
    yr = yr + jnp.sum(rr * kr * r_rk.astype(f32), -1, keepdims=True) * vr
    y_r = (yr.reshape(B, S, R_WIDTH) * g.astype(f32)).astype(h.dtype)

    return jnp.concatenate([y_m, y_r], -1) @ w_out

def mem_cross_attn(h, memn, w_q, w_kv, w_o):
    B, S, _ = h.shape
    M = memn.shape[1]
    q = (h @ w_q).reshape(B, S, X_HEADS, X_HDIM)
    kv = memn @ w_kv
    k = kv[..., :D_MODEL].reshape(B, M, X_HEADS, X_HDIM)
    v = kv[..., D_MODEL:].reshape(B, M, X_HEADS, X_HDIM)
    s = jnp.einsum('bshd,bmhd->bhsm', q, k).astype(jnp.float32) * (X_HDIM ** -0.5)
    pr = jax.nn.softmax(s, -1).astype(v.dtype)
    o = jnp.einsum('bhsm,bmhd->bshd', pr, v).reshape(B, S, D_MODEL)
    return o @ w_o

def conv_glu_ffn(h, w_up, conv_w, conv_b, w_down):
    u = h @ w_up
    gate, val = u[..., :D_FF], u[..., D_FF:]
    gate = causal_dwconv(gate, conv_w, conv_b)
    return (jax.nn.silu(gate) * val) @ w_down

def first_inputs(seed: int = 0) -> dict:
    key = jax.random.key(seed)
    ks = iter(jax.random.split(key, 48))
    L = DEPTH

    def nrm(shape, scale):
        return jax.random.normal(next(ks), shape, jnp.float32) * scale

    def gain(shape):
        return 1.0 + nrm(shape, 0.02)

    def unif(shape, lo, hi):
        return jax.random.uniform(next(ks), shape, jnp.float32, minval=lo, maxval=hi)

    x = nrm((BATCH, SEQ, D_MODEL), 1.0)
    mem = nrm((BATCH, N_MEM, D_MODEL), 1.0)
    f_bias = jnp.linspace(F_BIAS_LO, F_BIAS_HI, M_HEADS, dtype=jnp.float32)
    m_gate_b = jnp.concatenate([nrm((L, M_HEADS), 0.1), f_bias + nrm((L, M_HEADS), 0.1)], -1)
    return {
        'x': x,
        'mem': mem,
        'norm_mix': gain((L, D_MODEL)),
        'w_in': nrm((L, D_MODEL, IN_COLS), D_MODEL ** -0.5),
        'm_conv_w': nrm((L, M_CONV, 2 * M_WIDTH), M_CONV ** -0.5),
        'm_conv_b': nrm((L, 2 * M_WIDTH), 0.02),
        'm_gate_b': m_gate_b,
        'm_norm_g': gain((L, M_WIDTH)),
        'r_mu': unif((L, R_COLS), 0.0, 1.0),
        'r_w0': unif((L, R_WIDTH), -2.0, 2.0),
        'r_w_up': nrm((L, R_DECAY_LORA, R_WIDTH), R_DECAY_LORA ** -0.5),
        'r_a0': nrm((L, R_WIDTH), 0.1),
        'r_a_up': nrm((L, R_AAA_LORA, R_WIDTH), R_AAA_LORA ** -0.5),
        'r_g_up': nrm((L, R_GATE_LORA, R_WIDTH), R_GATE_LORA ** -0.5),
        'r_kk': 0.85 + nrm((L, R_WIDTH), 0.05),
        'r_ka': 1.0 + nrm((L, R_WIDTH), 0.05),
        'r_rk': nrm((L, R_HEADS, R_HDIM), 0.1),
        'r_gn_g': gain((L, R_WIDTH)),
        'r_gn_b': nrm((L, R_WIDTH), 0.02),
        'w_out': nrm((L, MIX_WIDTH, D_MODEL), MIX_WIDTH ** -0.5),
        'norm_x': gain((L, D_MODEL)),
        'norm_mem': gain((L, D_MODEL)),
        'x_wq': nrm((L, D_MODEL, D_MODEL), D_MODEL ** -0.5),
        'x_wkv': nrm((L, D_MODEL, 2 * D_MODEL), D_MODEL ** -0.5),
        'x_wo': nrm((L, D_MODEL, D_MODEL), D_MODEL ** -0.5),
        'norm_ffn': gain((L, D_MODEL)),
        'f_up': nrm((L, D_MODEL, 2 * D_FF), D_MODEL ** -0.5),
        'f_conv_w': nrm((L, FFN_CONV, D_FF), FFN_CONV ** -0.5),
        'f_conv_b': nrm((L, D_FF), 0.02),
        'f_down': nrm((L, D_FF, D_MODEL), D_FF ** -0.5),
        'norm_final': gain((D_MODEL,)),
    }

def first_block(x, mem, norm_mix, w_in, m_conv_w, m_conv_b, m_gate_b, m_norm_g, r_mu, r_w0,
              r_w_up, r_a0, r_a_up, r_g_up, r_kk, r_ka, r_rk, r_gn_g, r_gn_b, w_out,
              norm_x, norm_mem, x_wq, x_wkv, x_wo, norm_ffn, f_up, f_conv_w, f_conv_b,
              f_down, norm_final):
    for l in range(DEPTH):
        h = rmsnorm(x, norm_mix[l])
        x = x + hybrid_token_mixer(h, w_in[l], m_conv_w[l], m_conv_b[l], m_gate_b[l],
                                   m_norm_g[l], r_mu[l], r_w0[l], r_w_up[l], r_a0[l],
                                   r_a_up[l], r_g_up[l], r_kk[l], r_ka[l], r_rk[l],
                                   r_gn_g[l], r_gn_b[l], w_out[l])
        h = rmsnorm(x, norm_x[l])
        memn = rmsnorm(mem, norm_mem[l])
        x = x + mem_cross_attn(h, memn, x_wq[l], x_wkv[l], x_wo[l])
        h = rmsnorm(x, norm_ffn[l])
        x = x + conv_glu_ffn(h, f_up[l], f_conv_w[l], f_conv_b[l], f_down[l])
    return rmsnorm(x, norm_final)


MEM_LEN = 256
ROPE_THETA = 500000.0
EPS = 1e-6
NEG = -1e30
Q_BLOCK = 128
N_BRANCH = 3
BRANCH_WIDTH = 512
A_HEADS = 8
A_HEAD_DIM = 64
A_ROT = A_HEAD_DIM // 4
IDX_HEADS = 8
IDX_DIM = 64
IDX_ROT = IDX_DIM // 4
TOPK_MAX = 256
B_HEADS = 8
B_NOPE = 64
B_ROPE = 32
B_VDIM = 64
B_QK = B_NOPE + B_ROPE
B_Q_RANK = 384
B_KV_RANK = 256
M_HEAD_DIM = 128

SPLITS = (
    A_HEADS * A_HEAD_DIM,
    A_HEADS * A_HEAD_DIM,
    A_HEADS * A_HEAD_DIM,
    IDX_HEADS * IDX_DIM,
    IDX_DIM,
    IDX_HEADS,
    BRANCH_WIDTH,
    B_Q_RANK,
    B_KV_RANK,
    B_ROPE,
    BRANCH_WIDTH,
    M_HEADS * M_HEAD_DIM,
    BRANCH_WIDTH,
    N_BRANCH * D_MODEL,
)
D_IN = (4 * A_HEADS * A_HEAD_DIM + IDX_DIM + IDX_HEADS + BRANCH_WIDTH
        + B_Q_RANK + B_KV_RANK + B_ROPE + BRANCH_WIDTH
        + M_HEADS * M_HEAD_DIM + BRANCH_WIDTH + N_BRANCH * D_MODEL)


def rms_norm(x, g):
    xf = x.astype(jnp.float32)
    y = xf * lax.rsqrt(jnp.mean(xf * xf, axis=-1, keepdims=True) + EPS)
    return (y * g.astype(jnp.float32)).astype(x.dtype)

def rope_tables(positions, rot_dim):
    inv_freq = ROPE_THETA ** (-(jnp.arange(0, rot_dim, 2, dtype=jnp.float32) / rot_dim))
    ang = positions.astype(jnp.float32)[..., None] * inv_freq
    return jnp.cos(ang), jnp.sin(ang)

def rotate(x, cos, sin):
    half = x.shape[-1] // 2
    x1 = x[..., :half].astype(jnp.float32)
    x2 = x[..., half:].astype(jnp.float32)
    return jnp.concatenate([x1 * cos - x2 * sin, x2 * cos + x1 * sin], axis=-1).astype(x.dtype)

def partial_rope(x, cos, sin):
    rd = 2 * cos.shape[-1]
    return jnp.concatenate([rotate(x[..., :rd], cos, sin), x[..., rd:]], axis=-1)

def to_blocks(t, nb):
    b = t.shape[0]
    return jnp.moveaxis(t.reshape((b, nb, Q_BLOCK) + t.shape[2:]), 1, 0)

def from_blocks(t):
    t = jnp.moveaxis(t, 0, 1)
    return t.reshape((t.shape[0], t.shape[1] * t.shape[2]) + t.shape[3:])

def dsa_attention(q, k, v, qi, ki, wi):
    b, s, h, d = q.shape
    nb = s // Q_BLOCK
    topk = min(TOPK_MAX, s // 4)
    key_pos = jnp.arange(s)
    ki_f = ki.astype(jnp.float32)
    scale = d ** -0.5

    def one_block(args):
        qb, qib, wib, start = args
        q_pos = start + jnp.arange(Q_BLOCK)
        causal = key_pos[None, :] <= q_pos[:, None]
        dots = jnp.einsum('bqhc,bsc->bhqs', qib.astype(jnp.float32), ki_f) * (IDX_DIM ** -0.5)
        index = jnp.einsum('bhqs,bqh->bqs', jax.nn.relu(dots),
                           wib.astype(jnp.float32) * (IDX_HEADS ** -0.5))
        index = jnp.where(causal[None], index, NEG)
        _, idx = lax.top_k(index, topk)
        valid = idx <= q_pos[None, :, None]
        k_sel = jax.vmap(lambda kb, ib: kb[ib])(k, idx)
        v_sel = jax.vmap(lambda vb, ib: vb[ib])(v, idx)
        sc = jnp.einsum('bqhd,bqkhd->bhqk', qb, k_sel).astype(jnp.float32) * scale
        sc = jnp.where(valid[:, None], sc, NEG)
        p = jax.nn.softmax(sc, axis=-1).astype(v.dtype)
        return jnp.einsum('bhqk,bqkhd->bqhd', p, v_sel)

    starts = jnp.arange(nb) * Q_BLOCK
    out = lax.map(one_block, (to_blocks(q, nb), to_blocks(qi, nb), to_blocks(wi, nb), starts))
    return from_blocks(out)

def causal_attention(q, k, v):
    b, s, h, dq = q.shape
    nb = s // Q_BLOCK
    key_pos = jnp.arange(s)
    scale = dq ** -0.5

    def one_block(args):
        qb, start = args
        q_pos = start + jnp.arange(Q_BLOCK)
        sc = jnp.einsum('bqhd,bkhd->bhqk', qb, k).astype(jnp.float32) * scale
        sc = jnp.where((key_pos[None, :] <= q_pos[:, None])[None, None], sc, NEG)
        p = jax.nn.softmax(sc, axis=-1).astype(v.dtype)
        return jnp.einsum('bhqk,bkhd->bqhd', p, v)

    starts = jnp.arange(nb) * Q_BLOCK
    return from_blocks(lax.map(one_block, (to_blocks(q, nb), starts)))

def second_inputs(seed: int = 0) -> dict:
    key = jax.random.key(seed)
    ks = jax.random.split(key, 24)
    f32 = jnp.float32

    def w(k, shape, fan_in):
        return jax.random.normal(k, shape, f32) * (fan_in ** -0.5)

    def gain(k, shape):
        return 1.0 + 0.02 * jax.random.normal(k, shape, f32)

    x = jax.random.normal(ks[0], (BATCH, SEQ, D_MODEL), f32)
    mem = jax.random.normal(ks[1], (BATCH, MEM_LEN, D_MODEL), f32)
    offsets = jax.random.randint(ks[2], (BATCH, 1), 0, 4096, dtype=jnp.int32)
    positions = offsets + jnp.arange(SEQ, dtype=jnp.int32)[None, :]
    return {
        "x": x,
        "mem": mem,
        "positions": positions,
        "g_norm": gain(ks[3], (DEPTH, D_MODEL)),
        "w_in": w(ks[4], (DEPTH, D_MODEL, D_IN), D_MODEL),
        "g_qn_a": gain(ks[5], (DEPTH, A_HEAD_DIM)),
        "g_kn_a": gain(ks[6], (DEPTH, A_HEAD_DIM)),
        "g_cq": gain(ks[7], (DEPTH, B_Q_RANK)),
        "g_ckv": gain(ks[8], (DEPTH, B_KV_RANK)),
        "w_uq": w(ks[9], (DEPTH, B_Q_RANK, B_HEADS * B_QK), B_Q_RANK),
        "w_ukv": w(ks[10], (DEPTH, B_KV_RANK, B_HEADS * (B_NOPE + B_VDIM)), B_KV_RANK),
        "g_qn_b": gain(ks[11], (DEPTH, B_QK)),
        "g_kn_b": gain(ks[12], (DEPTH, B_QK)),
        "g_mem": gain(ks[13], (DEPTH, D_MODEL)),
        "w_mem_kv": w(ks[14], (DEPTH, D_MODEL, 2 * M_HEADS * M_HEAD_DIM), D_MODEL),
        "g_qn_m": gain(ks[15], (DEPTH, M_HEAD_DIM)),
        "g_kn_m": gain(ks[16], (DEPTH, M_HEAD_DIM)),
        "w_branch": w(ks[17], (DEPTH, N_BRANCH, BRANCH_WIDTH, D_MODEL), BRANCH_WIDTH),
        "w_out": w(ks[18], (DEPTH, D_MODEL, D_MODEL), D_MODEL),
    }

def second_block(x, mem, positions, g_norm, w_in, g_qn_a, g_kn_a, g_cq, g_ckv, w_uq, w_ukv,
              g_qn_b, g_kn_b, g_mem, w_mem_kv, g_qn_m, g_kn_m, w_branch, w_out):
    b, s, _ = x.shape
    m_len = mem.shape[1]
    cos_a, sin_a = rope_tables(positions, A_ROT)
    cos_b, sin_b = rope_tables(positions, B_ROPE)
    split_at = [int(o) for o in np.cumsum(SPLITS)[:-1]]

    for layer in range(DEPTH):
        h = rms_norm(x, g_norm[layer])
        proj = h @ w_in[layer]
        (q_a, k_a, v_a, q_i, k_i, w_i, z_a, c_q, c_kv, k_rope, z_b, q_m, z_m,
         gate_logits) = jnp.split(proj, split_at, axis=-1)

        q_a = partial_rope(rms_norm(q_a.reshape(b, s, A_HEADS, A_HEAD_DIM), g_qn_a[layer]),
                           cos_a[:, :, None], sin_a[:, :, None])
        k_a = partial_rope(rms_norm(k_a.reshape(b, s, A_HEADS, A_HEAD_DIM), g_kn_a[layer]),
                           cos_a[:, :, None], sin_a[:, :, None])
        v_a = v_a.reshape(b, s, A_HEADS, A_HEAD_DIM)
        q_i = partial_rope(q_i.reshape(b, s, IDX_HEADS, IDX_DIM), cos_a[:, :, None], sin_a[:, :, None])
        k_i = partial_rope(k_i, cos_a, sin_a)
        o_a = dsa_attention(q_a, k_a, v_a, q_i, k_i, w_i)

        q_b = (rms_norm(c_q, g_cq[layer]) @ w_uq[layer]).reshape(b, s, B_HEADS, B_QK)
        kv_b = (rms_norm(c_kv, g_ckv[layer]) @ w_ukv[layer]).reshape(b, s, B_HEADS, B_NOPE + B_VDIM)
        k_nope, v_b = kv_b[..., :B_NOPE], kv_b[..., B_NOPE:]
        k_b = jnp.concatenate(
            [k_nope, jnp.broadcast_to(k_rope[:, :, None, :], (b, s, B_HEADS, B_ROPE))], axis=-1)
        q_b = rms_norm(q_b, g_qn_b[layer])
        k_b = rms_norm(k_b, g_kn_b[layer])
        q_b = jnp.concatenate(
            [q_b[..., :B_NOPE], rotate(q_b[..., B_NOPE:], cos_b[:, :, None], sin_b[:, :, None])], axis=-1)
        k_b = jnp.concatenate(
            [k_b[..., :B_NOPE], rotate(k_b[..., B_NOPE:], cos_b[:, :, None], sin_b[:, :, None])], axis=-1)
        o_b = causal_attention(q_b, k_b, v_b)

        kv_m = (rms_norm(mem, g_mem[layer]) @ w_mem_kv[layer]).reshape(b, m_len, 2, M_HEADS, M_HEAD_DIM)
        k_m = rms_norm(kv_m[:, :, 0], g_kn_m[layer])
        v_m = kv_m[:, :, 1]
        q_m = rms_norm(q_m.reshape(b, s, M_HEADS, M_HEAD_DIM), g_qn_m[layer])
        sc_m = jnp.einsum('bqhd,bmhd->bhqm', q_m, k_m).astype(jnp.float32) * (M_HEAD_DIM ** -0.5)
        p_m = jax.nn.softmax(sc_m, axis=-1).astype(v_m.dtype)
        o_m = jnp.einsum('bhqm,bmhd->bqhd', p_m, v_m)

        ys = jnp.stack([
            o_a.reshape(b, s, BRANCH_WIDTH) * jax.nn.silu(z_a),
            o_b.reshape(b, s, BRANCH_WIDTH) * jax.nn.silu(z_b),
            o_m.reshape(b, s, BRANCH_WIDTH) * jax.nn.silu(z_m),
        ], axis=0)
        branch = jnp.einsum('nbsw,nwd->nbsd', ys, w_branch[layer])
        gates = jax.nn.sigmoid(
            gate_logits.reshape(b, s, N_BRANCH, D_MODEL).astype(jnp.float32)).astype(x.dtype)
        merged = jnp.einsum('bsnd,nbsd->bsd', gates, branch)
        x = x + merged @ w_out[layer]
    return x


def setup_inputs(seed=0):
    out = dict(first_inputs(seed))
    for name, value in second_inputs(seed + 1).items():
        if name != "x":
            out[name + "_2"] = value
    return out


def reference(
    x, mem, norm_mix, w_in, m_conv_w, m_conv_b, m_gate_b, m_norm_g, r_mu, r_w0, r_w_up, r_a0,
    r_a_up, r_g_up, r_kk, r_ka, r_rk, r_gn_g, r_gn_b, w_out, norm_x, norm_mem, x_wq, x_wkv,
    x_wo, norm_ffn, f_up, f_conv_w, f_conv_b, f_down, norm_final, mem_2, positions_2, g_norm_2,
    w_in_2, g_qn_a_2, g_kn_a_2, g_cq_2, g_ckv_2, w_uq_2, w_ukv_2, g_qn_b_2, g_kn_b_2, g_mem_2,
    w_mem_kv_2, g_qn_m_2, g_kn_m_2, w_branch_2, w_out_2,
):
    x = first_block(
        x, mem, norm_mix, w_in, m_conv_w, m_conv_b, m_gate_b, m_norm_g, r_mu, r_w0, r_w_up,
        r_a0, r_a_up, r_g_up, r_kk, r_ka, r_rk, r_gn_g, r_gn_b, w_out, norm_x, norm_mem, x_wq,
        x_wkv, x_wo, norm_ffn, f_up, f_conv_w, f_conv_b, f_down, norm_final,
    )
    return second_block(
        x, mem_2, positions_2, g_norm_2, w_in_2, g_qn_a_2, g_kn_a_2, g_cq_2, g_ckv_2, w_uq_2,
        w_ukv_2, g_qn_b_2, g_kn_b_2, g_mem_2, w_mem_kv_2, g_qn_m_2, g_kn_m_2, w_branch_2,
        w_out_2,
    )


_drawn_inputs = setup_inputs


def setup_inputs(seed=0):
    import zlib

    import numpy as np

    out = dict(_drawn_inputs(seed))
    spreads = {}
    factors = {'norm_mix': 2.811,
     'm_conv_b': 7.819,
     'm_norm_g': 6.73,
     'r_a0': 3.293,
     'r_kk': 8.0,
     'r_gn_g': 7.506,
     'r_gn_b': 6.72,
     'norm_x': 8.0,
     'norm_mem': 8.0,
     'norm_ffn': 3.866,
     'f_conv_b': 5.644,
     'norm_final': 2.756,
     'g_norm_2': 7.951,
     'g_qn_a_2': 8.0,
     'g_kn_a_2': 8.0,
     'g_cq_2': 8.0,
     'g_ckv_2': 8.0,
     'g_qn_b_2': 8.0,
     'g_kn_b_2': 8.0,
     'g_mem_2': 8.0,
     'g_qn_m_2': 8.0,
     'g_kn_m_2': 8.0}
    for name, (base, spread) in spreads.items():
        noise = np.random.default_rng([zlib.crc32(name.encode()), seed]).standard_normal(out[name].shape)
        drawn = base * np.exp(spread * noise) if base else spread * noise
        out[name] = __import__('jax').numpy.asarray(drawn.astype(out[name].dtype))
    for name, factor in factors.items():
        out[name] = (out[name] * factor).astype(out[name].dtype)
    return out
```

```python
import math
from contextlib import ExitStack, contextmanager

import numpy as np

import concourse.bass as bass
from concourse import mybir

F32 = mybir.dt.float32
I32 = mybir.dt.int32
ALU = mybir.AluOpType
ACT = mybir.ActivationFunctionType
AX = mybir.AxisListType.X

P = 128
S = 512
D = 1024
DT = D // P
ST = S // P
MEM = 256
EPS = 1e-6
GN_EPS = 64e-5
NEG = -1e30
CHOSEN = -3e38

MW, MH, MHD = 512, 4, 128
RW, RH, RHD = 512, 8, 64
CH = 64
NCH = S // CH
PAIRS = RW // P
LORA_G = 160
DECAY = math.exp(-0.5)
XH, XHD = 4, 256
DFF = 2816
FT = DFF // P
M_COLS = 4 * MW + 2 * MH

TOPK = 128
AH, AHD, AROT = 8, 64, 16
BH, BNOPE, BROPE, BV, BQK = 8, 64, 32, 64, 96
QR, KVR = 384, 256
NBR = 3
BW = 512
THETA = 500000.0
O2 = np.cumsum([0, 512, 512, 512, 512, 64, 8, 512, 384, 256, 32, 512, 512, 512, 3072]).tolist()
(C_QA, C_KA, C_VA, C_QI, C_KI, C_WI, C_ZA, C_CQ, C_CKV, C_KR, C_ZB, C_QM, C_ZM, C_GATE) = O2[:14]

SLOT = 1024
SLOTS = 8


def feature_tile(mat, col, cols=P, rows=D, row=0):
    return [(mat, row + r, min(P, rows - r), col, cols) for r in range(0, rows, P)]


def weight_plan():
    plan = []

    def feats(name, mat, col, width, rows=D, step=P):
        for c in range(0, width, step):
            plan.append((name, feature_tile(mat, col + c, min(step, width - c), rows)))

    def toks(name, mat, col, rows=D, width=512):
        for r in range(0, rows, 2 * P):
            plan.append((name, [(mat, r + q, P, col, width) for q in (0, P)]))

    feats("m_qk", "w_in", 0, 2 * MW)
    toks("m_v", "w_in", 2 * MW)
    feats("m_o", "w_in", 3 * MW, MW)
    plan.append(("m_gate_i", feature_tile("w_in", 4 * MW, MH)))
    plan.append(("m_gate_f", feature_tile("w_in", 4 * MW + MH, MH)))
    feats("r_rkv", "w_in", M_COLS, 3 * RW)
    feats("r_w", "w_in", M_COLS + 3 * RW, 64)
    feats("r_a", "w_in", M_COLS + 3 * RW + 64, 64)
    feats("r_g", "w_in", M_COLS + 3 * RW + 128, LORA_G)
    feats("w_out", "w_out", 0, D)
    feats("x_k", "x_wkv", 0, D)
    for half in range(2):
        toks("x_v", "x_wkv", D + 512 * half)
    feats("x_q", "x_wq", 0, D)
    feats("x_o", "x_wo", 0, D)
    for f in range(FT):
        plan.append(("f_up", feature_tile("f_up", f * P)))
        plan.append(("f_up", feature_tile("f_up", DFF + f * P)))
    for m in range(DT):
        for r0 in range(0, FT, 8):
            n = min(8, FT - r0)
            plan.append(("f_down", feature_tile("f_down", m * P, P, n * P, r0 * P)))
    w2 = "w_in_2"
    feats("a_qk", w2, C_QA, 1024)
    feats("a_qi", w2, C_QI, 512)
    plan.append(("a_ki", [(w2, r, P, C_KI, 64) for r in range(0, D, P) for _ in range(2)]))
    plan.append(("a_wi", feature_tile(w2, C_WI, AH)))
    toks("a_v", w2, C_VA)
    feats("a_z", w2, C_ZA, BW)
    feats("b_c", w2, C_CQ, QR + KVR)
    plan.append(("b_kr", feature_tile(w2, C_KR, BROPE)))
    for h in range(BH):
        plan.append(("b_uq", feature_tile("w_uq_2", h * BQK, BQK, QR)))
    plan.append(("b_uk", [(
        "w_ukv_2", r, P, h * (BNOPE + BV), BNOPE) for h in range(BH) for r in (0, P)]))
    plan.append(("b_uv", [(
        "w_ukv_2", r, P, h * (BNOPE + BV) + BNOPE, BV) for r in (0, P) for h in range(BH)]))
    feats("b_z", w2, C_ZB, BW)
    feats("m2_k", "w_mem_kv_2", 0, 512)
    toks("m2_v", "w_mem_kv_2", 512)
    feats("m2_q", w2, C_QM, 512)
    feats("m2_z", w2, C_ZM, BW)
    for m in range(DT):
        for n in range(NBR):
            plan.append(("gate", feature_tile(w2, C_GATE + n * D + m * P)))
            plan.append(("branch", feature_tile("w_branch_2", m * P, P, BW, n * BW)))
    feats("w_out_2", "w_out_2", 0, D)
    return plan


def block_width(blocks):
    return sum(b[4] for b in blocks)


VECTORS = {}


def vector_table(inputs):
    cols = []

    def put(name, vec, size=P, start=0):
        vec = np.asarray(vec).reshape(-1)
        VECTORS[name] = len(cols)
        for r in range(0, len(vec), size):
            c = np.zeros(P, np.float32)
            part = vec[r:r + size]
            c[start:start + len(part)] = part
            cols.append(c)

    for n in ("norm_mix", "norm_x", "norm_mem", "norm_ffn", "norm_final", "g_norm_2", "g_mem_2",
              "m_conv_b", "m_norm_g", "r_w0", "r_a0", "r_kk", "r_ka", "r_rk", "r_gn_g", "r_gn_b",
              "f_conv_b", "g_cq_2", "g_ckv_2", "g_qn_b_2", "g_kn_b_2", "g_qn_m_2", "g_kn_m_2"):
        put(n, inputs[n])
    for j in range(4):
        put(f"m_conv_w{j}", inputs["m_conv_w"][0, j])
    for j in range(3):
        put(f"f_conv_w{j}", inputs["f_conv_w"][0, j])
    put("bias_i", inputs["m_gate_b"][0, :MH])
    put("bias_f", inputs["m_gate_b"][0, MH:])
    mu = inputs["r_mu"][0]
    put("mu_rkv", mu[:3 * RW])
    put("mu_w", mu[3 * RW:3 * RW + 64])
    put("mu_a", mu[3 * RW + 64:3 * RW + 128])
    put("mu_g", mu[3 * RW + 128:])
    for n in ("g_qn_a_2", "g_kn_a_2"):
        put(n, np.concatenate([inputs[n][0], inputs[n][0]]))
    return np.stack(cols, 1)


def constant_table():
    at, parts, n = {}, [], 0

    def put(name, a):
        nonlocal n
        full = np.zeros((P, a.shape[1]), np.float32)
        full[:a.shape[0]] = a
        at[name] = (n, a.shape[1])
        parts.append(full)
        n += a.shape[1]

    i = np.arange(P)
    r, c = i[:, None], i[None, :]
    put("ident", np.eye(P))
    put("ones", np.ones((P, P)))
    put("ones_half", (r // 64 == c // 64) * 1.0)
    put("key_le_query", (r <= c) * 1.0)
    same = r // CH == c // CH
    put("before", (same & (r < c)) * 1.0)
    put("upto", (same & (r <= c)) * 1.0)
    b = 1
    while b < CH:
        put(f"level{b}", ((r // (2 * b) == c // (2 * b)) & (r % (2 * b) < b) & (c % (2 * b) >= b)) * 1.0)
        b *= 2
    put("level1_lower", ((r // 2 == c // 2) & (r % 2 == 1) & (c % 2 == 0)) * 1.0)
    put("row_of_head", np.concatenate([np.tile((np.arange(MH) == h)[:, None], (1, P)) for h in range(MH)], 1) * 1.0)
    a_rot = np.zeros((P, P))
    for base in (0, 64):
        for j in range(AROT // 2):
            a_rot[base + j + 8, base + j] = -1.0
            a_rot[base + j, base + j + 8] = 1.0
    put("rotate_a", a_rot)
    b_rot = np.zeros((BQK, BQK))
    for j in range(BROPE // 2):
        b_rot[BNOPE + j + 16, BNOPE + j] = -1.0
        b_rot[BNOPE + j, BNOPE + j + 16] = 1.0
    put("rotate_b", b_rot)
    fa = THETA ** (-(np.arange(0, AROT, 2, dtype=np.float32) / np.float32(AROT)))
    fb = THETA ** (-(np.arange(0, BROPE, 2, dtype=np.float32) / np.float32(BROPE)))
    put("freq_a", np.where(i % 64 < AROT, fa[i % 8], 0.0)[:, None])
    put("freq_b", np.where((i >= BNOPE) & (i < BQK), fb[(i - BNOPE) % 16], 0.0)[:, None])
    put("causal", np.concatenate([np.zeros((P, S - P)), np.where(c <= r, 0.0, NEG)], 1))
    put("chunk_start", np.tile((np.arange(S) % CH != 0)[None, :], (P, 1)) * 1.0)
    return np.concatenate(parts, 1).astype(np.float32), at


class Counter:

    def __init__(self, sem):
        self.sem, self.base, self.total = sem, 0, 0

    def inc(self):
        self.total += 1
        return self.sem, 1

    def ge(self, n):
        return self.sem, self.base + n

    def all(self):
        return self.sem, self.base + self.total


class Kernel:
    def __init__(self, nc, ctx):
        self.nc, self.ctx, self.counters, self.names = nc, ctx, {}, 0
        self.small = 0

    def counter(self, name):
        if name not in self.counters:
            self.counters[name] = Counter(self.ctx.enter_context(self.nc.semaphore(name)))
        return self.counters[name]

    @contextmanager
    def stage(self):
        with self.nc.Block() as block:
            yield block
        for s in self.counters.values():
            s.base += s.total
            s.total = 0

    def sbuf(self, ctx, name, shape, dt=F32):
        return ctx.enter_context(self.nc.sbuf_tensor(name, shape, dt))

    def fresh(self, name):
        self.names = self.names + 1
        return f"{name}_{self.names}"

    def const(self, name, rows=P):
        at, n = self.const_at[name]
        return self.consts[0:rows, at:at + n]

    def vec(self, name, tile=0, rows=P):
        c = VECTORS[name] + tile
        return self.vecs[0:rows, c:c + 1]

    def slot(self, t):
        return self.ring[:, t % SLOTS, :]

    def prefetch(self, sp, used_at_end):
        while self.loaded < min(len(self.plan), used_at_end + SLOTS):
            t = self.loaded
            if t >= SLOTS:
                sp.wait_ge(self.tile_used, t - SLOTS + 1)
            w = block_width(self.plan[t][1])
            sp.dma_start(self.ring[:, t % SLOTS, 0:w], self.weights[t, :, 0:w]).then_inc(self.landed[t % SLOTS], 16)
            self.loaded += 1

    def tile_landed(self, t):
        return self.landed[t % SLOTS], 16 * (t // SLOTS + 1)


class Chain:

    def __init__(self, eng, count):
        self.eng, self.count = eng, count

    def __call__(self, ins):
        ins.then_inc(*self.count.inc())
        self.eng.wait_ge(*self.count.all())



def feature_major(x, ktiles=DT, cols=P, n=S, row=0, offset=0):
    def emit(k, slots, bank):
        for kt in range(ktiles):
            w = slots[kt // 8][:, offset + (kt % 8) * cols:offset + (kt % 8 + 1) * cols]
            last = k.nc.tensor.matmul(bank[row:row + cols, 0:n], w, x[:, kt, 0:n],
                                      start=(kt == 0), stop=(kt == ktiles - 1))
        return last
    return emit


class Job:

    def __init__(self, name, emit, engine, take, tiles=1):
        self.name, self.emit, self.engine, self.take, self.tiles = name, emit, engine, take, tiles


def project(k, jobs, banks=8, extra=None):
    taken = {"act": k.counter("bank_taken_act"), "dve": k.counter("bank_taken_dve")}
    count, nth, slots = {"act": 0, "dve": 0}, [], []
    for job in jobs:
        count[job.engine] += 1
        nth.append(count[job.engine])
        slots.append((k.used, k.used + job.tiles))
        k.used += job.tiles

    with k.stage() as block:
        @block.sync
        def _(sp):
            k.prefetch(sp, k.used)

        @block.tensor
        def _(pe):
            for i, (job, (t0, t1)) in enumerate(zip(jobs, slots)):
                for t in range(t0, t1):
                    assert k.plan[t][0] == job.name, (k.plan[t][0], job.name)
                    pe.wait_ge(*k.tile_landed(t))
                if i >= banks:
                    pe.wait_ge(*taken[jobs[i - banks].engine].ge(nth[i - banks]))
                last = job.emit(k, [k.slot(t) for t in range(t0, t1)], k.banks[i % banks])
                last.then_inc(k.tile_used, job.tiles)

        def take_out(eng, name):
            chain = Chain(eng, k.counter(f"{name}_step"))
            for i, (job, (t0, t1)) in enumerate(zip(jobs, slots)):
                if job.engine == name:
                    eng.wait_ge(k.tile_used, t1)
                    job.take(eng, chain, k.banks[i % banks]).then_inc(*taken[name].inc())

        @block.scalar
        def _(act):
            take_out(act, "act")

        @block.vector
        def _(dve):
            take_out(dve, "dve")


def project_tokens(k, name, x, tokens, take, ktiles=DT, width=512):
    nt = tokens // P
    first, per = k.used, SLOT // width
    n = ktiles // per
    k.used += n
    out_taken = k.counter("bank_taken_act")

    with k.stage() as block:
        @block.sync
        def _(sp):
            k.prefetch(sp, k.used)

        @block.tensor
        def _(pe):
            for q in range(n):
                assert k.plan[first + q][0] == name, (k.plan[first + q][0], name)
                pe.wait_ge(*k.tile_landed(first + q))
                for j in range(per):
                    kt = q * per + j
                    for t in range(nt):
                        last = k.nc.tensor.matmul(
                            k.banks[t][:, 0:width], x[:, kt, t * P:(t + 1) * P],
                            k.slot(first + q)[:, j * width:(j + 1) * width],
                            start=(kt == 0), stop=(kt == ktiles - 1))
                last.then_inc(k.tile_used, 1)

        @block.scalar
        def _(act):
            act.wait_ge(k.tile_used, first + n)
            for t in range(nt):
                take(act, t, k.banks[t][:, 0:width])


def rms_norm(k, src, dst, gain, n, tiles=DT):
    nc = k.nc
    square_ready, sums_ready = k.counter("square_ready"), k.counter("sums_ready")
    mean_ready, root_ready = k.counter("mean_ready"), k.counter("root_ready")
    with ExitStack() as ctx:
        sq = k.sbuf(ctx, k.fresh("square"), [P, 4, n])
        rs = k.sbuf(ctx, k.fresh("rstd"), [P, n])
        with k.stage() as block:
            @block.scalar
            def _(act):
                for t in range(tiles):
                    if t >= 4:
                        act.wait_ge(*sums_ready.ge(t - 3))
                    nc.scalar.activation(sq[:, t % 4, :], src[:, t, 0:n], ACT.Square).then_inc(*square_ready.inc())
                act.wait_ge(*mean_ready.ge(1))
                nc.scalar.activation(rs[:], rs[:], ACT.Sqrt).then_inc(*root_ready.inc())

            @block.tensor
            def _(pe):
                for t in range(tiles):
                    pe.wait_ge(*square_ready.ge(t + 1))
                    nc.tensor.matmul(k.banks[0][:, 0:n], k.const("ones"), sq[:, t % 4, :], start=(t == 0),
                                     stop=(t == tiles - 1)).then_inc(*sums_ready.inc())

            @block.vector
            def _(dve):
                chain = Chain(dve, k.counter("dve_step"))
                dve.wait_ge(*sums_ready.ge(tiles))
                nc.vector.tensor_scalar(rs[:], k.banks[0][:, 0:n], 1.0 / (tiles * P), EPS, ALU.mult,
                                        ALU.add).then_inc(*mean_ready.inc())
                dve.wait_ge(*root_ready.ge(1))
                chain(nc.vector.reciprocal(rs[:], rs[:]))
                for t in range(tiles):
                    nc.vector.scalar_tensor_tensor(out=dst[:, t, 0:n], in0=src[:, t, 0:n], scalar=k.vec(gain, t),
                                                   in1=rs[:], op0=ALU.mult, op1=ALU.mult)


def conv(k, dve, chain, bank, dst, weights, bias, tile, taps):
    nc = k.nc
    chain(nc.vector.tensor_scalar(dst, bank, k.vec(f"{weights}{taps - 1}", tile), k.vec(bias, tile),
                                  ALU.mult, ALU.add))
    for j in range(taps - 2, -1, -1):
        lag = taps - 1 - j
        ins = nc.vector.scalar_tensor_tensor(out=dst[:, lag:S], in0=bank[:, 0:S - lag], scalar=k.vec(f"{weights}{j}", tile),
                                             in1=dst[:, lag:S], op0=ALU.mult, op1=ALU.add)
        if j:
            chain(ins)
    return ins


def mlstm(k, ctx_y):
    nc = k.nc
    y = k.y
    with ExitStack() as ctx:
        qk = k.sbuf(ctx, "qk", [P, 2 * MH, S])
        v = k.sbuf(ctx, "m_v", [P, ST, MW])
        o = k.sbuf(ctx, "m_o", [P, MH, S])
        ipre, fpre = k.sbuf(ctx, "ipre", [MH, S]), k.sbuf(ctx, "fpre", [MH, S])

        jobs = []
        for t in range(2 * MH):
            jobs.append(Job("m_qk", feature_major(k.h), "dve",
                            lambda e, c, b, t=t: conv(k, e, c, b, qk[:, t, :], "m_conv_w", "m_conv_b", t, 4)))
        project(k, jobs)

        def keep_v(act, t, bank):
            nc.scalar.copy(v[:, t, :], bank)
        project_tokens(k, "m_v", k.h, S, keep_v)

        jobs = [Job("m_o", feature_major(k.h), "act",
                    lambda e, c, b, t=t: nc.scalar.activation(o[:, t, :], b, ACT.Sigmoid)) for t in range(MH)]
        jobs.append(Job("m_gate_i", feature_major(k.h, cols=MH), "dve",
                        lambda e, c, b: nc.vector.tensor_scalar(ipre[:], b[0:MH, :], k.vec("bias_i", 0, MH), None, ALU.add)))
        jobs.append(Job("m_gate_f", feature_major(k.h, cols=MH), "dve",
                        lambda e, c, b: nc.vector.tensor_scalar(fpre[:], b[0:MH, :], k.vec("bias_f", 0, MH), None, ALU.add)))
        project(k, jobs)

        tmp = k.sbuf(ctx, "gate_tmp", [MH, S])
        run = k.sbuf(ctx, "gate_sum", [MH, S])
        u = k.sbuf(ctx, "gate_u", [MH, S])
        top = k.sbuf(ctx, "gate_top", [MH, S])
        low = k.sbuf(ctx, "gate_floor", [MH, S])
        u_col = k.sbuf(ctx, "u_col", [P, ST, MH])
        abs_ready, ln_ready, rows_ready = k.counter("abs_ready"), k.counter("ln_ready"), k.counter("rows_ready")
        floor_ready = k.counter("floor_ready")
        with k.stage() as block:
            @block.scalar
            def _(act):
                chain = Chain(act, k.counter("act_step"))
                for t in range(2 * MH):
                    nc.scalar.activation(qk[:, t, :], qk[:, t, :], ACT.Silu)
                act.wait_ge(*abs_ready.ge(1))
                chain(nc.scalar.activation(tmp[:], tmp[:], ACT.Exp, scale=-1.0))
                nc.scalar.activation(tmp[:], tmp[:], ACT.Ln, bias=1.0).then_inc(*ln_ready.inc())
                act.wait_ge(*rows_ready.ge(2))
                nc.scalar.activation(low[:], low[:], ACT.Exp, scale=-1.0).then_inc(*floor_ready.inc())

            @block.vector
            def _(dve):
                chain = Chain(dve, k.counter("dve_step"))
                nc.vector.scalar_tensor_tensor(out=tmp[:], in0=fpre[:], scalar=-1.0, in1=fpre[:],
                                               op0=ALU.mult, op1=ALU.max).then_inc(*abs_ready.inc())
                dve.wait_ge(*ln_ready.ge(1))
                chain(nc.vector.scalar_tensor_tensor(out=fpre[:], in0=fpre[:], scalar=0.0, in1=tmp[:],
                                                     op0=ALU.min, op1=ALU.subtract))
                chain(nc.vector.tensor_tensor_scan(run[:], fpre[:], fpre[:], 0.0, ALU.add, ALU.bypass))
                nc.vector.tensor_tensor(u[:], ipre[:], run[:], ALU.subtract).then_inc(*rows_ready.inc())
                dve.wait_ge(*rows_ready.ge(1))
                chain(nc.vector.tensor_tensor_scan(top[:], u[:], u[:], 0.0, ALU.max, ALU.max))
                nc.vector.tensor_tensor(low[:], top[:], run[:], ALU.add).then_inc(*rows_ready.inc())
                dve.wait_ge(*floor_ready.ge(1))
                dve.wait_ge(*k.counter("u_turned").ge(1))
                nc.vector.tensor_copy(u_col[:].rearrange("p t h -> p (t h)"), k.banks[0][:, 0:ST * MH])

            @block.tensor
            def _(pe):
                pe.wait_ge(*rows_ready.ge(1))
                for t in range(ST):
                    last = nc.tensor.matmul(k.banks[0][:, t * MH:(t + 1) * MH], u[:, t * P:(t + 1) * P],
                                            k.const("ident", MH)[:, 0:MH], start=True, stop=True)
                last.then_inc(*k.counter("u_turned").inc())

        topb = k.sbuf(ctx, "top_b", [P, 2, S])
        lowb = k.sbuf(ctx, "floor_b", [P, 2, S])
        e = k.sbuf(ctx, "m_e", [P, 4, S])
        hm = k.sbuf(ctx, "m_hm", [P, 2, S])
        sq = k.sbuf(ctx, "m_sq", [P, 2, S])
        rs = k.sbuf(ctx, "m_rs", [P, 2, S])
        sel = k.const("row_of_head", MH)
        G = k.counter
        sent, put, made, expd = G("score_ready"), G("rows_spread"), G("arg_ready"), G("exp_ready")
        prob, summed, meaned = G("prob_ready"), G("num_den_ready"), G("mean_ready")
        rooted, normed = G("root_ready"), G("head_ready")
        width = [S - j * P for j in range(ST)]

        def nums(pe, h, j):
            n = ST * h + j
            pe.wait_ge(*prob.ge(n + 1))
            if j == 0 and h:
                pe.wait_ge(*G("hidden_ready").ge(h))
            nc.tensor.matmul(k.banks[3][:, j * P:S], v[:, j, h * P:(h + 1) * P], e[:, n % 4, 0:width[j]],
                             start=(j == 0), stop=(j == ST - 1))
            nc.tensor.matmul(k.banks[4][:, j * P:S], k.const("ones"), e[:, n % 4, 0:width[j]],
                             start=(j == 0), stop=(j == ST - 1)).then_inc(*summed.inc())

        def weigh(dve, chain, h, j):
            n = ST * h + j
            ed = e[:, n % 4, 0:width[j]]
            dve.wait_ge(*expd.ge(n + 1))
            dve.wait_ge(*sent.ge(n + 1))
            chain(nc.vector.scalar_tensor_tensor(out=ed, in0=k.banks[1 + n % 2][:, 0:width[j]],
                                                 scalar=MHD ** -0.5, in1=ed, op0=ALU.mult, op1=ALU.mult))
            nc.vector.tensor_tensor(e[:, n % 4, 0:P], e[:, n % 4, 0:P], k.const("key_le_query"),
                                    ALU.mult).then_inc(*prob.inc())

        with k.stage() as block:
            @block.tensor
            def _(pe):
                for h in range(MH):
                    for j in range(2):
                        if h >= 1 or j:
                            pe.wait_ge(*G("spread_taken").ge(2 * h + j))
                        src = top if j == 0 else low
                        nc.tensor.matmul(k.banks[0], sel[:, h * P:(h + 1) * P], src[:],
                                         start=True, stop=True).then_inc(*put.inc())
                    for j in range(ST):
                        n = ST * h + j
                        if n >= 2:
                            pe.wait_ge(*prob.ge(n - 1))
                        nc.tensor.matmul(k.banks[1 + n % 2][:, 0:width[j]], qk[:, MH + h, j * P:(j + 1) * P],
                                         qk[:, h, j * P:S], start=True, stop=True).then_inc(*sent.inc())
                        if j:
                            nums(pe, h, j - 1)
                    nums(pe, h, ST - 1)
                    pe.wait_ge(*G("hidden_ready").ge(h + 1))
                    nc.tensor.matmul(k.banks[5], k.const("ones"), hm[:, h % 2, :], start=True,
                                     stop=True).then_inc(*meaned.inc())
                    pe.wait_ge(*G("square_ready").ge(h + 1))
                    nc.tensor.matmul(k.banks[6], k.const("ones"), sq[:, h % 2, :], start=True,
                                     stop=True).then_inc(*meaned.inc())

            @block.scalar
            def _(act):
                chain = Chain(act, k.counter("act_step"))
                for h in range(MH):
                    for j, dst in enumerate((topb, lowb)):
                        act.wait_ge(*put.ge(2 * h + j + 1))
                        if h >= 2:
                            act.wait_ge(*normed.ge(h - 1))
                        nc.scalar.copy(dst[:, h % 2, :], k.banks[0]).then_inc(*G("spread_taken").inc())
                    for j in range(ST):
                        n = ST * h + j
                        act.wait_ge(*made.ge(n + 1))
                        nc.scalar.activation(e[:, n % 4, 0:width[j]], e[:, n % 4, 0:width[j]],
                                             ACT.Exp).then_inc(*expd.inc())
                    act.wait_ge(*summed.ge(ST * h + ST))
                    if h >= 2:
                        act.wait_ge(*normed.ge(h - 1))
                    nc.scalar.activation(rs[:, h % 2, :], k.banks[4], ACT.Abs).then_inc(*G("den_ready").inc())
                    act.wait_ge(*G("centred_ready").ge(h + 1))
                    nc.scalar.activation(sq[:, h % 2, :], hm[:, h % 2, :], ACT.Square).then_inc(*G("square_ready").inc())
                    act.wait_ge(*G("var_ready").ge(h + 1))
                    nc.scalar.activation(rs[:, h % 2, :], rs[:, h % 2, :], ACT.Sqrt).then_inc(*rooted.inc())

            @block.vector
            def _(dve):
                chain = Chain(dve, k.counter("dve_step"))
                for h in range(MH):
                    dve.wait_ge(*G("spread_taken").ge(2 * h + 2))
                    for j in range(ST):
                        n = ST * h + j
                        if n >= 4:
                            dve.wait_ge(*summed.ge(n - 3))
                        ed = e[:, n % 4, 0:width[j]]
                        chain(nc.vector.tensor_scalar(ed, topb[:, h % 2, j * P:S], u_col[:, j, h:h + 1], -1.0,
                                                      ALU.subtract, ALU.mult))
                        nc.vector.tensor_scalar(ed, ed, 0.0, None, ALU.min).then_inc(*made.inc())
                        if j:
                            weigh(dve, chain, h, j - 1)
                    weigh(dve, chain, h, ST - 1)
                    hb, rb = hm[:, h % 2, :], rs[:, h % 2, :]
                    dve.wait_ge(*G("den_ready").ge(h + 1))
                    chain(nc.vector.tensor_tensor(rb, rb, lowb[:, h % 2, :], ALU.max))
                    chain(nc.vector.reciprocal(rb, rb))
                    nc.vector.tensor_tensor(hb, k.banks[3], rb, ALU.mult).then_inc(*G("hidden_ready").inc())
                    dve.wait_ge(*meaned.ge(2 * h + 1))
                    nc.vector.scalar_tensor_tensor(out=hb, in0=k.banks[5], scalar=-1.0 / MHD, in1=hb,
                                                   op0=ALU.mult, op1=ALU.add).then_inc(*G("centred_ready").inc())
                    dve.wait_ge(*meaned.ge(2 * h + 2))
                    nc.vector.tensor_scalar(rb, k.banks[6], 1.0 / MHD, EPS, ALU.mult, ALU.add).then_inc(*G("var_ready").inc())
                    dve.wait_ge(*rooted.ge(h + 1))
                    chain(nc.vector.reciprocal(rb, rb))
                    chain(nc.vector.scalar_tensor_tensor(out=hb, in0=hb, scalar=k.vec("m_norm_g", h), in1=rb,
                                                         op0=ALU.mult, op1=ALU.mult))
                    nc.vector.tensor_tensor(y[:, h, :], hb, o[:, h, :], ALU.mult).then_inc(*normed.inc())

def shifted(k, dve, chain, bank, dst, mu, tile, rows=P):
    nc = k.nc
    chain(nc.vector.tensor_scalar(dst, bank[0:rows, :], k.keep_share[0:rows, VECTORS[mu] - VECTORS["mu_rkv"] + tile:][:, 0:1],
                                  None, ALU.mult))
    return nc.vector.scalar_tensor_tensor(out=dst[:, 1:S], in0=bank[0:rows, 0:S - 1], scalar=k.vec(mu, tile, rows),
                                          in1=dst[:, 1:S], op0=ALU.mult, op1=ALU.add)


def over_units(mask, n=ST):
    return mask.unsqueeze(1).to_broadcast([mask.shape[0], n, mask.shape[1]])


def rwkv(k):
    nc, G, y = k.nc, k.counter, k.y
    with ExitStack() as ctx:
        rkv = k.sbuf(ctx, "rkv", [P, 3 * PAIRS, S])
        wd, ad = k.sbuf(ctx, "wd", [64, S]), k.sbuf(ctx, "ad", [64, S])
        gd = k.sbuf(ctx, "gd", [P, 2, S])
        lora = k.sbuf(ctx, "lora_w", [P, 4, RW])
        k.keep_share = k.sbuf(ctx, "keep_share", [P, 16])
        with k.stage() as block:
            @block.sync
            def _(sp):
                sp.dma_start(lora[:], k.lora).then_inc(k.small_landed, 16)
                k.small += 16
                sp.wait_ge(k.small_landed, k.small)

            @block.vector
            def _(dve):
                c = VECTORS["mu_rkv"]
                nc.vector.tensor_scalar(k.keep_share[:], k.vecs[:, c:c + 16], -1.0, 1.0, ALU.mult, ALU.add)

        jobs = [Job("r_rkv", feature_major(k.h), "dve",
                    lambda e, c, b, t=t: shifted(k, e, c, b, rkv[:, t, :], "mu_rkv", t)) for t in range(3 * PAIRS)]
        jobs.append(Job("r_w", feature_major(k.h, cols=64), "dve",
                        lambda e, c, b: shifted(k, e, c, b, wd[:], "mu_w", 0, 64)))
        jobs.append(Job("r_a", feature_major(k.h, cols=64), "dve",
                        lambda e, c, b: shifted(k, e, c, b, ad[:], "mu_a", 0, 64)))
        jobs.append(Job("r_g", feature_major(k.h), "dve",
                        lambda e, c, b: shifted(k, e, c, b, gd[:, 0, :], "mu_g", 0)))
        jobs.append(Job("r_g", feature_major(k.h, cols=LORA_G - P), "dve",
                        lambda e, c, b: shifted(k, e, c, b, gd[0:LORA_G - P, 1, :], "mu_g", 1, LORA_G - P)))
        project(k, jobs)
        with k.stage() as block:
            @block.scalar
            def _(act):
                nc.scalar.activation(wd[:], wd[:], ACT.Tanh)
                nc.scalar.activation(gd[:, 0, :], gd[:, 0, :], ACT.Sigmoid)
                nc.scalar.activation(gd[0:LORA_G - P, 1, :], gd[0:LORA_G - P, 1, :], ACT.Sigmoid)

        step_T = k.sbuf(ctx, "step_T", [P, PAIRS, NCH, CH])
        gain = k.sbuf(ctx, "gain", [P, PAIRS, NCH, CH])
        query = k.sbuf(ctx, "query", [P, PAIRS, S])
        decay = k.sbuf(ctx, "decay", [P, PAIRS, NCH])
        with ExitStack() as pair_ctx:
            bufs = {n: k.sbuf(pair_ctx, n, [P, 2, ST, P]) for n in ("lbT", "lkT", "mbT", "mkT", "inv", "invT", "tmpU")}
            bufs["z"] = k.sbuf(pair_ctx, "zU", [P, 2, ST, CH])
            turned = k.sbuf(pair_ctx, "turned", [P, 4, ST, P])
            for p in range(PAIRS):
                rwkv_operands(k, p, rkv, wd, ad, lora, decay)
                rwkv_units(k, p, rkv, bufs, turned, step_T, gain, query, decay)
        rwkv_recurrence(k, step_T, gain, query, decay)
        rwkv_finish(k, rkv, gd, lora)


def rwkv_operands(k, p, rkv, wd, ad, lora, decay):
    nc, G = k.nc, k.counter
    alpha, rho, beta, kappa, c, a, t1, t2 = (k.h[:, i, :] for i in range(8))
    r, kr, v = rkv[:, p, :], rkv[:, PAIRS + p, :], rkv[:, 2 * PAIRS + p, :]
    w_cols = slice(p * P, (p + 1) * P)
    with k.stage() as block:
        @block.tensor
        def _(pe):
            nc.tensor.matmul(k.banks[0], lora[0:64, 0, w_cols], wd[:], start=True, stop=True)
            nc.tensor.matmul(k.banks[1], lora[0:64, 1, w_cols], ad[:], start=True, stop=True).then_inc(*G("lora_ready").inc())
            pe.wait_ge(*G("square_ready").ge(1))
            nc.tensor.matmul(k.banks[2], k.const("ones_half"), t1, start=True, stop=True).then_inc(*G("sums_ready").inc())
            pe.wait_ge(*G("bonus_terms").ge(1))
            nc.tensor.matmul(k.banks[3], k.const("ones_half"), t1, start=True, stop=True).then_inc(*G("sums_ready").inc())

        @block.scalar
        def _(act):
            chain = Chain(act, G("act_step"))
            act.wait_ge(*G("lora_ready").ge(1))
            nc.scalar.activation(c, k.banks[0], ACT.Sigmoid, bias=k.vec("r_w0", p)).then_inc(*G("gates_ready").inc())
            nc.scalar.activation(a, k.banks[1], ACT.Sigmoid, bias=k.vec("r_a0", p)).then_inc(*G("gates_ready").inc())
            act.wait_ge(*G("kk_ready").ge(1))
            nc.scalar.activation(t1, t2, ACT.Square).then_inc(*G("square_ready").inc())
            act.wait_ge(*G("sums_ready").ge(1))
            nc.scalar.activation(t1, k.banks[2], ACT.Sqrt).then_inc(*G("root_ready").inc())
            act.wait_ge(*G("decays_ready").ge(2))
            nc.scalar.activation(alpha, alpha, ACT.Exp).then_inc(*G("exps_ready").inc())
            nc.scalar.activation(rho, c, ACT.Exp).then_inc(*G("exps_ready").inc())
            nc.scalar.activation(kappa, c, ACT.Exp, scale=-1.0).then_inc(*G("exps_ready").inc())

        @block.vector
        def _(dve):
            chain = Chain(dve, G("dve_step"))
            nc.vector.tensor_scalar(t2, kr, k.vec("r_kk", p), None, ALU.mult).then_inc(*G("kk_ready").inc())
            dve.wait_ge(*G("gates_ready").ge(1))
            chain(nc.vector.tensor_scalar(beta, c, -DECAY, None, ALU.mult))
            nc.vector.tensor_tensor_scan(c, k.const("chunk_start"), beta, 0.0, ALU.mult, ALU.add).then_inc(*G("decays_ready").inc())
            dve.wait_ge(*G("decays_ready").ge(1))
            nc.vector.tensor_tensor(alpha, c, beta, ALU.subtract).then_inc(*G("decays_ready").inc())
            dve.wait_ge(*G("root_ready").ge(1))
            chain(nc.vector.tensor_scalar(t1, t1, 1e-12, None, ALU.max))
            chain(nc.vector.reciprocal(t1, t1))
            chain(nc.vector.tensor_tensor(t2, t2, t1, ALU.mult))
            dve.wait_ge(*G("gates_ready").ge(2))
            chain(nc.vector.tensor_tensor(beta, t2, a, ALU.mult))
            chain(nc.vector.tensor_scalar(a, a, -1.0, k.vec("r_ka", p), ALU.add, ALU.mult))
            chain(nc.vector.scalar_tensor_tensor(out=a, in0=a, scalar=1.0, in1=kr, op0=ALU.add, op1=ALU.mult))
            nc.vector.scalar_tensor_tensor(out=t1, in0=r, scalar=k.vec("r_rk", p), in1=a, op0=ALU.mult,
                                           op1=ALU.mult).then_inc(*G("bonus_terms").inc())
            dve.wait_ge(*G("exps_ready").ge(3))
            chain(nc.vector.tensor_copy(decay[:, p, :], rho.rearrange("p (c t) -> p c t", t=CH)[:, :, CH - 1]))
            nc.vector.tensor_tensor(alpha, alpha, t2, ALU.mult)
            nc.vector.tensor_tensor(rho, rho, r, ALU.mult)
            chain(nc.vector.tensor_tensor(beta, beta, kappa, ALU.mult))
            chain(nc.vector.tensor_tensor(kappa, kappa, a, ALU.mult))
            dve.wait_ge(*G("sums_ready").ge(2))
            nc.vector.tensor_tensor(r, k.banks[3], v, ALU.mult)


def rwkv_units(k, p, rkv, bufs, turned, step_T, gain, query, decay):
    nc, G = k.nc, k.counter
    alpha, rho, beta, kappa = (k.h[:, i, :] for i in range(4))
    v = rkv[:, 2 * PAIRS + p, :]
    ident = k.const("ident")
    lbT, lkT, mbT, mkT, inv, invT, tmp, z = (bufs[n] for n in ("lbT", "lkT", "mbT", "mkT", "inv", "invT", "tmpU", "z"))
    bank = [b.rearrange("p (u t) -> p u t", u=ST) for b in k.banks]
    tok = lambda u: slice(u * P, (u + 1) * P)
    half = [slice(0, CH), slice(CH, P)]

    with k.stage() as block:
        @block.tensor
        def _(pe):
            for i, src in enumerate((alpha, beta, kappa, v)):
                for u in range(ST):
                    last = nc.tensor.transpose(bank[i][:, u, :], src[:, tok(u)], ident)
                last.then_inc(*G("turned_ready").inc())
            for e in range(2):
                rows = half[e]
                for i, (left, right) in enumerate(((beta, alpha), (kappa, alpha), (beta, rho), (kappa, rho), (alpha, beta))):
                    n = 5 * e + i
                    b = (4 + n) % 8
                    if n >= 4:
                        pe.wait_ge(*G("masked_ready").ge(1 + n - 8 + 0) if n >= 8 else G("turned_taken").ge(n - 3))
                    for u in range(ST):
                        last = nc.tensor.matmul(bank[b][:, u, :], left[rows, tok(u)], right[rows, tok(u)],
                                                start=True, stop=True)
                    last.then_inc(*G("product_ready").inc())

        @block.scalar
        def _(act):
            for i in range(4):
                act.wait_ge(*G("turned_ready").ge(i + 1))
                nc.scalar.copy(turned[:, i, :, :], bank[i]).then_inc(*G("turned_taken").inc())

        @block.vector
        def _(dve):
            chain = Chain(dve, G("dve_step"))
            for e in range(2):
                for i, (dst, mask) in enumerate(((lbT, "before"), (lkT, "before"), (mbT, "upto"), (mkT, "upto"))):
                    n = 5 * e + i
                    dve.wait_ge(*G("product_ready").ge(n + 1))
                    if i == 0:
                        nc.vector.tensor_tensor(invT[:, e], bank[(4 + n) % 8], over_units(k.const("level1")), ALU.mult)
                    nc.vector.tensor_tensor(dst[:, e], bank[(4 + n) % 8], over_units(k.const(mask)),
                                            ALU.mult).then_inc(*G("masked_ready").inc())
                n = 5 * e + 4
                dve.wait_ge(*G("product_ready").ge(n + 1))
                chain(nc.vector.tensor_tensor(inv[:, e], bank[(4 + n) % 8], over_units(k.const("level1_lower")), ALU.mult))
                nc.vector.tensor_tensor(invT[:, e], over_units(ident), invT[:, e], ALU.subtract)
                nc.vector.tensor_tensor(inv[:, e], over_units(ident), inv[:, e], ALU.subtract).then_inc(*G("masked_ready").inc())

    levels = [b for b in (2, 4, 8, 16, 32) if b < CH]
    with k.stage() as block:
        @block.tensor
        def _(pe):
            for e in range(2):
                for u in range(ST):
                    last = nc.tensor.matmul(bank[6][:, u, e * CH:(e + 1) * CH], lkT[:, e, u, :], turned[:, 3, u, half[e]],
                                            start=True, stop=True)
            last.then_inc(*G("z_ready").inc())
            for i, b in enumerate(levels):
                for e in range(2):
                    n = 2 * i + e
                    pe.wait_ge(*G("part_ready").ge(n + 1))
                    if i:
                        pe.wait_ge(*G("inverse_ready").ge(n - 1))
                    for u in range(ST):
                        last = nc.tensor.matmul(bank[3 * e][:, u, :], lkT[:, e, u, :], inv[:, e, u, :], start=True, stop=True)
                    last.then_inc(*G("cx_ready").inc())
                for e in range(2):
                    n = 2 * i + e
                    pe.wait_ge(*G("cx_taken").ge(n + 1))
                    for u in range(ST):
                        nc.tensor.matmul(bank[3 * e + 1][:, u, :], invT[:, e, u, :], tmp[:, e, u, :], start=True, stop=True)
                        last = nc.tensor.matmul(bank[3 * e + 2][:, u, :], tmp[:, e, u, :], invT[:, e, u, :], start=True, stop=True)
                    last.then_inc(*G("xcx_ready").inc())

        @block.gpsimd
        def _(pool):
            for i, b in enumerate(levels):
                for e in range(2):
                    n = 2 * i + e
                    if i == 0:
                        pool.wait_ge(*G("z_ready").ge(1))
                    else:
                        pool.wait_ge(*G("cx_ready").ge(n - 1))
                    nc.gpsimd.tensor_tensor(lkT[:, e], lbT[:, e], over_units(k.const(f"level{b}")),
                                            ALU.mult).then_inc(*G("part_ready").inc())

        @block.scalar
        def _(act):
            act.wait_ge(*G("z_ready").ge(1))
            for e in range(2):
                nc.scalar.copy(z[:, e], bank[6][:, :, e * CH:(e + 1) * CH])
            for i, b in enumerate(levels):
                for e in range(2):
                    n = 2 * i + e
                    act.wait_ge(*G("cx_ready").ge(n + 1))
                    if i:
                        act.wait_ge(*G("xcx_ready").ge(n - 1))
                    nc.scalar.copy(tmp[:, e], bank[3 * e]).then_inc(*G("cx_taken").inc())

        @block.vector
        def _(dve):
            for i, b in enumerate(levels):
                for e in range(2):
                    dve.wait_ge(*G("xcx_ready").ge(2 * i + e + 1))
                    nc.vector.tensor_tensor(inv[:, e], inv[:, e], bank[3 * e + 1], ALU.subtract)
                    nc.vector.tensor_tensor(invT[:, e], invT[:, e], bank[3 * e + 2], ALU.subtract).then_inc(*G("inverse_ready").inc())

    wu = inv
    with k.stage() as block:
        @block.tensor
        def _(pe):
            for e in range(2):
                for u in range(ST):
                    nc.tensor.matmul(bank[e][:, u, 0:CH], invT[:, e, u, :], turned[:, 0, u, half[e]], start=True, stop=True)
                    last = nc.tensor.matmul(bank[e][:, u, CH:P], invT[:, e, u, :], z[:, e, u, :], start=True, stop=True)
                last.then_inc(*G("wu_ready").inc())
            for e in range(2):
                rows = half[e]
                pe.wait_ge(*G("wu_taken").ge(e + 1))
                for u in range(ST):
                    nc.tensor.matmul(bank[2][rows, u, :], wu[:, e, u, 0:CH], mbT[:, e, u, :], start=True, stop=True)
                for u in range(ST):
                    nc.tensor.matmul(bank[3][rows, u, :], turned[:, 3, u, rows], mkT[:, e, u, :], start=True, stop=False)
                    nc.tensor.matmul(bank[3][rows, u, :], wu[:, e, u, CH:P], mbT[:, e, u, :], start=False, stop=True)
                for c in range(NCH):
                    u, t, q = c // 2, half[c % 2], 2 * (c % 2)
                    to = slice(u * CH, (u + 1) * CH)
                    nc.tensor.matmul(k.banks[4 + q][rows, to], wu[t, e, u, 0:CH], turned[t, 1, u, rows], start=True, stop=True)
                    nc.tensor.matmul(k.banks[5 + q][rows, to], turned[t, 2, u, rows], turned[t, 3, u, rows], start=True, stop=False)
                    last = nc.tensor.matmul(k.banks[5 + q][rows, to], turned[t, 1, u, rows], wu[t, e, u, CH:P], start=False, stop=True)
            last.then_inc(*G("parts_ready").inc())

        @block.scalar
        def _(act):
            for e in range(2):
                act.wait_ge(*G("wu_ready").ge(e + 1))
                nc.scalar.mul(wu[:, e], bank[e], -1.0).then_inc(*G("wu_taken").inc())
            act.wait_ge(*G("parts_ready").ge(1))
            nc.scalar.copy(k.y[:, 4 + p, :], k.banks[3])

        @block.vector
        def _(dve):
            dve.wait_ge(*G("parts_ready").ge(1))
            nc.vector.tensor_tensor(query[:, p, :], k.banks[2], rho, ALU.add)
            for q in range(2):
                step, new = (k.banks[b + 2 * q][:, 0:ST * CH].rearrange("p (c k) -> p c k", c=ST) for b in (4, 5))
                for e in range(2):
                    nc.vector.tensor_tensor(step_T[half[e], p, q::2], step[half[e]], over_units(ident[half[e], half[e]]), ALU.add)
                nc.vector.tensor_tensor(gain[:, p, q::2], new, decay[:, p, q::2].unsqueeze(2).to_broadcast([P, ST, CH]), ALU.mult)


def rwkv_recurrence(k, step_T, gain, query, decay):
    nc, G = k.nc, k.counter
    half = [slice(0, CH), slice(CH, P)]
    state = k.h[:, 0:4, :].rearrange("p t n -> p (t n)").rearrange("p (c q v) -> p c q v", c=NCH, q=PAIRS)
    bank = [b[:, 0:PAIRS * CH].rearrange("p (q v) -> p q v", q=PAIRS) for b in k.banks]
    with k.stage() as block:
        @block.vector
        def _(dve):
            chain = Chain(dve, G("dve_step"))
            nc.vector.memset(state[:, 0], 0.0).then_inc(*G("state_ready").inc())
            for c in range(NCH - 1):
                dve.wait_ge(*G("stepped").ge(c + 1))
                chain(nc.vector.tensor_tensor(state[:, c + 1], bank[c % 2],
                                              decay[:, :, c].unsqueeze(2).to_broadcast([P, PAIRS, CH]), ALU.mult))
                nc.vector.tensor_tensor(state[:, c + 1], state[:, c + 1], gain[:, :, c, :],
                                        ALU.add).then_inc(*G("state_ready").inc())
            for p in range(PAIRS):
                dve.wait_ge(*G("output_ready").ge(p + 1))
                nc.vector.tensor_tensor(k.y[:, 4 + p, :], k.banks[2 + p], k.y[:, 4 + p, :], ALU.add)

        @block.tensor
        def _(pe):
            for c in range(NCH - 1):
                pe.wait_ge(*G("state_ready").ge(c + 1))
                for p in range(PAIRS):
                    for rows in half:
                        last = nc.tensor.matmul(bank[c % 2][rows, p, :], step_T[rows, p, c, :], state[rows, c, p, :],
                                                start=True, stop=True)
                last.then_inc(*G("stepped").inc())
            pe.wait_ge(*G("state_ready").ge(NCH))
            for p in range(PAIRS):
                for c in range(NCH):
                    for rows in half:
                        last = nc.tensor.matmul(k.banks[2 + p][rows, c * CH:(c + 1) * CH], state[rows, c, p, :],
                                                query[rows, p, c * CH:(c + 1) * CH], start=True, stop=True)
                last.then_inc(*G("output_ready").inc())


def rwkv_finish(k, rkv, gd, lora):
    nc, G = k.nc, k.counter
    t = [k.h[:, i, :] for i in range(8)]
    with k.stage() as block:
        @block.tensor
        def _(pe):
            for p in range(PAIRS):
                cols = slice(p * P, (p + 1) * P)
                if p >= 2:
                    pe.wait_ge(*G("normed").ge(p - 1))
                b = 4 * (p % 2)
                nc.tensor.matmul(k.banks[b], k.const("ones_half"), k.y[:, 4 + p, :], start=True,
                                 stop=True).then_inc(*G("sums_ready").inc())
                nc.tensor.matmul(k.banks[b + 2], lora[:, 2, cols], gd[:, 0, :], start=True, stop=False)
                nc.tensor.matmul(k.banks[b + 2], lora[0:LORA_G - P, 3, cols], gd[0:LORA_G - P, 1, :], start=False, stop=True)
                pe.wait_ge(*G("square_ready").ge(p + 1))
                nc.tensor.matmul(k.banks[b + 1], k.const("ones_half"), t[p % 2], start=True,
                                 stop=True).then_inc(*G("sums_ready").inc())

        @block.scalar
        def _(act):
            for p in range(PAIRS):
                act.wait_ge(*G("centred_ready").ge(p + 1))
                nc.scalar.activation(t[p % 2], k.y[:, 4 + p, :], ACT.Square).then_inc(*G("square_ready").inc())
                act.wait_ge(*G("var_ready").ge(p + 1))
                nc.scalar.activation(t[2 + p % 2], t[2 + p % 2], ACT.Sqrt).then_inc(*G("root_ready").inc())

        @block.vector
        def _(dve):
            chain = Chain(dve, G("dve_step"))
            for p in range(PAIRS):
                b, y, rs = 4 * (p % 2), k.y[:, 4 + p, :], t[2 + p % 2]
                dve.wait_ge(*G("sums_ready").ge(2 * p + 1))
                nc.vector.scalar_tensor_tensor(out=y, in0=k.banks[b], scalar=-1.0 / RHD, in1=y, op0=ALU.mult,
                                               op1=ALU.add).then_inc(*G("centred_ready").inc())
                dve.wait_ge(*G("sums_ready").ge(2 * p + 2))
                nc.vector.tensor_scalar(rs, k.banks[b + 1], 1.0 / RHD, GN_EPS, ALU.mult, ALU.add).then_inc(*G("var_ready").inc())
                dve.wait_ge(*G("root_ready").ge(p + 1))
                chain(nc.vector.reciprocal(rs, rs))
                chain(nc.vector.scalar_tensor_tensor(out=y, in0=y, scalar=k.vec("r_gn_g", p), in1=rs, op0=ALU.mult, op1=ALU.mult))
                chain(nc.vector.scalar_tensor_tensor(out=y, in0=y, scalar=k.vec("r_gn_b", p), in1=rkv[:, p, :],
                                                     op0=ALU.add, op1=ALU.add))
                nc.vector.tensor_tensor(y, k.banks[b + 2], y, ALU.mult).then_inc(*G("normed").inc())


def add_to_x(k, name, x, ktiles=DT, tiles=1):
    nc = k.nc
    project(k, [Job(name, feature_major(x, ktiles), "dve", lambda e, c, b, m=m: nc.vector.tensor_tensor(
        k.x[:, m, :], k.x[:, m, :], b, ALU.add), tiles) for m in range(DT)])


class Unit:

    def __init__(self, pairs, keys, value, width, out, row=0, mask=None):
        self.pairs, self.keys, self.value, self.width, self.out, self.row, self.mask = (
            pairs, keys, value, width, out, row, mask)


def attend(k, units, scale):
    nc, G = k.nc, k.counter
    n = len(units)
    scored, maxed, expd, scaled = G("score_ready"), G("max_ready"), G("exp_ready"), G("prob_ready")
    turned, copied, summed, taken = G("turned_ready"), G("turned_taken"), G("sum_ready"), G("out_taken")
    with ExitStack() as ctx:
        s = k.sbuf(ctx, k.fresh("scores"), [P, 3, S])
        pT = k.sbuf(ctx, k.fresh("probT"), [P, 2, S])
        small = k.sbuf(ctx, k.fresh("row_stats"), [P, 3, 4])

        with k.stage() as block:
            @block.sync
            def _(sp):
                k.prefetch(sp, k.used)

            @block.tensor
            def _(pe):
                for i in range(n + 2):
                    if i < n:
                        un = units[i]
                        if i >= 2:
                            pe.wait_ge(*expd.ge(i - 1))
                        for j, (q, key) in enumerate(un.pairs):
                            last = nc.tensor.matmul(k.banks[i % 2][:, 0:un.keys], q, key, start=(j == 0),
                                                    stop=(j == len(un.pairs) - 1))
                        last.then_inc(*scored.inc())
                    if 1 <= i <= n:
                        m, un = i - 1, units[i - 1]
                        pe.wait_ge(*scaled.ge(m + 1))
                        if m >= 2:
                            pe.wait_ge(*copied.ge(m - 1))
                        for c in range(0, un.keys, P):
                            last = nc.tensor.transpose(k.banks[2 + m % 2][:, c:c + P], s[:, m % 3, c:c + P], k.const("ident"))
                        last.then_inc(*turned.inc())
                    if 2 <= i:
                        m, un = i - 2, units[i - 2]
                        pe.wait_ge(*copied.ge(m + 1))
                        if m >= 2:
                            pe.wait_ge(*taken.ge(m - 1))
                        rows = slice(un.row, un.row + un.width)
                        for part, (lo, value) in enumerate(un.value):
                            for c in range(0, un.keys, P):
                                last = nc.tensor.matmul(k.banks[4 + m % 2][rows, lo:lo + P], value(c // P),
                                                        pT[:, m % 2, c:c + P], start=(c == 0), stop=(c == un.keys - P))
                        last.then_inc(*summed.inc())

            @block.vector
            def _(dve):
                chain = Chain(dve, G("dve_step"))
                for i in range(n + 1):
                    if i < n:
                        un = units[i]
                        st = small[:, i % 3, :]
                        dve.wait_ge(*scored.ge(i + 1))
                        src = k.banks[i % 2][:, 0:un.keys]
                        if un.mask is not None:
                            if i >= 3:
                                dve.wait_ge(*turned.ge(i - 2))
                            chain(nc.vector.scalar_tensor_tensor(out=s[:, i % 3, 0:un.keys], in0=src, scalar=scale,
                                                                 in1=un.mask, op0=ALU.mult, op1=ALU.add))
                            src = s[:, i % 3, 0:un.keys]
                        chain(nc.vector.tensor_reduce(st[:, 0:1], src, AX, ALU.max))
                        nc.vector.tensor_scalar(st[:, 1:2], st[:, 0:1], -1.0 if un.mask is not None else -scale, None,
                                                ALU.mult).then_inc(*maxed.inc())
                    if i:
                        m, un = i - 1, units[i - 1]
                        st = small[:, m % 3, :]
                        dve.wait_ge(*expd.ge(m + 1))
                        chain(nc.vector.reciprocal(st[:, 3:4], st[:, 2:3]))
                        nc.vector.tensor_scalar(s[:, m % 3, 0:un.keys], s[:, m % 3, 0:un.keys], st[:, 3:4], None,
                                                ALU.mult).then_inc(*scaled.inc())

            @block.scalar
            def _(act):
                for i in range(n + 2):
                    if i < n:
                        un = units[i]
                        act.wait_ge(*maxed.ge(i + 1))
                        if i >= 3:
                            act.wait_ge(*turned.ge(i - 2))
                        src = s[:, i % 3, 0:un.keys] if un.mask is not None else k.banks[i % 2][:, 0:un.keys]
                        nc.scalar.activation(s[:, i % 3, 0:un.keys], src, ACT.Exp, bias=small[:, i % 3, 1:2],
                                             scale=1.0 if un.mask is not None else scale,
                                             accum_out=small[:, i % 3, 2:3]).then_inc(*expd.inc())
                    if 1 <= i <= n:
                        m, un = i - 1, units[i - 1]
                        act.wait_ge(*turned.ge(m + 1))
                        if m >= 2:
                            act.wait_ge(*summed.ge(m - 1))
                        nc.scalar.copy(pT[:, m % 2, 0:un.keys], k.banks[2 + m % 2][:, 0:un.keys]).then_inc(*copied.inc())
                    if 2 <= i:
                        m, un = i - 2, units[i - 2]
                        act.wait_ge(*summed.ge(m + 1))
                        rows = slice(un.row, un.row + un.width)
                        w = len(un.value) * P
                        nc.scalar.copy(un.out, k.banks[4 + m % 2][rows, 0:w] if w == P else
                                       k.banks[4 + m % 2][rows, 0:w].rearrange("p (a t) -> p a t", t=P)).then_inc(*taken.inc())


def copy_to(k, dst, n=S):
    return lambda e, c, b, t: k.nc.scalar.copy(dst[:, t, 0:n], b[:, 0:n])


def memory_attention(k):
    nc = k.nc
    with ExitStack() as ctx:
        key = k.sbuf(ctx, "x_key", [P, DT, MEM])
        value = k.sbuf(ctx, "x_value", [P, MEM // P, D])
        q = k.sbuf(ctx, "x_query", [P, DT, S])
        o = k.sbuf(ctx, "x_out", [P, DT, S])
        load_memory(k, k.memT, "norm_mem", o)
        mem = o[:, :, 0:MEM]
        project(k, [Job("x_k", feature_major(mem, n=MEM), "act",
                        lambda e, c, b, t=t: nc.scalar.copy(key[:, t, :], b[:, 0:MEM])) for t in range(DT)])
        for half in range(2):
            project_tokens(k, "x_v", mem, MEM, lambda act, t, b: nc.scalar.copy(value[:, t, half * 512:(half + 1) * 512], b))
        rms_norm(k, k.x, k.h, "norm_x", S)
        project(k, [Job("x_q", feature_major(k.h), "act",
                        lambda e, c, b, t=t: nc.scalar.copy(q[:, t, :], b)) for t in range(DT)])
        units = []
        for h in range(XH):
            for t in range(ST):
                tok = slice(t * P, (t + 1) * P)
                units.append(Unit([(q[:, 2 * h + j, tok], key[:, 2 * h + j, :]) for j in range(2)], MEM,
                                  [(P * j, lambda c, h=h, j=j: value[:, c, (2 * h + j) * P:(2 * h + j + 1) * P]) for j in range(2)],
                                  P, o[:, 2 * h:2 * h + 2, tok]))
        attend(k, units, XHD ** -0.5)
        add_to_x(k, "x_o", o)


def load_memory(k, dram, gain, dst):
    with k.stage() as block:
        @block.sync
        def _(sp):
            sp.dma_start(dst[:, :, MEM:2 * MEM], dram).then_inc(k.small_landed, 16)
            k.small += 16
            sp.wait_ge(k.small_landed, k.small)
    rms_norm(k, dst[:, :, MEM:2 * MEM], dst, gain, MEM)


def conv_glu(k):
    nc = k.nc
    rms_norm(k, k.x, k.h, "norm_ffn", S)
    with ExitStack() as ctx:
        act_t = k.sbuf(ctx, "ffn_act", [P, FT, S])
        conv_ready, silu_ready = k.counter("conv_ready"), k.counter("silu_ready")
        value_taken = k.counter("value_taken")
        first = k.used
        k.used += 2 * FT

        def times_value(dve, f):
            dve.wait_ge(*silu_ready.ge(f + 1))
            dve.wait_ge(k.tile_used, first + 2 * f + 2)
            nc.vector.tensor_tensor(act_t[:, f, :], k.banks[2 * (f % 4) + 1], act_t[:, f, :],
                                    ALU.mult).then_inc(*value_taken.inc())

        with k.stage() as block:
            @block.sync
            def _(sp):
                k.prefetch(sp, k.used)

            @block.tensor
            def _(pe):
                for f in range(FT):
                    for half, taken in enumerate((conv_ready, value_taken)):
                        t = first + 2 * f + half
                        pe.wait_ge(*k.tile_landed(t))
                        if f >= 4:
                            pe.wait_ge(*taken.ge(f - 3))
                        feature_major(k.h)(k, [k.slot(t)], k.banks[2 * (f % 4) + half]).then_inc(k.tile_used, 1)

            @block.vector
            def _(dve):
                chain = Chain(dve, k.counter("dve_step"))
                for f in range(FT):
                    dve.wait_ge(k.tile_used, first + 2 * f + 1)
                    conv(k, dve, chain, k.banks[2 * (f % 4)], act_t[:, f, :], "f_conv_w", "f_conv_b",
                         f, 3).then_inc(*conv_ready.inc())
                    if f:
                        times_value(dve, f - 1)
                times_value(dve, FT - 1)

            @block.scalar
            def _(act):
                for f in range(FT):
                    act.wait_ge(*conv_ready.ge(f + 1))
                    nc.scalar.activation(act_t[:, f, :], act_t[:, f, :], ACT.Silu).then_inc(*silu_ready.inc())
        add_to_x(k, "f_down", act_t, FT, 3)


def rope_tables(k, tables):
    nc, G = k.nc, k.counter
    magic = 1.5 * 2.0 ** 23
    c1 = 6.28125
    c2 = float(np.float32(2 * math.pi - c1))
    c2 = float((np.array([c2], np.float32).view(np.uint32) & 0xFFFFF000).view(np.float32)[0])
    c3 = 2 * math.pi - c1 - c2
    top = float(np.nextafter(np.float32(math.pi), np.float32(0)))
    with ExitStack() as ctx:
        raw = k.sbuf(ctx, "pos_raw", [P, S], I32)
        pos = k.sbuf(ctx, "pos", [P, S])
        turns = k.sbuf(ctx, "pos_turns", [P, S])
        with k.stage() as block:
            @block.sync
            def _(sp):
                sp.dma_start(raw[:], k.positions.to_broadcast([P, S])).then_inc(k.small_landed, 16)
                k.small += 16

            @block.vector
            def _(dve):
                chain = Chain(dve, G("dve_step"))
                dve.wait_ge(k.small_landed, k.small)
                chain(nc.vector.tensor_copy(pos[:], raw[:]))
                for i, (freq, cos, sin) in enumerate(tables):
                    chain(nc.vector.tensor_scalar(cos, pos[:], k.const(freq), None, ALU.mult))
                    chain(nc.vector.tensor_scalar(turns[:], cos, 1.0 / (2 * math.pi), magic, ALU.mult, ALU.add))
                    chain(nc.vector.tensor_scalar(turns[:], turns[:], -magic, None, ALU.add))
                    for part in (c1, c2, c3):
                        chain(nc.vector.scalar_tensor_tensor(out=cos, in0=turns[:], scalar=-part, in1=cos,
                                                             op0=ALU.mult, op1=ALU.add))
                    nc.vector.tensor_scalar(cos, cos, top, -top, ALU.min, ALU.max).then_inc(*G("angle_ready").inc())
                for i, (freq, cos, sin) in enumerate(tables):
                    dve.wait_ge(*G("abs_ready").ge(i + 1))
                    nc.vector.tensor_scalar(cos, cos, -1.0, math.pi / 2, ALU.mult, ALU.add).then_inc(*G("cos_arg_ready").inc())

            @block.scalar
            def _(act):
                for i, (freq, cos, sin) in enumerate(tables):
                    act.wait_ge(*G("angle_ready").ge(i + 1))
                    nc.scalar.activation(sin, cos, ACT.Sin)
                    nc.scalar.activation(cos, cos, ACT.Abs).then_inc(*G("abs_ready").inc())
                for i, (freq, cos, sin) in enumerate(tables):
                    act.wait_ge(*G("cos_arg_ready").ge(i + 1))
                    nc.scalar.activation(cos, cos, ACT.Sin)


def head_norms(k, items, n=S):
    nc, G = k.nc, k.counter
    with ExitStack() as ctx:
        sq = k.sbuf(ctx, k.fresh("head_sq"), [P, 2, n])
        rs = k.sbuf(ctx, k.fresh("head_rs"), [P, 2, n])
        with k.stage() as block:
            @block.sync
            def _(sp):
                k.prefetch(sp, k.used)

            @block.scalar
            def _(act):
                for i in range(len(items) + 1):
                    if i < len(items):
                        x, rows = items[i][:2]
                        if i >= 2:
                            act.wait_ge(*G("sums_ready").ge(i - 1))
                        nc.scalar.activation(sq[0:rows, i % 2, :], x, ACT.Square).then_inc(*G("square_ready").inc())
                    if i:
                        act.wait_ge(*G("mean_ready").ge(i))
                        r = rs[0:items[i - 1][1], (i - 1) % 2, :]
                        nc.scalar.activation(r, r, ACT.Sqrt).then_inc(*G("root_ready").inc())

            @block.tensor
            def _(pe):
                for i, (x, rows, ones, size, gain) in enumerate(items):
                    pe.wait_ge(*G("square_ready").ge(i + 1))
                    if i >= 2:
                        pe.wait_ge(*G("mean_ready").ge(i - 1))
                    nc.tensor.matmul(k.banks[i % 2][0:rows, 0:n], ones, sq[0:rows, i % 2, :], start=True,
                                     stop=True).then_inc(*G("sums_ready").inc())

            @block.vector
            def _(dve):
                chain = Chain(dve, G("dve_step"))
                for i, (x, rows, ones, size, gain) in enumerate(items):
                    r = rs[0:rows, i % 2, :]
                    dve.wait_ge(*G("sums_ready").ge(i + 1))
                    nc.vector.tensor_scalar(r, k.banks[i % 2][0:rows, 0:n], 1.0 / size, EPS, ALU.mult,
                                            ALU.add).then_inc(*G("mean_ready").inc())
                    dve.wait_ge(*G("root_ready").ge(i + 1))
                    chain(nc.vector.reciprocal(r, r))
                    nc.vector.scalar_tensor_tensor(out=x, in0=x, scalar=k.vec(gain, 0, rows), in1=r, op0=ALU.mult,
                                                   op1=ALU.mult).then_inc(*G("head_ready").inc())


def rotate_tiles(k, items):
    nc, G = k.nc, k.counter
    with ExitStack() as ctx:
        tmp = k.sbuf(ctx, k.fresh("turned_half"), [P, 2, S])
        with k.stage() as block:
            @block.sync
            def _(sp):
                k.prefetch(sp, k.used)

            @block.tensor
            def _(pe):
                for i, (x, rows, matrix, cos, sin) in enumerate(items):
                    if i >= 2:
                        pe.wait_ge(*G("sin_taken").ge(i - 1))
                    nc.tensor.matmul(k.banks[i % 2][0:rows, :], matrix, x, start=True, stop=True).then_inc(*G("swapped").inc())

            @block.vector
            def _(dve):
                chain = Chain(dve, G("dve_step"))
                for i, (x, rows, matrix, cos, sin) in enumerate(items):
                    dve.wait_ge(*G("swapped").ge(i + 1))
                    nc.vector.tensor_tensor(tmp[0:rows, i % 2, :], k.banks[i % 2][0:rows, :], sin,
                                            ALU.mult).then_inc(*G("sin_taken").inc())
                    chain(nc.vector.tensor_tensor(x, x, cos, ALU.mult))
                    nc.vector.tensor_tensor(x, x, tmp[0:rows, i % 2, :], ALU.add)


def choose_keys(k, qi, ki, wi, chosen):
    nc, G = k.nc, k.counter
    with ExitStack() as ctx:
        r = k.sbuf(ctx, "relu_dots", [P, 2, S])
        top = k.sbuf(ctx, "top8", [P, 8])
        with k.stage() as block:
            @block.sync
            def _(sp):
                k.prefetch(sp, k.used)

            @block.tensor
            def _(pe):
                for t in range(1, ST):
                    keys = (t + 1) * P
                    for h in range(AH):
                        i = (t - 1) * AH + h
                        rows = slice(64 * (h % 2), 64 * (h % 2) + 64)
                        if i >= 2:
                            pe.wait_ge(*G("relu_ready").ge(i - 1))
                        nc.tensor.matmul(k.banks[i % 2][:, 0:keys], qi[rows, h // 2, t * P:(t + 1) * P], ki[rows, 0:keys],
                                         start=True, stop=True).then_inc(*G("dots_ready").inc())

            @block.scalar
            def _(act):
                for t in range(1, ST):
                    keys = (t + 1) * P
                    for h in range(AH):
                        i = (t - 1) * AH + h
                        act.wait_ge(*G("dots_ready").ge(i + 1))
                        if i >= 2:
                            act.wait_ge(*G("dots_added").ge(i - 1))
                        nc.scalar.activation(r[:, i % 2, 0:keys], k.banks[i % 2][:, 0:keys], ACT.Relu,
                                             scale=AHD ** -0.5).then_inc(*G("relu_ready").inc())

            @block.vector
            def _(dve):
                chain = Chain(dve, G("dve_step"))
                chain(nc.vector.tensor_scalar(wi, wi, AH ** -0.5, None, ALU.mult))
                chain(nc.vector.tensor_copy(chosen[:, 0, 0:P], k.const("causal")[:, S - P:S]))
                for t in range(1, ST):
                    keys = (t + 1) * P
                    acc = chosen[:, t, 0:keys]
                    for h in range(AH):
                        i = (t - 1) * AH + h
                        dve.wait_ge(*G("relu_ready").ge(i + 1))
                        w = wi[:, t, h:h + 1]
                        if h == 0:
                            ins = nc.vector.tensor_scalar(acc, r[:, i % 2, 0:keys], w, None, ALU.mult)
                        else:
                            dve.wait_ge(*G("dots_added").ge(i))
                            ins = nc.vector.scalar_tensor_tensor(out=acc, in0=r[:, i % 2, 0:keys], scalar=w, in1=acc,
                                                                 op0=ALU.mult, op1=ALU.add)
                        ins.then_inc(*G("dots_added").inc())
                    dve.wait_ge(*G("dots_added").ge(t * AH))
                    chain(nc.vector.tensor_tensor(acc, acc, k.const("causal")[:, S - keys:S], ALU.add))
                    for _ in range(TOPK // 8):
                        chain(nc.vector.max(out=top[:], in_=acc))
                        chain(nc.vector.match_replace(out=acc, in_to_replace=top[:], in_values=acc, imm_value=CHOSEN))
                    chain(nc.vector.tensor_scalar(acc, acc, CHOSEN / 2, NEG, ALU.is_gt, ALU.mult))


def gate_branch(k, y, z):
    nc = k.nc
    with k.stage() as block:
        @block.vector
        def _(dve):
            for t in range(BW // P):
                nc.vector.tensor_tensor(y[:, t, :], y[:, t, :], z[:, t, :], ALU.mult)


def silu_jobs(k, name, z):
    return [Job(name, feature_major(k.h), "act", lambda e, c, b, t=t: k.nc.scalar.activation(z[:, t, :], b, ACT.Silu))
            for t in range(BW // P)]


def sparse_branch(k, y, cos, sin):
    nc = k.nc
    with ExitStack() as ctx:
        qk = k.sbuf(ctx, "a_qk", [P, 8, S])
        qi = k.sbuf(ctx, "a_qi", [P, 4, S])
        ki = k.sbuf(ctx, "a_ki", [P, S])
        wi = k.sbuf(ctx, "a_wi", [P, ST, AH])
        wiT = k.sbuf(ctx, "a_wiT", [AH, S])
        v = k.sbuf(ctx, "a_v", [P, ST, AH * AHD])
        z = k.sbuf(ctx, "a_z", [P, 4, S])
        chosen = k.sbuf(ctx, "a_chosen", [P, ST, S])

        jobs = [Job("a_qk", feature_major(k.h), "act", lambda e, c, b, t=t: nc.scalar.copy(qk[:, t, :], b)) for t in range(8)]
        jobs += [Job("a_qi", feature_major(k.h), "act", lambda e, c, b, t=t: nc.scalar.copy(qi[:, t, :], b)) for t in range(4)]
        jobs.append(Job("a_ki", feature_major(k.h), "act", lambda e, c, b: nc.scalar.copy(ki[:], b)))
        jobs.append(Job("a_wi", feature_major(k.h, cols=AH), "act", lambda e, c, b: nc.scalar.copy(wiT[:], b[0:AH, :])))
        project(k, jobs)
        project_tokens(k, "a_v", k.h, S, lambda act, t, b: nc.scalar.copy(v[:, t, :], b))
        project(k, silu_jobs(k, "a_z", z))
        with k.stage() as block:
            @block.tensor
            def _(pe):
                for t in range(ST):
                    last = nc.tensor.matmul(k.banks[0][:, t * AH:(t + 1) * AH], wiT[:, t * P:(t + 1) * P],
                                            k.const("ident", AH)[:, 0:AH], start=True, stop=True)
                last.then_inc(*k.counter("turned_ready").inc())

            @block.vector
            def _(dve):
                dve.wait_ge(*k.counter("turned_ready").ge(1))
                nc.vector.tensor_copy(wi[:].rearrange("p t h -> p (t h)"), k.banks[0][:, 0:ST * AH])
        half = k.const("ones_half")
        head_norms(k, [(qk[:, t, :], P, half, AHD, "g_qn_a_2" if t < 4 else "g_kn_a_2") for t in range(8)])
        tiles = [qk[:, t, :] for t in range(8)] + [qi[:, t, :] for t in range(4)] + [ki[:]]
        rotate_tiles(k, [(x, P, k.const("rotate_a"), cos, sin) for x in tiles])
        choose_keys(k, qi, ki, wi[:], chosen)
        units = []
        for h in range(AH):
            rows = slice(AHD * (h % 2), AHD * (h % 2) + AHD)
            for t in range(ST):
                keys, tok = (t + 1) * P, slice(t * P, (t + 1) * P)
                units.append(Unit([(qk[rows, h // 2, tok], qk[rows, 4 + h // 2, 0:keys])], keys,
                                  [(0, lambda c, h=h: v[:, c, h * AHD:(h + 1) * AHD])], AHD,
                                  y[rows, h // 2, tok], AHD * (h % 2), chosen[:, t, 0:keys]))
        attend(k, units, AHD ** -0.5)
        gate_branch(k, y, z)


def latent_branch(k, y, cos, sin):
    nc = k.nc
    with ExitStack() as ctx:
        c = k.sbuf(ctx, "b_c", [P, 5, S])
        q, key = k.sbuf(ctx, "b_q", [BQK, BH, S]), k.sbuf(ctx, "b_k", [BQK, BH, S])
        v = k.sbuf(ctx, "b_v", [P, ST, BH * BV])
        z = k.sbuf(ctx, "b_z", [P, 4, S])
        rope = slice(BNOPE, BQK)

        def spread_rope(e, ch, b):
            for h in range(BH):
                last = nc.scalar.copy(key[rope, h, :], b[rope, :])
            return last
        jobs = [Job("b_c", feature_major(k.h), "act", lambda e, ch, b, t=t: nc.scalar.copy(c[:, t, :], b)) for t in range(5)]
        jobs.append(Job("b_kr", feature_major(k.h, cols=BROPE, row=BNOPE), "act", spread_rope))
        project(k, jobs)
        rms_norm(k, c[:, 0:3, :], c[:, 0:3, :], "g_cq_2", S, 3)
        rms_norm(k, c[:, 3:5, :], c[:, 3:5, :], "g_ckv_2", S, 2)
        project(k, [Job("b_uq", feature_major(c, 3, BQK), "act",
                        lambda e, ch, b, h=h: nc.scalar.copy(q[:, h, :], b[0:BQK, :])) for h in range(BH)])
        t = k.used
        k.used += 1
        with k.stage() as block:
            @block.sync
            def _(sp):
                k.prefetch(sp, k.used)

            @block.tensor
            def _(pe):
                assert k.plan[t][0] == "b_uk"
                pe.wait_ge(*k.tile_landed(t))
                for h in range(BH):
                    w = k.slot(t)[:, h * P:(h + 1) * P]
                    for j in range(2):
                        last = nc.tensor.matmul(k.banks[h][0:BNOPE, :], w[:, j * BNOPE:(j + 1) * BNOPE], c[:, 3 + j, :],
                                                start=(j == 0), stop=(j == 1))
                last.then_inc(k.tile_used, 1)

            @block.scalar
            def _(act):
                act.wait_ge(k.tile_used, t + 1)
                for h in range(BH):
                    nc.scalar.copy(key[0:BNOPE, h, :], k.banks[h][0:BNOPE, :])
        project_tokens(k, "b_uv", c[:, 3:5, :], S, lambda act, t, b: nc.scalar.copy(v[:, t, :], b), ktiles=2)
        project(k, silu_jobs(k, "b_z", z))
        ones = k.const("ones", BQK)[:, 0:BQK]
        rot = k.const("rotate_b", BQK)
        head_norms(k, [(q[:, h, :], BQK, ones, BQK, "g_qn_b_2") for h in range(BH)] +
                   [(key[:, h, :], BQK, ones, BQK, "g_kn_b_2") for h in range(BH)])
        rotate_tiles(k, [(x[:, h, :], BQK, rot, cos, sin) for x in (q, key) for h in range(BH)])
        units = []
        for h in range(BH):
            rows = slice(BV * (h % 2), BV * (h % 2) + BV)
            for t in range(ST):
                keys, tok = (t + 1) * P, slice(t * P, (t + 1) * P)
                units.append(Unit([(q[:, h, tok], key[:, h, 0:keys])], keys,
                                  [(0, lambda c, h=h: v[:, c, h * BV:(h + 1) * BV])], BV,
                                  y[rows, h // 2, tok], BV * (h % 2), k.const("causal")[:, S - keys:S]))
        attend(k, units, BQK ** -0.5)
        gate_branch(k, y, z)


def memory_branch(k, y):
    nc = k.nc
    with ExitStack() as ctx:
        key = k.sbuf(ctx, "m2_k", [P, 4, MEM])
        value = k.sbuf(ctx, "m2_v", [P, MEM // P, 512])
        q, z = k.sbuf(ctx, "m2_q", [P, 4, S]), k.sbuf(ctx, "m2_z", [P, 4, S])
        memory = k.sbuf(ctx, "m2_mem", [P, DT, S])
        load_memory(k, k.mem2T, "g_mem_2", memory)
        mem = memory[:, :, 0:MEM]
        project(k, [Job("m2_k", feature_major(mem, n=MEM), "act",
                        lambda e, c, b, t=t: nc.scalar.copy(key[:, t, :], b[:, 0:MEM])) for t in range(4)])
        project_tokens(k, "m2_v", mem, MEM, lambda act, t, b: nc.scalar.copy(value[:, t, :], b))
        project(k, [Job("m2_q", feature_major(k.h), "act",
                        lambda e, c, b, t=t: nc.scalar.copy(q[:, t, :], b)) for t in range(4)] + silu_jobs(k, "m2_z", z))
        ones = k.const("ones")
        head_norms(k, [(q[:, h, :], P, ones, P, "g_qn_m_2") for h in range(4)])
        head_norms(k, [(key[:, h, :], P, ones, P, "g_kn_m_2") for h in range(4)], MEM)
        units = []
        for h in range(4):
            for t in range(ST):
                tok = slice(t * P, (t + 1) * P)
                units.append(Unit([(q[:, h, tok], key[:, h, :])], MEM,
                                  [(0, lambda c, h=h: value[:, c, h * P:(h + 1) * P])], P, y[:, h, tok]))
        attend(k, units, P ** -0.5)
        gate_branch(k, y, z)


def merge(k, ys, merged):
    nc = k.nc
    gate_ready, part_taken = k.counter("gate_ready"), k.counter("part_taken")
    first = k.used
    k.used += 2 * NBR * DT
    with ExitStack() as ctx:
        sg = k.sbuf(ctx, "gate_sigmoid", [P, 4, S])
        part = k.sbuf(ctx, "branch_part", [P, S])
        with k.stage() as block:
            @block.sync
            def _(sp):
                k.prefetch(sp, k.used)

            @block.tensor
            def _(pe):
                for i in range(NBR * DT):
                    t = first + 2 * i
                    for half, (x, kt, taken) in enumerate(((k.h, DT, gate_ready), (ys[:, 4 * (i % NBR):4 * (i % NBR) + 4, :], 4, part_taken))):
                        pe.wait_ge(*k.tile_landed(t + half))
                        if i >= 4:
                            pe.wait_ge(*taken.ge(i - 3))
                        feature_major(x, kt)(k, [k.slot(t + half)], k.banks[2 * (i % 4) + half]).then_inc(k.tile_used, 1)

            @block.scalar
            def _(act):
                for i in range(NBR * DT):
                    act.wait_ge(k.tile_used, first + 2 * i + 1)
                    if i >= 4:
                        act.wait_ge(*part_taken.ge(i - 3))
                    nc.scalar.activation(sg[:, i % 4, :], k.banks[2 * (i % 4)], ACT.Sigmoid).then_inc(*gate_ready.inc())

            @block.vector
            def _(dve):
                chain = Chain(dve, k.counter("dve_step"))
                for i in range(NBR * DT):
                    m, n = i // NBR, i % NBR
                    dve.wait_ge(*gate_ready.ge(i + 1))
                    dve.wait_ge(k.tile_used, first + 2 * i + 2)
                    dst = merged[:, m, :] if n == 0 else part[:]
                    nc.vector.tensor_tensor(dst, k.banks[2 * (i % 4) + 1], sg[:, i % 4, :], ALU.mult).then_inc(*part_taken.inc())
                    dve.wait_ge(*part_taken.ge(i + 1))
                    if n:
                        chain(nc.vector.tensor_tensor(merged[:, m, :], merged[:, m, :], part[:], ALU.add))


def second_block(k):
    nc = k.nc
    with ExitStack() as ctx:
        rms_norm(k, k.x, k.h, "g_norm_2", S)
        ys = k.sbuf(ctx, "branches", [P, NBR * 4, S])
        with ExitStack() as table_ctx:
            cos_a, sin_a = k.sbuf(table_ctx, "cos_a", [P, S]), k.sbuf(table_ctx, "sin_a", [P, S])
            cos_b, sin_b = k.sbuf(table_ctx, "cos_b", [P, S]), k.sbuf(table_ctx, "sin_b", [P, S])
            rope_tables(k, [("freq_a", cos_a[:], sin_a[:]), ("freq_b", cos_b[:], sin_b[:])])
            sparse_branch(k, ys[:, 0:4, :], cos_a[:], sin_a[:])
            latent_branch(k, ys[:, 4:8, :], cos_b[0:BQK], sin_b[0:BQK])
        memory_branch(k, ys[:, 8:12, :])
        merged = k.sbuf(ctx, "merged", [P, DT, S])
        merge(k, ys, merged)
        add_to_x(k, "w_out_2", merged)
    with k.stage() as block:
        @block.sync
        def _(sp):
            sp.dma_start(k.out, k.x[:]).then_inc(k.stored, 16)
            sp.wait_ge(k.stored, 16)


def build(nc, weights, vectors, constants, xT, memT, mem2T, lora, positions, out, plan, const_at, n_vec):
    with ExitStack() as ctx:
        k = Kernel(nc, ctx)
        k.plan, k.weights, k.const_at, k.loaded, k.used, k.out = plan, weights, const_at, 0, 0, out
        k.ring = k.sbuf(ctx, "ring", [P, SLOTS, SLOT])
        k.consts = k.sbuf(ctx, "consts", [P, constants.shape[1]])
        k.vecs = k.sbuf(ctx, "vecs", [P, n_vec])
        k.x = k.sbuf(ctx, "x", [P, DT, S])
        k.h = k.sbuf(ctx, "h", [P, DT, S])
        psum = ctx.enter_context(nc.psum_tensor("banks", [P, 8, 512], F32))
        k.banks = [psum[:, b, :] for b in range(8)]
        k.landed = [ctx.enter_context(nc.semaphore(f"slot{i}_landed")) for i in range(SLOTS)]
        k.tile_used = ctx.enter_context(nc.semaphore("tile_used"))
        inputs_landed = ctx.enter_context(nc.semaphore("inputs_landed"))
        k.small_landed = ctx.enter_context(nc.semaphore("small_landed"))
        k.stored = ctx.enter_context(nc.semaphore("out_stored"))
        k.lora, k.memT, k.mem2T, k.positions = lora, memT, mem2T, positions
        with k.stage() as block:
            @block.sync
            def _(sp):
                sp.dma_start(k.x[:], xT).then_inc(inputs_landed, 16)
                sp.dma_start(k.consts[:], constants).then_inc(inputs_landed, 16)
                sp.dma_start(k.vecs[:], vectors).then_inc(inputs_landed, 16)
                k.prefetch(sp, 0)
                sp.wait_ge(inputs_landed, 48)
        stages(k)


def stages(k):
    rms_norm(k, k.x, k.h, "norm_mix", S)
    with ExitStack() as ctx:
        k.y = k.sbuf(ctx, "y", [P, DT, S])
        mlstm(k, ctx)
        rwkv(k)
        add_to_x(k, "w_out", k.y)
    memory_attention(k)
    conv_glu(k)
    rms_norm(k, k.x, k.x, "norm_final", S)
    second_block(k)


def kernel(**inputs):
    import concourse.bacc as _bacc
    from concourse.bass_utils import run_bass_kernel_spmd as _run

    plan = weight_plan()
    weights = np.zeros((len(plan), P, SLOT), np.float32)
    mats = {n: np.asarray(inputs[n][0]) for n in ("w_in", "w_out", "x_wq", "x_wkv", "x_wo", "f_up", "f_down",
                                      "w_in_2", "w_uq_2", "w_ukv_2", "w_mem_kv_2", "w_branch_2", "w_out_2")}
    mats["w_branch_2"] = mats["w_branch_2"].reshape(-1, D)
    for t, (_, blocks) in enumerate(plan):
        at = 0
        for mat, row, rows, col, cols in blocks:
            weights[t, :rows, at:at + cols] = mats[mat][row:row + rows, col:col + cols]
            at += cols

    def tiles(a):
        return np.ascontiguousarray(np.asarray(a).T.reshape(DT, P, -1).transpose(1, 0, 2))

    lora = np.zeros((P, 4, RW), np.float32)
    lora[:64, 0], lora[:64, 1] = inputs["r_w_up"][0], inputs["r_a_up"][0]
    lora[:, 2], lora[:LORA_G - P, 3] = inputs["r_g_up"][0, :P], inputs["r_g_up"][0, P:]
    vectors = vector_table(inputs)
    constants, const_at = constant_table()
    arrays = {
        "weights": weights, "vectors": vectors, "constants": constants, "xT": tiles(inputs["x"][0]),
        "memT": tiles(inputs["mem"][0]), "mem2T": tiles(inputs["mem_2"][0]), "lora": lora,
        "positions": np.ascontiguousarray(inputs["positions_2"]),
    }
    nc = _bacc.Bacc("TRN2", target_bir_lowering=False, num_devices=1)
    args = [nc.dram_tensor(n, a.shape, mybir.dt.from_np(a.dtype), kind="ExternalInput").ap() for n, a in arrays.items()]
    out = nc.dram_tensor("outT", (P, DT, S), F32, kind="ExternalOutput").ap()
    build(nc, *args, out, plan, const_at, vectors.shape[1])
    r = _run(nc, [arrays], core_ids=[0])
    got = np.asarray(r.results[0]["outT"])
    return np.ascontiguousarray(got.transpose(1, 0, 2).reshape(D, S).T)[None]
```

```python
import math
from contextlib import ExitStack, contextmanager

import numpy as np

import concourse.bass as bass
from concourse import mybir

F32 = mybir.dt.float32
F32R = mybir.dt.float32r
I32 = mybir.dt.int32
ALU = mybir.AluOpType
ACT = mybir.ActivationFunctionType
AX = mybir.AxisListType.X

P = 128
S = 512
D = 1024
DT = D // P
ST = S // P
MEM = 256
EPS = 1e-6
GN_EPS = 64e-5
NEG = -1e30
CHOSEN = -3e38

MW, MH, MHD = 512, 4, 128
RW, RH, RHD = 512, 8, 64
CH = 64
NCH = S // CH
PAIRS = RW // P
LORA_G = 160
CHOOSE_STEPS = 72
GATES = 4
DECAY = math.exp(-0.5)
XH, XHD = 4, 256
DFF = 2816
FT = DFF // P
M_COLS = 4 * MW + 2 * MH

TOPK = 128
AH, AHD, AROT = 8, 64, 16
BH, BNOPE, BROPE, BV, BQK = 8, 64, 32, 64, 96
QR, KVR = 384, 256
NBR = 3
BW = 512
THETA = 500000.0
O2 = np.cumsum([0, 512, 512, 512, 512, 64, 8, 512, 384, 256, 32, 512, 512, 512, 3072]).tolist()
(C_QA, C_KA, C_VA, C_QI, C_KI, C_WI, C_ZA, C_CQ, C_CKV, C_KR, C_ZB, C_QM, C_ZM, C_GATE) = O2[:14]

SLOT = 1024
SLOTS = 4
PARTS = 4
LEAD = PARTS - 1


def feature_tile(mat, col, cols=P, rows=D, row=0):
    return [b for r in range(0, rows, P) for b in padded([(mat, row + r, min(P, rows - r), col, cols)])]


def padded(blocks, before=0):
    width = before + sum(b[4] for b in blocks)
    return ([(None, 0, 0, 0, before)] if before else []) + blocks + ([(None, 0, 0, 0, P - width)] if width < P else [])


def weight_plan():
    plan = []

    def feats(name, mat, col, width, rows=D, step=P):
        for c in range(0, width, step):
            plan.append((name, feature_tile(mat, col + c, min(step, width - c), rows)))

    def toks(name, mat, col, rows=D, width=512):
        for r in range(0, rows, 2 * P):
            plan.append((name, [(mat, r + q, P, col, width) for q in (0, P)]))

    feats("m_qk", "w_in", 0, 2 * MW)
    toks("m_v", "w_in", 2 * MW)
    feats("m_o", "w_in", 3 * MW, MW)
    plan.append(("m_gates", [b for r in range(0, D, P) for b in padded([
        ("w_in", r, P, 4 * MW, MH), (None, 0, 0, 0, 32 - MH), ("w_in", r, P, 4 * MW + MH, MH), (None, 0, 0, 0, 32 - MH),
        ("w_in", r, P, M_COLS + 3 * RW + 2 * P, LORA_G - P)])]))
    feats("r_rkv", "w_in", M_COLS, 3 * RW)
    feats("r_wa", "w_in", M_COLS + 3 * RW, P)
    feats("r_g", "w_in", M_COLS + 3 * RW + P, P)
    feats("w_out", "w_out", 0, D)
    feats("x_q", "x_wq", 0, D)
    feats("x_k", "x_wkv", 0, D)
    for half in range(2):
        toks("x_v", "x_wkv", D + 512 * half)
    feats("x_o", "x_wo", 0, D)
    for f in range(FT):
        plan.append(("f_up", feature_tile("f_up", f * P)))
        plan.append(("f_up", feature_tile("f_up", DFF + f * P)))
    for m in range(DT):
        for r0 in range(0, FT, 8):
            n = min(8, FT - r0)
            plan.append(("f_down", feature_tile("f_down", m * P, P, n * P, r0 * P)))
    w2 = "w_in_2"

    def merge_tiles(n):
        for m in range(DT):
            plan.append(("gate", feature_tile(w2, C_GATE + n * D + m * P)))
        for m in range(DT):
            plan.append(("branch", feature_tile("w_branch_2", m * P, P, BW, n * BW)))

    feats("a_qk", w2, C_QA, 1024)
    feats("a_qi", w2, C_QI, 512)
    plan.append(("a_small", [b for r in range(0, D, P) for b in padded([
        (w2, r, P, C_KI, AHD), (w2, r, P, C_WI, AH), (None, 0, 0, 0, 32 - AH), (w2, r, P, C_KR, BROPE)])]))
    toks("a_v", w2, C_VA)
    feats("a_z", w2, C_ZA, BW)
    merge_tiles(0)
    feats("b_c", w2, C_CQ, QR + KVR)
    for h in range(BH):
        plan.append(("b_uq", feature_tile("w_uq_2", h * BQK, BQK, QR)))
    plan.append(("b_uk", [(
        "w_ukv_2", r, P, h * (BNOPE + BV), BNOPE) for p in range(BH // 2) for r in (0, P) for h in (2 * p, 2 * p + 1)]))
    plan.append(("b_uv", [(
        "w_ukv_2", r, P, h * (BNOPE + BV) + BNOPE, BV) for r in (0, P) for h in range(BH)]))
    feats("b_z", w2, C_ZB, BW)
    merge_tiles(1)
    feats("m2_k", "w_mem_kv_2", 0, 512)
    toks("m2_v", "w_mem_kv_2", 512)
    feats("m2_q", w2, C_QM, 512)
    feats("m2_z", w2, C_ZM, BW)
    merge_tiles(2)
    feats("w_out_2", "w_out_2", 0, D)
    return plan


def block_width(blocks):
    return sum(b[4] for b in blocks)


VECTORS = {}


def vector_table(inputs):
    cols = []

    def put(name, vec, size=P, start=0):
        vec = np.asarray(vec).reshape(-1)
        VECTORS[name] = len(cols)
        for r in range(0, len(vec), size):
            c = np.zeros(P, np.float32)
            part = vec[r:r + size]
            c[start:start + len(part)] = part
            cols.append(c)

    for n in ("norm_mix", "norm_x", "norm_mem", "norm_ffn", "norm_final", "g_norm_2", "g_mem_2",
              "m_conv_b", "m_norm_g", "r_w0", "r_a0", "r_kk", "r_ka", "r_rk", "r_gn_g", "r_gn_b",
              "f_conv_b", "g_cq_2", "g_ckv_2", "g_qn_b_2", "g_kn_b_2", "g_qn_m_2", "g_kn_m_2"):
        put(n, inputs[n])
    for j in range(4):
        put(f"m_conv_w{j}", inputs["m_conv_w"][0, j])
    for j in range(3):
        put(f"f_conv_w{j}", inputs["f_conv_w"][0, j])
    put("bias_i", inputs["m_gate_b"][0, :MH])
    put("bias_f", inputs["m_gate_b"][0, MH:], start=32)
    mu = inputs["r_mu"][0]
    put("mu_rkv", mu[:3 * RW])
    put("mu_w", mu[3 * RW:3 * RW + 64])
    put("mu_a", mu[3 * RW + 64:3 * RW + 128])
    put("mu_g", mu[3 * RW + 128:])
    for n in ("g_qn_a_2", "g_kn_a_2"):
        put(n, np.concatenate([inputs[n][0], inputs[n][0]]))
    return np.stack(cols, 1)


def constant_table():
    at, parts, n = {}, [], 0

    def put(name, a):
        nonlocal n
        full = np.zeros((P, a.shape[1]), np.float32)
        full[:a.shape[0]] = a
        at[name] = (n, a.shape[1])
        parts.append(full)
        n += a.shape[1]

    i = np.arange(P)
    r, c = i[:, None], i[None, :]
    put("ident", np.eye(P))
    put("ones", np.ones((P, P)))
    put("ones_half", (r // 64 == c // 64) * 1.0)
    put("key_le_query", (r <= c) * 1.0)
    same = r // CH == c // CH
    put("before", (same & (r < c)) * 1.0)
    put("upto", (same & (r <= c)) * 1.0)
    b = 1
    while b < CH:
        put(f"level{b}", ((r // (2 * b) == c // (2 * b)) & (r % (2 * b) < b) & (c % (2 * b) >= b)) * 1.0)
        b *= 2
    put("level1_lower", ((r // 2 == c // 2) & (r % 2 == 1) & (c % 2 == 0)) * 1.0)
    a_rot = np.zeros((P, P))
    for base in (0, 64):
        for j in range(AROT // 2):
            a_rot[base + j + 8, base + j] = -1.0
            a_rot[base + j, base + j + 8] = 1.0
    put("rotate_a", a_rot)
    b_rot = np.zeros((BQK, BQK))
    for j in range(BROPE // 2):
        b_rot[BNOPE + j + 16, BNOPE + j] = -1.0
        b_rot[BNOPE + j, BNOPE + j + 16] = 1.0
    put("rotate_b", b_rot)
    fa = THETA ** (-(np.arange(0, AROT, 2, dtype=np.float32) / np.float32(AROT)))
    fb = THETA ** (-(np.arange(0, BROPE, 2, dtype=np.float32) / np.float32(BROPE)))
    put("freq_a", np.where(i % 64 < AROT, fa[i % 8], 0.0)[:, None])
    put("freq_b", np.where((i >= BNOPE) & (i < BQK), fb[(i - BNOPE) % 16], 0.0)[:, None])
    put("causal", np.concatenate([np.zeros((P, S - P)), np.where(c <= r, 0.0, NEG)], 1))
    put("chunk_start", np.tile((np.arange(S) % CH != 0)[None, :], (P, 1)) * 1.0)
    return np.concatenate(parts, 1).astype(np.float32), at


class Counter:

    def __init__(self, sem):
        self.sem, self.base, self.total = sem, 0, 0

    def inc(self):
        self.total += 1
        return self.sem, 1

    def ge(self, n):
        return self.sem, self.base + n

    def all(self):
        return self.sem, self.base + self.total


class Kernel:
    def __init__(self, nc, ctx):
        self.nc, self.ctx, self.counters, self.names = nc, ctx, {}, 0
        self.small = 0

    def counter(self, name):
        if name not in self.counters:
            self.counters[name] = Counter(self.ctx.enter_context(self.nc.semaphore(name)))
        return self.counters[name]

    @contextmanager
    def stage(self):
        with self.nc.Block() as block:
            yield block
        for s in self.counters.values():
            s.base += s.total
            s.total = 0

    def sbuf(self, ctx, name, shape, dt=F32):
        return ctx.enter_context(self.nc.sbuf_tensor(name, shape, dt))

    def fresh(self, name):
        self.names = self.names + 1
        return f"{name}_{self.names}"

    def const(self, name, rows=P):
        at, n = self.const_at[name]
        return self.consts[0:rows, at:at + n]

    def vec(self, name, tile=0, rows=P):
        c = VECTORS[name] + tile
        return self.vecs[0:rows, c:c + 1]

    def slot(self, t):
        return self.parts[:, t % PARTS, 0, :], self.parts[:, t % PARTS, 1, :]

    def prefetch(self, sp, used_at_end):
        if used_at_end > self.used_before:
            self.used_before, self.split_at_end = used_at_end, used_at_end + LEAD
        while self.loaded < min(len(self.plan), self.split_at_end + SLOTS):
            t = self.loaded
            if t >= SLOTS:
                sp.wait_ge(self.low_ready, t - SLOTS + 1)
            w = block_width(self.plan[t][1])
            sp.dma_start(self.ring[:, t % SLOTS, 0:w], self.weights[t, :, 0:w]).then_inc(self.landed[t % SLOTS], 16)
            self.loaded += 1

    def split_high(self, act, upto):
        while self.split_h < min(len(self.plan), upto):
            t, w = self.split_h, block_width(self.plan[self.split_h][1])
            act.wait_ge(self.landed[t % SLOTS], 16 * (t // SLOTS + 1))
            if t >= PARTS:
                act.wait_ge(self.tile_used, t - PARTS + 1)
            self.nc.scalar.copy(self.parts[:, t % PARTS, 0, 0:w], self.ring[:, t % SLOTS, 0:w]).then_inc(self.high_ready, 1)
            self.split_h += 1

    def split_low(self, pool, upto):
        while self.split_l < min(len(self.plan), upto):
            t, w = self.split_l, block_width(self.plan[self.split_l][1])
            pool.wait_ge(self.high_ready, t + 1)
            self.nc.gpsimd.tensor_tensor(self.parts[:, t % PARTS, 1, 0:w], self.ring[:, t % SLOTS, 0:w],
                                         self.parts[:, t % PARTS, 0, 0:w].bitcast(F32), ALU.subtract).then_inc(self.low_ready, 1)
            self.split_l += 1

    def prefetch_split(self, sp):
        self.split_at_end = max(self.split_at_end, self.split_l)
        self.prefetch(sp, self.used_before)

    def load_small(self, sp, dst, src):
        sp.dma_start(dst, src).then_inc(self.small_landed, 16)
        self.small += 16

    def small_load(self):
        return self.small_landed, self.small

    def tile_ready(self, t):
        return self.low_ready, t + 1


class Halves:

    def __init__(self, hi, lo):
        self.hi, self.lo = hi, lo

    def __getitem__(self, at):
        return Halves(self.hi[at], self.lo[at])


def halves(k, ctx, name, shape):
    return Halves(k.sbuf(ctx, name + "_hi", shape, F32R), k.sbuf(ctx, name + "_lo", shape, F32R))


def product(k, out, w, x, first, last):
    nc = k.nc
    nc.tensor.matmul(out, w.hi, x.hi, start=first, stop=False)
    nc.tensor.matmul(out, w.hi, x.lo, start=False, stop=False)
    return nc.tensor.matmul(out, w.lo, x.hi, start=False, stop=last)


class Chain:

    def __init__(self, eng, count):
        self.eng, self.count = eng, count

    def __call__(self, ins):
        ins.then_inc(*self.count.inc())
        self.eng.wait_ge(*self.count.all())



def feature_major(x, ktiles=DT, n=S):
    def emit(k, pe, t0, bank, arriving=None):
        for kt in range(ktiles):
            t = t0 + kt // 8
            if kt % 8 == 0:
                pe.wait_ge(*k.tile_ready(t))
            if arriving:
                pe.wait_ge(*arriving.ready(kt))
            hi, lo = k.slot(t)
            cols = slice((kt % 8) * P, (kt % 8 + 1) * P)
            last = product(k, bank[:, 0:n], Halves(hi[:, cols], lo[:, cols]), x[:, kt, 0:n], kt == 0, kt == ktiles - 1)
            if kt % 8 == 7 or kt == ktiles - 1:
                last.then_inc(k.tile_used, 1)
    return emit


class Job:

    def __init__(self, name, emit, engine, take, tiles=1):
        self.name, self.emit, self.engine, self.take, self.tiles = name, emit, engine, take, tiles


def project(k, jobs, arriving=None, before=None, after=None, banks=8):
    taken = {"act": k.counter("bank_taken_act"), "dve": k.counter("bank_taken_dve")}
    count, nth, slots = {"act": 0, "dve": 0}, [], []
    for job in jobs:
        count[job.engine] += 1
        nth.append(count[job.engine])
        slots.append((k.used, k.used + job.tiles))
        k.used += job.tiles

    with k.stage() as block:
        @block.sync
        def _(sp):
            if before:
                before(sp)
            k.prefetch(sp, k.used)
            if after:
                after(sp)

        @block.tensor
        def _(pe):
            if arriving:
                arriving.pe(pe)
            for i, (job, (t0, t1)) in enumerate(zip(jobs, slots)):
                assert all(k.plan[t][0] == job.name for t in range(t0, t1))
                if i == 1 and arriving:
                    arriving.all_ready(pe)
                if i >= banks:
                    pe.wait_ge(*taken[jobs[i - banks].engine].ge(nth[i - banks]))
                job.emit(k, pe, t0, k.banks[i % banks], None if i else arriving)

        def take_out(eng, name):
            chain = Chain(eng, k.counter(f"{name}_step"))
            for i, (job, (t0, t1)) in enumerate(zip(jobs, slots)):
                if name == "act":
                    k.split_high(eng, t1 + LEAD)
                if job.engine == name:
                    eng.wait_ge(k.tile_used, t1)
                    job.take(eng, chain, k.banks[i % banks]).then_inc(*taken[name].inc())

        @block.scalar
        def _(act):
            if arriving:
                if slots[0][0]:
                    k.split_high(act, slots[0][0] + LEAD)
                arriving.act(act)
            take_out(act, "act")

        @block.vector
        def _(dve):
            if arriving:
                arriving.dve(dve)
            take_out(dve, "dve")

        @block.gpsimd
        def _(pool):
            if arriving:
                if slots[0][0]:
                    k.split_low(pool, slots[0][0] + LEAD)
                arriving.pool(pool)
            k.split_low(pool, k.used + LEAD)


class Background:

    def __init__(self, k, jobs):
        self.k, self.jobs, self.first = k, jobs, k.used
        self.pe_at = self.act_at = 0
        self.taken = k.taken_in_background
        k.taken_in_background += len(jobs)

    def pe(self, pe, steps):
        k, bank = self.k, self.k.banks[7]
        for at in range(self.pe_at, min(self.pe_at + steps, DT * len(self.jobs))):
            i, kt = divmod(at, DT)
            t = self.first + i
            if kt == 0:
                assert k.plan[t][0] == self.jobs[i][0]
                pe.wait_ge(*k.tile_ready(t))
                if i:
                    pe.wait_ge(k.background_taken, self.taken + i)
            hi, lo = k.slot(t)
            cols = slice(kt * P, (kt + 1) * P)
            last = product(k, bank, Halves(hi[:, cols], lo[:, cols]), k.h[:, kt, :], kt == 0, kt == DT - 1)
            self.pe_at = at + 1
            if kt == DT - 1:
                last.then_inc(k.tile_used, 1)
                k.used += 1

    def take(self, act, i):
        act.wait_ge(self.k.tile_used, self.first + i + 1)
        self.k.nc.scalar.copy(self.jobs[i][1], self.k.banks[7]).then_inc(self.k.background_taken, 1)

    def act(self, act, steps):
        for at in range(self.act_at, min(self.act_at + steps, DT * len(self.jobs))):
            i, kt = divmod(at, DT)
            if kt == 0:
                if i:
                    self.take(act, i - 1)
                self.k.split_high(act, self.first + i + 1 + LEAD)
            self.act_at = at + 1

    def finish(self):
        k, rest = self.k, DT * len(self.jobs)
        with k.stage() as block:
            @block.tensor
            def _(pe):
                self.pe(pe, rest)

            @block.scalar
            def _(act):
                self.act(act, rest)
                self.take(act, len(self.jobs) - 1)

            @block.gpsimd
            def _(pool):
                k.split_low(pool, k.split_h)

            @block.sync
            def _(sp):
                k.prefetch_split(sp)


class Idle:

    def pe(self, pe, steps):
        pass

    def act(self, act, steps):
        pass


def project_tokens(k, name, x, tokens, take, ktiles=DT, width=512, before=None):
    nt = tokens // P
    first, per = k.used, SLOT // width
    n = ktiles // per
    k.used += n
    out_taken = k.counter("bank_taken_act")

    with k.stage() as block:
        @block.sync
        def _(sp):
            if before:
                before(sp)
            k.prefetch(sp, k.used)

        @block.tensor
        def _(pe):
            for q in range(n):
                assert k.plan[first + q][0] == name, (k.plan[first + q][0], name)
                pe.wait_ge(*k.tile_ready(first + q))
                hi, lo = k.slot(first + q)
                for j in range(per):
                    kt, cols = q * per + j, slice(j * width, (j + 1) * width)
                    for t in range(nt):
                        last = product(k, k.banks[t][:, 0:width], x[:, kt, t * P:(t + 1) * P],
                                       Halves(hi[:, cols], lo[:, cols]), kt == 0, kt == ktiles - 1)
                last.then_inc(k.tile_used, 1)

        @block.scalar
        def _(act):
            k.split_high(act, first + n + LEAD)
            act.wait_ge(k.tile_used, first + n)
            for t in range(nt):
                take(act, t, k.banks[t][:, 0:width])

        @block.gpsimd
        def _(pool):
            k.split_low(pool, k.used + LEAD)


class Norms:

    def __init__(self, k, ctx, groups, n=S, per=1, room=None, landed=None):
        nt = n // P
        self.landed = landed
        self.k, self.groups, self.n, self.per, self.nt = k, groups, n, per, nt
        self.tiles = [(g, first, last) + tile for g, (size, members) in enumerate(groups)
                      for first, last, tile in [(m == 0, m == len(members) - 1, t) for m, t in enumerate(members)]]
        self.by_pool = [i % 3 == 2 for i in range(len(self.tiles))]
        self.st = k.sbuf(ctx, k.fresh("rstd"), [P, nt, len(groups) * per])
        self.split = self.tiles[0][4].__class__ is Halves
        if room is None:
            room = k.sbuf(ctx, k.fresh("norm_room"), [P, 6, n])
        self.multi = len(groups[0][1]) > 1
        self.W = 2 if room.shape[1] >= 6 else 1
        added = self.W + (len(groups) if self.multi else 0)
        self.R, self.N = min(4, room.shape[1] - added), min(4, room.shape[1] - self.W)
        self.wide = room[:, 0:self.W].rearrange("p g (j m) -> p g j m", m=P)
        self.added, self.sq, self.whole = room[:, self.W:], room[:, added:], room[:, self.W:]
        self.squares, uses, done = [], 0, {"square_act": 0, "square_pool": 0}
        for i, (g, first, last, src, dst, rows, gain) in enumerate(self.tiles):
            name = "square_pool" if self.by_pool[i] else "square_act"
            done[name] += 1
            if self.multi and first:
                self.squares.append((self.added[0:rows, g, :], None, name, done[name]))
            else:
                self.squares.append((self.sq[0:rows, uses % self.R, :], uses, name, done[name]))
                uses += 1

    def ready(self, i):
        G = self.k.counter
        return G("norm_low").ge((i + 1) // 2) if i % 2 else G("low_dve").ge(i // 2 + 1)

    def all_ready(self, pe):
        for i in range(max(0, len(self.tiles) - 2), len(self.tiles)):
            pe.wait_ge(*self.ready(i))

    def act(self, act):
        k, nc, G, n, nt, per, tiles = self.k, self.k.nc, self.k.counter, self.n, self.nt, self.per, self.tiles
        for i, (g, first, last, src, dst, rows, gain) in enumerate(tiles):
            if not self.by_pool[i]:
                square, use = self.squares[i][0:2]
                if use is not None and use >= self.R:
                    act.wait_ge(*G("added" if self.multi else "sums_ready").ge(use - self.R + 1))
                if self.landed:
                    act.wait_ge(*self.landed(i))
                nc.scalar.activation(square, src, ACT.Square).then_inc(*G("square_act").inc())
        act.wait_ge(*G("mean_ready").ge(1))
        nc.scalar.activation(self.st[:], self.st[:], ACT.Sqrt).then_inc(*G("root_ready").inc())
        for g in range(len(self.groups)):
            rows = self.groups[g][1][0][2]
            act.wait_ge(*G("rstd_ready").ge(1))
            if g >= self.W:
                act.wait_ge(*G("turned_ready").ge(g - self.W + 1))
            for h in range(per):
                last = nc.scalar.copy(self.wide[:, g % self.W, :, h * RHD:(h + 1) * RHD] if per == 2 else self.wide[:, g % self.W, :, 0:rows],
                                      self.st[:, :, g * per + h:g * per + h + 1].to_broadcast([P, nt, RHD if per == 2 else rows]))
            last.then_inc(*G("wide_ready").inc())
        if self.split:
            for i, (g, first, last, src, dst, rows, gain) in enumerate(tiles):
                act.wait_ge(*G("whole_ready").ge(i + 1))
                nc.scalar.copy(dst.hi, self.whole[0:rows, i % self.N, :]).then_inc(*G("norm_high").inc())

    def pool(self, pool):
        k, nc, G, n, nt, per, tiles = self.k, self.k.nc, self.k.counter, self.n, self.nt, self.per, self.tiles
        for i, (g, first, last, src, dst, rows, gain) in enumerate(tiles):
            if self.by_pool[i]:
                square, use = self.squares[i][0:2]
                if use is not None and use >= self.R:
                    pool.wait_ge(*G("added" if self.multi else "sums_ready").ge(use - self.R + 1))
                if self.landed:
                    pool.wait_ge(*self.landed(i))
                nc.gpsimd.tensor_tensor(square, src, src, ALU.mult).then_inc(*G("square_pool").inc())
        if self.split:
            for i, (g, first, last, src, dst, rows, gain) in enumerate(tiles):
                if i % 2:
                    pool.wait_ge(*G("norm_high").ge(i + 1))
                    nc.gpsimd.tensor_tensor(dst.lo, self.whole[0:rows, i % self.N, :], dst.hi.bitcast(F32),
                                            ALU.subtract).then_inc(*G("norm_low").inc())

    def pe(self, pe):
        k, nc, G, n, nt, per, tiles = self.k, self.k.nc, self.k.counter, self.n, self.nt, self.per, self.tiles
        ones = k.const("ones_half")[:, 0:P:RHD] if per == 2 else k.const("ones")[:, 0:1]
        if self.landed:
            pe.wait_ge(*self.landed(None))
        adds = 0
        for i, (g, first, last, src, dst, rows, gain) in enumerate(tiles):
            square, use, name, count = self.squares[i]
            if self.multi:
                adds += not first
                if not last:
                    continue
                square = self.added[0:rows, g, :]
                pe.wait_ge(*G("added").ge(adds))
            else:
                pe.wait_ge(*G(name).ge(count))
            for j in range(nt):
                mm = nc.tensor.matmul(k.banks[j][:, g * per:(g + 1) * per], square[:, j * P:(j + 1) * P],
                                      ones[0:rows], start=True, stop=True)
            mm.then_inc(*G("sums_ready").inc())
        for g in range(len(self.groups)):
            rows = self.groups[g][1][0][2]
            pe.wait_ge(*G("wide_ready").ge(g + 1))
            if g >= 3:
                pe.wait_ge(*G("normed").ge(g - 2))
            for j in range(nt):
                mm = nc.tensor.transpose(k.banks[4 + g % 3][0:rows, j * P:(j + 1) * P], self.wide[:, g % self.W, j, 0:rows],
                                         k.const("ident"))
            mm.then_inc(*G("turned_ready").inc())

    def dve(self, dve):
        k, nc, G, n, nt, per, tiles = self.k, self.k.nc, self.k.counter, self.n, self.nt, self.per, self.tiles
        if self.landed:
            dve.wait_ge(*self.landed(None))
        if self.multi:
            for i, (g, first, last, src, dst, rows, gain) in enumerate(tiles):
                if not first:
                    square, use, name, count = self.squares[i]
                    dve.wait_ge(*G(name).ge(count))
                    if tiles[i - 1][1]:
                        dve.wait_ge(*G("square_act").ge(self.squares[i - 1][3]))
                    elif use:
                        dve.wait_ge(*G("added").ge(use))
                    nc.vector.tensor_tensor(self.added[0:rows, g, :], self.added[0:rows, g, :], square,
                                            ALU.add).then_inc(*G("added").inc())
        dve.wait_ge(*G("sums_ready").ge(len(self.groups)))
        g0 = 0
        while g0 < len(self.groups):
            size, g1 = self.groups[g0][0], g0
            while g1 < len(self.groups) and self.groups[g1][0] == size:
                g1 += 1
            cols = slice(g0 * per, g1 * per)
            ins = nc.vector.tensor_scalar(self.st[:, :, cols], k.psum[:, 0:nt, cols], 1.0 / size, EPS, ALU.mult, ALU.add)
            g0 = g1
        ins.then_inc(*G("mean_ready").inc())
        dve.wait_ge(*G("root_ready").ge(1))
        nc.vector.reciprocal(self.st[:], self.st[:]).then_inc(*G("rstd_ready").inc())
        def low(i):
            dst, rows = tiles[i][4:6]
            dve.wait_ge(*G("norm_high").ge(i + 1))
            nc.vector.tensor_tensor(dst.lo, self.whole[0:rows, i % self.N, :], dst.hi.bitcast(F32),
                                    ALU.subtract).then_inc(*G("low_dve").inc())

        i = 0
        for g, (_, members) in enumerate(self.groups):
            dve.wait_ge(*G("turned_ready").ge(g + 1))
            for m, (src, dst, rows, gain) in enumerate(members):
                if self.split and i >= self.N:
                    dve.wait_ge(*self.ready(i - self.N))
                ins = nc.vector.scalar_tensor_tensor(out=self.whole[0:rows, i % self.N, :] if self.split else dst, in0=src, scalar=gain[0:rows],
                                                     in1=k.banks[4 + g % 3][0:rows, 0:n], op0=ALU.mult, op1=ALU.mult)
                ins.then_inc(*(G("whole_ready") if self.split else G("normed")).inc())
                if self.split and i % 2 == 1:
                    low(i - 1)
                i += 1
        if self.split and i % 2:
            low(i - 1)


def norm_stage(k, groups, n=S, per=1, room=None):
    with ExitStack() as ctx:
        norms = Norms(k, ctx, groups, n, per, room)
        with k.stage() as block:
            @block.scalar
            def _(act):
                norms.act(act)

            @block.gpsimd
            def _(pool):
                norms.pool(pool)
                k.split_low(pool, k.split_h)

            @block.tensor
            def _(pe):
                norms.pe(pe)

            @block.vector
            def _(dve):
                norms.dve(dve)

            @block.sync
            def _(sp):
                k.prefetch_split(sp)


def rms_norm(k, ctx, src, dst, gain, n=S, tiles=DT, room=None, landed=None):
    return Norms(k, ctx, [(tiles * P, [(src[:, t, 0:n], dst[:, t, 0:n], P, k.vec(gain, t)) for t in range(tiles)])], n,
                 room=room, landed=landed)


def head_norms(k, items, n=S, room=None):
    norm_stage(k, [(size, [(x, x, rows, k.vec(gain))]) for x, rows, per, size, gain in items], n, items[0][2], room)


def conv(k, dve, chain, bank, dst, weights, bias, tile, taps):
    nc = k.nc
    chain(nc.vector.tensor_scalar(dst, bank, k.vec(f"{weights}{taps - 1}", tile), k.vec(bias, tile),
                                  ALU.mult, ALU.add))
    for j in range(taps - 2, -1, -1):
        lag = taps - 1 - j
        ins = nc.vector.scalar_tensor_tensor(out=dst[:, lag:S], in0=bank[:, 0:S - lag], scalar=k.vec(f"{weights}{j}", tile),
                                             in1=dst[:, lag:S], op0=ALU.mult, op1=ALU.add)
        if j:
            chain(ins)
    return ins


class Gating:

    def __init__(self, k, y, z, sg, dst, tiles):
        self.k, self.y, self.z, self.sg, self.dst, self.tiles = k, y, z, sg, dst, tiles

    def ready(self, t):
        return self.k.counter("low_made").ge(t + 1)

    def all_ready(self, pe):
        pe.wait_ge(*self.ready(self.tiles - 1))

    def pe(self, pe):
        pass

    def pool(self, pool):
        pass

    def act(self, act):
        G = self.k.counter
        for t in range(self.tiles):
            self.k.nc.scalar.activation(self.z[:, t, :], self.z[:, t, :], ACT.Silu).then_inc(*G("silu_ready").inc())
        for t in range(self.tiles):
            act.wait_ge(*G("gated_ready").ge(t + 1))
            self.k.nc.scalar.copy(self.dst.hi[:, t, :], self.z[:, t, :]).then_inc(*G("high_made").inc())
        for m in range(DT):
            self.k.nc.scalar.activation(self.sg[:, m, :], self.sg[:, m, :], ACT.Sigmoid).then_inc(*G("gate_ready").inc())

    def dve(self, dve):
        for t in range(self.tiles):
            dve.wait_ge(*self.k.counter("silu_ready").ge(t + 1))
            self.k.nc.vector.tensor_tensor(self.z[:, t, :], self.y[:, t, :], self.z[:, t, :],
                                           ALU.mult).then_inc(*self.k.counter("gated_ready").inc())
        for t in range(self.tiles):
            dve.wait_ge(*self.k.counter("high_made").ge(t + 1))
            self.k.nc.vector.tensor_tensor(self.dst.lo[:, t, :], self.z[:, t, :], self.dst.hi[:, t, :].bitcast(F32),
                                           ALU.subtract).then_inc(*self.k.counter("low_made").inc())


class Splitting:

    def __init__(self, k, src, dst, tiles):
        self.k, self.src, self.dst, self.tiles = k, src, dst, tiles

    def ready(self, t):
        return self.k.counter("low_made").ge(t + 1)

    def all_ready(self, pe):
        pe.wait_ge(*self.ready(self.tiles - 1))

    def pe(self, pe):
        pass

    def act(self, act):
        for t in range(self.tiles):
            self.k.nc.scalar.copy(self.dst.hi[:, t, :], self.src[:, t, :]).then_inc(*self.k.counter("high_made").inc())

    def dve(self, dve):
        for t in range(self.tiles):
            dve.wait_ge(*self.k.counter("high_made").ge(t + 1))
            self.k.nc.vector.tensor_tensor(self.dst.lo[:, t, :], self.src[:, t, :], self.dst.hi[:, t, :].bitcast(F32),
                                           ALU.subtract).then_inc(*self.k.counter("low_made").inc())

    def pool(self, pool):
        pass


def mixer(k):
    nc = k.nc
    with ExitStack() as ctx:
        k.y = k.sbuf(ctx, "y", [P, DT, S])
        with ExitStack() as in_ctx:
            rkv = k.sbuf(in_ctx, "rkv", [P, 3 * PAIRS, S])
            wd, ad = k.sbuf(in_ctx, "wd", [64, S]), k.sbuf(in_ctx, "ad", [64, S])
            gd = k.sbuf(in_ctx, "gd", [P, 2, S])
            k.keep_share = k.sbuf(in_ctx, "keep_share", [P, 16])
            lora = k.sbuf(in_ctx, "lora_w", [P, 4, RW])
            decay = k.sbuf(in_ctx, "decay", [P, PAIRS, NCH])
            first = Operands(k, 0, rkv, wd, ad, lora, decay, k.x[:, 0:4, :])
            with ExitStack() as m_ctx:
                qk = k.sbuf(m_ctx, "qk", [P, 2 * MH, S])
                v = k.sbuf(m_ctx, "m_v", [P, ST, MW])
                o = k.sbuf(m_ctx, "m_o", [P, MH, S])
                ipre, fpre = k.sbuf(m_ctx, "ipre", [MH, S]), k.sbuf(m_ctx, "fpre", [MH, S])
                with ExitStack() as h_ctx:
                    h = halves(k, h_ctx, "h", [P, DT, S])
                    normed = rms_norm(k, h_ctx, k.x, h, "norm_mix", room=rkv, landed=k.inputs_landed)
                    mixer_inputs(k, h, normed, lora, qk, v, o, ipre, fpre, rkv, wd, ad, gd)
                mlstm(k, qk, v, o, ipre, fpre, wd, gd, first)
            rwkv(k, rkv, wd, ad, gd, lora, first)
        yh = halves(k, ctx, "y_parts", [P, DT, S])
        add_to_x(k, "w_out", yh, arriving=Splitting(k, k.y, yh, DT))


def mixer_inputs(k, h, normed, lora, qk, v, o, ipre, fpre, rkv, wd, ad, gd):
    nc = k.nc

    def loads(sp):
        k.load_inputs(sp)
        k.load_small(sp, lora[:], k.lora)

    project(k, [Job("m_qk", feature_major(h), "dve", lambda e, c, b, t=t: conv(k, e, c, b, qk[:, t, :], "m_conv_w", "m_conv_b", t, 4))
                for t in range(2 * MH)], normed, before=loads)
    with k.stage() as block:
        @block.vector
        def _(dve):
            c = VECTORS["mu_rkv"]
            nc.vector.tensor_scalar(k.keep_share[:], k.vecs[:, c:c + 16], -1.0, 1.0, ALU.mult, ALU.add)
    project_tokens(k, "m_v", h, S, lambda act, t, bank: nc.scalar.copy(v[:, t, :], bank))

    def gates(dve, chain, bank):
        chain(nc.vector.tensor_scalar(ipre[:], bank[0:MH, :], k.vec("bias_i", 0, MH), None, ALU.add))
        chain(nc.vector.tensor_scalar(fpre[:], bank[32:32 + MH, :], k.vec("bias_f", 0, 32 + MH)[32:32 + MH], None, ALU.add))
        return shifted(k, dve, chain, bank, gd[0:LORA_G - P, 1, :], "mu_g", 1, LORA_G - P, 64)

    jobs = [Job("m_o", feature_major(h), "act",
                lambda e, c, b, t=t: nc.scalar.activation(o[:, t, :], b, ACT.Sigmoid)) for t in range(MH)]
    jobs.append(Job("m_gates", feature_major(h), "dve", gates))
    jobs += [Job("r_rkv", feature_major(h), "dve", lambda e, c, b, t=t: shifted(k, e, c, b, rkv[:, t, :], "mu_rkv", t))
             for t in range(3 * PAIRS)]

    def low_ranks(dve, chain, bank):
        chain(shifted(k, dve, chain, bank, wd[:], "mu_w", 0, 64))
        return shifted(k, dve, chain, bank, ad[:], "mu_a", 0, 64, 64)

    jobs.append(Job("r_wa", feature_major(h), "dve", low_ranks))
    jobs.append(Job("r_g", feature_major(h), "dve", lambda e, c, b: shifted(k, e, c, b, gd[:, 0, :], "mu_g", 0)))
    project(k, jobs)


def mlstm(k, qk, v, o, ipre, fpre, wd, gd, first):
    nc = k.nc
    y = k.y
    with ExitStack() as ctx:
        tmp = k.sbuf(ctx, "gate_tmp", [MH, S])
        run = k.sbuf(ctx, "gate_sum", [MH, S])
        u = k.sbuf(ctx, "gate_u", [MH, S])
        top = k.sbuf(ctx, "gate_top", [MH, S])
        low = k.sbuf(ctx, "gate_floor", [MH, S])
        u_col = k.sbuf(ctx, "u_col", [P, ST, MH])
        abs_ready, ln_ready, rows_ready = k.counter("abs_ready"), k.counter("ln_ready"), k.counter("rows_ready")
        floor_ready = k.counter("floor_ready")
        with k.stage() as block:
            @block.scalar
            def _(act):
                chain = Chain(act, k.counter("act_step"))
                nc.scalar.activation(wd[:], wd[:], ACT.Tanh).then_inc(*k.counter("tanh_ready").inc())
                first.act(act, 0)
                act.wait_ge(*abs_ready.ge(1))
                chain(nc.scalar.activation(tmp[:], tmp[:], ACT.Exp, scale=-1.0))
                nc.scalar.activation(tmp[:], tmp[:], ACT.Ln, bias=1.0).then_inc(*ln_ready.inc())
                act.wait_ge(*rows_ready.ge(2))
                nc.scalar.activation(low[:], low[:], ACT.Exp, scale=-2.0).then_inc(*floor_ready.inc())
                first.act(act, 2)
                first.act(act, 1)
                for t in range(2 * MH):
                    nc.scalar.activation(qk[:, t, :], qk[:, t, :], ACT.Silu)

            @block.vector
            def _(dve):
                chain = Chain(dve, k.counter("dve_step"))
                nc.vector.scalar_tensor_tensor(out=tmp[:], in0=fpre[:], scalar=-1.0, in1=fpre[:],
                                               op0=ALU.mult, op1=ALU.max).then_inc(*abs_ready.inc())
                first.dve(dve, 0)
                dve.wait_ge(*ln_ready.ge(1))
                chain(nc.vector.scalar_tensor_tensor(out=fpre[:], in0=fpre[:], scalar=0.0, in1=tmp[:],
                                                     op0=ALU.min, op1=ALU.subtract))
                chain(nc.vector.tensor_tensor_scan(run[:], fpre[:], fpre[:], 0.0, ALU.add, ALU.bypass))
                nc.vector.tensor_tensor(u[:], ipre[:], run[:], ALU.subtract).then_inc(*rows_ready.inc())
                dve.wait_ge(*rows_ready.ge(1))
                chain(nc.vector.tensor_tensor_scan(top[:], u[:], u[:], 0.0, ALU.max, ALU.max))
                nc.vector.tensor_tensor(low[:], top[:], run[:], ALU.add).then_inc(*rows_ready.inc())
                dve.wait_ge(*floor_ready.ge(1))
                chain(nc.vector.tensor_scalar(low[:], low[:], EPS, 1e-37, ALU.mult, ALU.max))
                nc.vector.tensor_scalar(low[:], low[:], 1e37, None, ALU.min)
                dve.wait_ge(*k.counter("u_turned").ge(1))
                nc.vector.tensor_copy(u_col[:].rearrange("p t h -> p (t h)"), k.banks[0][:, 0:ST * MH])
                for step in range(1, 4):
                    first.dve(dve, step)

            @block.tensor
            def _(pe):
                pe.wait_ge(*k.counter("tanh_ready").ge(1))
                first.pe(pe, 0)
                first.pe(pe, 1)
                pe.wait_ge(*rows_ready.ge(1))
                for t in range(ST):
                    last = nc.tensor.matmul(k.banks[0][:, t * MH:(t + 1) * MH], u[:, t * P:(t + 1) * P],
                                            k.const("ident", MH)[:, 0:MH], start=True, stop=True)
                last.then_inc(*k.counter("u_turned").inc())
                first.pe(pe, 2)

        topb = k.sbuf(ctx, "top_b", [P, 2, S])
        lowb = k.sbuf(ctx, "floor_b", [P, 2, S])
        e = k.sbuf(ctx, "m_e", [P, 4, S])
        hm = k.sbuf(ctx, "m_hm", [P, 2, S])
        sq, rs = y[:, MH:MH + 2, :], y[:, MH + 2:MH + 4, :]
        G = k.counter
        sent, put, made, expd = G("score_ready"), G("rows_spread"), G("arg_ready"), G("exp_ready")
        prob, summed, meaned = G("prob_ready"), G("num_den_ready"), G("mean_ready")
        rooted, normed = G("root_ready"), G("head_ready")
        width = [S - j * P for j in range(ST)]

        def nums(pe, h, j):
            n = ST * h + j
            pe.wait_ge(*prob.ge(n + 1))
            if j == 0 and h >= 2:
                pe.wait_ge(*G("den_ready").ge(h - 1))
            num, den = k.banks[3 + 2 * (h % 2)], k.banks[4 + 2 * (h % 2)]
            nc.tensor.matmul(num[:, j * P:S], v[:, j, h * P:(h + 1) * P], e[:, n % 4, 0:width[j]],
                             start=(j == 0), stop=(j == ST - 1))
            nc.tensor.matmul(den[:, j * P:S], k.const("ones"), e[:, n % 4, 0:width[j]],
                             start=(j == 0), stop=(j == ST - 1)).then_inc(*summed.inc())

        def weigh(dve, chain, h, j):
            n = ST * h + j
            ed = e[:, n % 4, 0:width[j]]
            dve.wait_ge(*expd.ge(n + 1))
            dve.wait_ge(*sent.ge(n + 1))
            chain(nc.vector.scalar_tensor_tensor(out=ed, in0=k.banks[1 + n % 2][:, 0:width[j]],
                                                 scalar=MHD ** -0.5, in1=ed, op0=ALU.mult, op1=ALU.mult))
            nc.vector.tensor_tensor(e[:, n % 4, 0:P], e[:, n % 4, 0:P], k.const("key_le_query"),
                                    ALU.mult).then_inc(*prob.inc())

        def norm_sums(pe, h, step):
            if step == 1:
                pe.wait_ge(*G("hidden_ready").ge(h + 1))
                if h:
                    pe.wait_ge(*G("var_ready").ge(h))
                nc.tensor.matmul(k.banks[7], k.const("ones"), hm[:, h % 2, :], start=True, stop=True).then_inc(*meaned.inc())
            if step == 2:
                pe.wait_ge(*G("square_ready").ge(h + 1))
                nc.tensor.matmul(k.banks[7], k.const("ones"), sq[:, h % 2, :], start=True, stop=True).then_inc(*meaned.inc())

        def norm_functions(act, h, step):
            if step == 0:
                act.wait_ge(*summed.ge(ST * h + ST))
                if h >= 2:
                    act.wait_ge(*normed.ge(h - 1))
                nc.scalar.copy(hm[:, h % 2, :], k.banks[3 + 2 * (h % 2)]).then_inc(*G("hidden_ready").inc())
                nc.scalar.activation(rs[:, h % 2, :], k.banks[4 + 2 * (h % 2)], ACT.Square,
                                     scale=math.sqrt(EPS)).then_inc(*G("den_ready").inc())
            if step == 1:
                act.wait_ge(*G("centred_ready").ge(h + 1))
                nc.scalar.activation(sq[:, h % 2, :], hm[:, h % 2, :], ACT.Square).then_inc(*G("square_ready").inc())
            if step == 2:
                act.wait_ge(*G("var_ready").ge(h + 1))
                nc.scalar.activation(rs[:, h % 2, :], rs[:, h % 2, :], ACT.Sqrt).then_inc(*rooted.inc())

        def norm_values(dve, chain, h, step):
            hb, rb = hm[:, h % 2, :], rs[:, h % 2, :]
            if step == 1:
                dve.wait_ge(*meaned.ge(2 * h + 1))
                nc.vector.scalar_tensor_tensor(out=hb, in0=k.banks[7], scalar=-1.0 / MHD, in1=hb,
                                               op0=ALU.mult, op1=ALU.add).then_inc(*G("centred_ready").inc())
            if step == 2:
                dve.wait_ge(*G("den_ready").ge(h + 1))
                chain(nc.vector.tensor_tensor(rb, rb, lowb[:, h % 2, :], ALU.max))
                dve.wait_ge(*meaned.ge(2 * h + 2))
                nc.vector.scalar_tensor_tensor(out=rb, in0=k.banks[7], scalar=1.0 / MHD, in1=rb,
                                               op0=ALU.mult, op1=ALU.add).then_inc(*G("var_ready").inc())
            if step == 3:
                dve.wait_ge(*rooted.ge(h + 1))
                chain(nc.vector.reciprocal(rb, rb))
                chain(nc.vector.scalar_tensor_tensor(out=hb, in0=hb, scalar=k.vec("m_norm_g", h), in1=rb,
                                                     op0=ALU.mult, op1=ALU.mult))
                nc.vector.tensor_tensor(y[:, h, :], hb, o[:, h, :], ALU.mult).then_inc(*normed.inc())

        with k.stage() as block:
            @block.tensor
            def _(pe):
                for h in range(MH):
                    for j in range(2):
                        if h >= 1 or j:
                            pe.wait_ge(*G("spread_taken").ge(2 * h + j))
                        src = top if j == 0 else low
                        nc.tensor.matmul(k.banks[0], k.const("ident", MH)[:, h:h + 1].to_broadcast([MH, P]), src[:],
                                         start=True, stop=True).then_inc(*put.inc())
                    for j in range(ST):
                        n = ST * h + j
                        if h:
                            norm_sums(pe, h - 1, j)
                        if n >= 2:
                            pe.wait_ge(*prob.ge(n - 1))
                        nc.tensor.matmul(k.banks[1 + n % 2][:, 0:width[j]], qk[:, MH + h, j * P:(j + 1) * P],
                                         qk[:, h, j * P:S], start=True, stop=True).then_inc(*sent.inc())
                        if j:
                            nums(pe, h, j - 1)
                    nums(pe, h, ST - 1)
                for step in range(ST):
                    norm_sums(pe, MH - 1, step)

            @block.scalar
            def _(act):
                nc.scalar.activation(gd[:, 0, :], gd[:, 0, :], ACT.Sigmoid)
                nc.scalar.activation(gd[0:LORA_G - P, 1, :], gd[0:LORA_G - P, 1, :], ACT.Sigmoid)
                for h in range(MH):
                    for j, dst in enumerate((topb, lowb)):
                        act.wait_ge(*put.ge(2 * h + j + 1))
                        if h >= 2:
                            act.wait_ge(*G("var_ready").ge(h - 1))
                        nc.scalar.copy(dst[:, h % 2, :], k.banks[0]).then_inc(*G("spread_taken").inc())
                    for j in range(ST):
                        n = ST * h + j
                        act.wait_ge(*made.ge(n + 1))
                        nc.scalar.activation(e[:, n % 4, 0:width[j]], e[:, n % 4, 0:width[j]],
                                             ACT.Exp).then_inc(*expd.inc())
                        if h:
                            norm_functions(act, h - 1, j)
                for step in range(ST):
                    norm_functions(act, MH - 1, step)

            @block.vector
            def _(dve):
                chain = Chain(dve, k.counter("dve_step"))
                for h in range(MH):
                    dve.wait_ge(*G("spread_taken").ge(2 * h + 2))
                    for j in range(ST):
                        n = ST * h + j
                        if n >= 4:
                            dve.wait_ge(*summed.ge(n - 3))
                        ed = e[:, n % 4, 0:width[j]]
                        chain(nc.vector.tensor_scalar(ed, topb[:, h % 2, j * P:S], u_col[:, j, h:h + 1], -1.0,
                                                      ALU.subtract, ALU.mult))
                        nc.vector.tensor_scalar(ed, ed, 0.0, None, ALU.min).then_inc(*made.inc())
                        if j:
                            weigh(dve, chain, h, j - 1)
                        if h and j < 3:
                            norm_values(dve, chain, h - 1, j)
                    weigh(dve, chain, h, ST - 1)
                    if h:
                        norm_values(dve, chain, h - 1, 3)
                for step in range(ST):
                    norm_values(dve, chain, MH - 1, step)


def shifted(k, dve, chain, bank, dst, mu, tile, rows=P, at=0):
    nc = k.nc
    chain(nc.vector.tensor_scalar(dst, bank[at:at + rows, :], k.keep_share[0:rows, VECTORS[mu] - VECTORS["mu_rkv"] + tile:][:, 0:1],
                                  None, ALU.mult))
    return nc.vector.scalar_tensor_tensor(out=dst[:, 1:S], in0=bank[at:at + rows, 0:S - 1], scalar=k.vec(mu, tile, rows),
                                          in1=dst[:, 1:S], op0=ALU.mult, op1=ALU.add)


def over_units(mask, n=ST):
    return mask.unsqueeze(1).to_broadcast([mask.shape[0], n, mask.shape[1]])


def rwkv(k, rkv, wd, ad, gd, lora, first):
    nc, G, y = k.nc, k.counter, k.y
    with ExitStack() as ctx:
        step_T = k.sbuf(ctx, "step_T", [P, PAIRS, NCH, CH])
        gain = k.sbuf(ctx, "gain", [P, PAIRS, NCH, CH])
        query = k.sbuf(ctx, "query", [P, PAIRS, S])
        decay = first.decay
        with ExitStack() as pair_ctx:
            bufs = {n: k.sbuf(pair_ctx, n, [P, 2, ST, P]) for n in ("lbT", "lkT", "mbT", "mkT", "inv", "invT", "tmpU")}
            bufs["z"] = k.sbuf(pair_ctx, "zU", [P, 2, ST, CH])
            turned = k.sbuf(pair_ctx, "turned", [P, 4, ST, P])
            values = [k.x[:, 0:4, :], k.sbuf(pair_ctx, "odd_operands", [P, 4, S])]
            pairs = [first] + [Operands(k, p, rkv, wd, ad, lora, decay, values[p % 2]) for p in range(1, PAIRS)]
            for p in range(PAIRS):
                rwkv_units(k, p, pairs[p], pairs[p + 1] if p + 1 < PAIRS else None, bufs, turned, step_T, gain, query, decay)
        state = k.sbuf(ctx, "state", [P, NCH, PAIRS, CH])
        rwkv_recurrence(k, state, step_T, gain, query, decay)
        rwkv_finish(k, rkv, gd, lora, k.sbuf(ctx, "finish", [P, 4, S]))


class Operands:

    def __init__(self, k, p, rkv, wd, ad, lora, decay, values):
        self.k, self.p, self.wd, self.ad, self.lora, self.decay = k, p, wd, ad, lora, decay
        self.alpha, self.rho, self.beta, self.kappa = (values[:, i, :] for i in range(4))
        self.c, self.a, self.t1, self.t2 = (k.x[:, 4 + i, :] for i in range(4))
        self.r, self.kr, self.v = rkv[:, p, :], rkv[:, PAIRS + p, :], rkv[:, 2 * PAIRS + p, :]

    def pe(self, pe, step):
        k, nc, G, lora = self.k, self.k.nc, self.k.counter, self.lora
        w_cols = slice(self.p * P, (self.p + 1) * P)
        if step == 0:
            if self.p == 0:
                pe.wait_ge(*k.small_load())
            nc.tensor.matmul(k.banks[7], lora[0:64, 0, w_cols], self.wd[:], start=True, stop=True)
            nc.tensor.matmul(k.banks[6], lora[0:64, 1, w_cols], self.ad[:], start=True, stop=True).then_inc(*G("lora_ready").inc())
        if step == 1:
            pe.wait_ge(*G("square_ready").ge(1))
            pe.wait_ge(*G("gates_ready").ge(2))
            nc.tensor.matmul(k.banks[7], k.const("ones_half"), self.t1, start=True, stop=True).then_inc(*G("sums_ready").inc())
        if step == 2:
            pe.wait_ge(*G("bonus_terms").ge(1))
            nc.tensor.matmul(k.banks[6], k.const("ones_half"), self.t1, start=True, stop=True).then_inc(*G("sums_ready").inc())

    def act(self, act, step):
        k, nc, G, p = self.k, self.k.nc, self.k.counter, self.p
        if step == 0:
            act.wait_ge(*G("lora_ready").ge(1))
            nc.scalar.activation(self.c, k.banks[7], ACT.Sigmoid, bias=k.vec("r_w0", p)).then_inc(*G("gates_ready").inc())
            nc.scalar.activation(self.a, k.banks[6], ACT.Sigmoid, bias=k.vec("r_a0", p)).then_inc(*G("gates_ready").inc())
            act.wait_ge(*G("kk_ready").ge(1))
            nc.scalar.activation(self.t1, self.t2, ACT.Square).then_inc(*G("square_ready").inc())
        if step == 1:
            act.wait_ge(*G("sums_ready").ge(1))
            nc.scalar.activation(self.t1, k.banks[7], ACT.Sqrt).then_inc(*G("root_ready").inc())
        if step == 2:
            act.wait_ge(*G("decays_ready").ge(2))
            nc.scalar.activation(self.alpha, self.alpha, ACT.Exp).then_inc(*G("exps_ready").inc())
            nc.scalar.activation(self.rho, self.c, ACT.Exp).then_inc(*G("exps_ready").inc())
            nc.scalar.activation(self.kappa, self.c, ACT.Exp, scale=-1.0).then_inc(*G("exps_ready").inc())

    def dve(self, dve, step):
        k, nc, G, p = self.k, self.k.nc, self.k.counter, self.p
        chain = Chain(dve, G("dve_step"))
        alpha, rho, beta, kappa, c, a, t1, t2 = (self.alpha, self.rho, self.beta, self.kappa,
                                                 self.c, self.a, self.t1, self.t2)
        if step == 0:
            nc.vector.tensor_scalar(t2, self.kr, k.vec("r_kk", p), None, ALU.mult).then_inc(*G("kk_ready").inc())
            dve.wait_ge(*G("gates_ready").ge(1))
            chain(nc.vector.tensor_scalar(beta, c, -DECAY, None, ALU.mult))
            nc.vector.tensor_tensor_scan(c, k.const("chunk_start"), beta, 0.0, ALU.mult, ALU.add).then_inc(*G("decays_ready").inc())
            dve.wait_ge(*G("decays_ready").ge(1))
            nc.vector.tensor_tensor(alpha, c, beta, ALU.subtract).then_inc(*G("decays_ready").inc())
        if step == 1:
            dve.wait_ge(*G("root_ready").ge(1))
            chain(nc.vector.tensor_scalar(t1, t1, 1e-12, None, ALU.max))
            chain(nc.vector.reciprocal(t1, t1))
        if step == 2:
            chain(nc.vector.tensor_tensor(t2, t2, t1, ALU.mult))
            dve.wait_ge(*G("gates_ready").ge(2))
            chain(nc.vector.tensor_tensor(beta, t2, a, ALU.mult))
            chain(nc.vector.tensor_scalar(a, a, -1.0, k.vec("r_ka", p), ALU.add, ALU.mult))
            chain(nc.vector.scalar_tensor_tensor(out=a, in0=a, scalar=1.0, in1=self.kr, op0=ALU.add, op1=ALU.mult))
            nc.vector.scalar_tensor_tensor(out=t1, in0=self.r, scalar=k.vec("r_rk", p), in1=a, op0=ALU.mult,
                                           op1=ALU.mult).then_inc(*G("bonus_terms").inc())
        if step == 3:
            dve.wait_ge(*G("exps_ready").ge(3))
            chain(nc.vector.tensor_copy(self.decay[:, p, :], rho.rearrange("p (c t) -> p c t", t=CH)[:, :, CH - 1]))
            nc.vector.tensor_tensor(alpha, alpha, t2, ALU.mult)
            nc.vector.tensor_tensor(rho, rho, self.r, ALU.mult)
            chain(nc.vector.tensor_tensor(beta, beta, kappa, ALU.mult))
            chain(nc.vector.tensor_tensor(kappa, kappa, a, ALU.mult))
            dve.wait_ge(*G("sums_ready").ge(2))
            nc.vector.tensor_tensor(self.r, k.banks[6], self.v, ALU.mult)


def rwkv_units(k, p, own, following, bufs, turned, step_T, gain, query, decay):
    nc, G = k.nc, k.counter
    alpha, rho, beta, kappa, v = own.alpha, own.rho, own.beta, own.kappa, own.v
    ident = k.const("ident")
    lbT, lkT, mbT, mkT, inv, invT, tmp, z = (bufs[n] for n in ("lbT", "lkT", "mbT", "mkT", "inv", "invT", "tmpU", "z"))
    bank = [b.rearrange("p (u t) -> p u t", u=ST) for b in k.banks]
    tok = lambda u: slice(u * P, (u + 1) * P)
    half = [slice(0, CH), slice(CH, P)]

    with k.stage() as block:
        @block.tensor
        def _(pe):
            for i, src in enumerate((alpha, beta, kappa, v)):
                for u in range(ST):
                    last = nc.tensor.transpose(bank[i][:, u, :], src[:, tok(u)], ident)
                last.then_inc(*G("turned_ready").inc())
            for e in range(2):
                rows = half[e]
                for i, (left, right) in enumerate(((beta, alpha), (kappa, alpha), (beta, rho), (kappa, rho), (alpha, beta))):
                    n = 5 * e + i
                    b = (4 + n) % 8
                    if n >= 4:
                        pe.wait_ge(*G("masked_ready").ge(1 + n - 8 + 0) if n >= 8 else G("turned_taken").ge(n - 3))
                    for u in range(ST):
                        last = nc.tensor.matmul(bank[b][:, u, :], left[rows, tok(u)], right[rows, tok(u)],
                                                start=True, stop=True)
                    last.then_inc(*G("product_ready").inc())

        @block.scalar
        def _(act):
            for i in range(4):
                act.wait_ge(*G("turned_ready").ge(i + 1))
                nc.scalar.copy(turned[:, i, :, :], bank[i]).then_inc(*G("turned_taken").inc())

        @block.vector
        def _(dve):
            chain = Chain(dve, G("dve_step"))
            for e in range(2):
                for i, (dst, mask) in enumerate(((lbT, "before"), (lkT, "before"), (mbT, "upto"), (mkT, "upto"))):
                    n = 5 * e + i
                    dve.wait_ge(*G("product_ready").ge(n + 1))
                    if i == 0:
                        nc.vector.tensor_tensor(invT[:, e], bank[(4 + n) % 8], over_units(k.const("level1")), ALU.mult)
                    nc.vector.tensor_tensor(dst[:, e], bank[(4 + n) % 8], over_units(k.const(mask)),
                                            ALU.mult).then_inc(*G("masked_ready").inc())
                n = 5 * e + 4
                dve.wait_ge(*G("product_ready").ge(n + 1))
                chain(nc.vector.tensor_tensor(inv[:, e], bank[(4 + n) % 8], over_units(k.const("level1_lower")), ALU.mult))
                nc.vector.tensor_tensor(invT[:, e], over_units(ident), invT[:, e], ALU.subtract)
                nc.vector.tensor_tensor(inv[:, e], over_units(ident), inv[:, e], ALU.subtract).then_inc(*G("masked_ready").inc())

    levels = [b for b in (2, 4, 8, 16, 32) if b < CH]
    with k.stage() as block:
        @block.tensor
        def _(pe):
            for e in range(2):
                for u in range(ST):
                    last = nc.tensor.matmul(bank[6][:, u, e * CH:(e + 1) * CH], lkT[:, e, u, :], turned[:, 3, u, half[e]],
                                            start=True, stop=True)
            last.then_inc(*G("z_ready").inc())
            for i, b in enumerate(levels):
                for e in range(2):
                    n = 2 * i + e
                    pe.wait_ge(*G("part_ready").ge(n + 1))
                    if i:
                        pe.wait_ge(*G("inverse_ready").ge(n - 1))
                    for u in range(ST):
                        last = nc.tensor.matmul(bank[3 * e][:, u, :], lkT[:, e, u, :], inv[:, e, u, :], start=True, stop=True)
                    last.then_inc(*G("cx_ready").inc())
                for e in range(2):
                    n = 2 * i + e
                    pe.wait_ge(*G("cx_taken").ge(n + 1))
                    for u in range(ST):
                        nc.tensor.matmul(bank[3 * e + 1][:, u, :], invT[:, e, u, :], tmp[:, e, u, :], start=True, stop=True)
                        last = nc.tensor.matmul(bank[3 * e + 2][:, u, :], tmp[:, e, u, :], invT[:, e, u, :], start=True, stop=True)
                    last.then_inc(*G("xcx_ready").inc())
                if following and i in (0, 1, 4):
                    if i == 0:
                        pe.wait_ge(*G("z_taken").ge(1))
                    following.pe(pe, (0, 1, 4).index(i))

        @block.gpsimd
        def _(pool):
            for i, b in enumerate(levels):
                for e in range(2):
                    n = 2 * i + e
                    if i == 0:
                        pool.wait_ge(*G("z_ready").ge(1))
                    else:
                        pool.wait_ge(*G("cx_ready").ge(n - 1))
                    nc.gpsimd.tensor_tensor(lkT[:, e], lbT[:, e], over_units(k.const(f"level{b}")),
                                            ALU.mult).then_inc(*G("part_ready").inc())

        @block.scalar
        def _(act):
            act.wait_ge(*G("z_ready").ge(1))
            for e in range(2):
                last = nc.scalar.copy(z[:, e], bank[6][:, :, e * CH:(e + 1) * CH])
            last.then_inc(*G("z_taken").inc())
            for i, b in enumerate(levels):
                for e in range(2):
                    n = 2 * i + e
                    act.wait_ge(*G("cx_ready").ge(n + 1))
                    if i:
                        act.wait_ge(*G("xcx_ready").ge(n - 1))
                    nc.scalar.copy(tmp[:, e], bank[3 * e]).then_inc(*G("cx_taken").inc())
                if following and i in (0, 1, 3):
                    following.act(act, (0, 1, 3).index(i))

        @block.vector
        def _(dve):
            for i, b in enumerate(levels):
                for e in range(2):
                    dve.wait_ge(*G("xcx_ready").ge(2 * i + e + 1))
                    nc.vector.tensor_tensor(inv[:, e], inv[:, e], bank[3 * e + 1], ALU.subtract)
                    nc.vector.tensor_tensor(invT[:, e], invT[:, e], bank[3 * e + 2], ALU.subtract).then_inc(*G("inverse_ready").inc())
                if following and i != 1:
                    following.dve(dve, (0, 2, 3, 4).index(i))

    wu = inv
    with k.stage() as block:
        @block.tensor
        def _(pe):
            for e in range(2):
                for u in range(ST):
                    nc.tensor.matmul(bank[e][:, u, 0:CH], invT[:, e, u, :], turned[:, 0, u, half[e]], start=True, stop=True)
                    last = nc.tensor.matmul(bank[e][:, u, CH:P], invT[:, e, u, :], z[:, e, u, :], start=True, stop=True)
                last.then_inc(*G("wu_ready").inc())
            for e in range(2):
                rows = half[e]
                pe.wait_ge(*G("wu_taken").ge(e + 1))
                for u in range(ST):
                    nc.tensor.matmul(bank[2][rows, u, :], wu[:, e, u, 0:CH], mbT[:, e, u, :], start=True, stop=True)
                for u in range(ST):
                    nc.tensor.matmul(bank[3][rows, u, :], turned[:, 3, u, rows], mkT[:, e, u, :], start=True, stop=False)
                    nc.tensor.matmul(bank[3][rows, u, :], wu[:, e, u, CH:P], mbT[:, e, u, :], start=False, stop=True)
                for c in range(NCH):
                    u, t, q = c // 2, half[c % 2], 2 * (c % 2)
                    to = slice(u * CH, (u + 1) * CH)
                    nc.tensor.matmul(k.banks[4 + q][rows, to], wu[t, e, u, 0:CH], turned[t, 1, u, rows], start=True, stop=True)
                    nc.tensor.matmul(k.banks[5 + q][rows, to], turned[t, 2, u, rows], turned[t, 3, u, rows], start=True, stop=False)
                    last = nc.tensor.matmul(k.banks[5 + q][rows, to], turned[t, 1, u, rows], wu[t, e, u, CH:P], start=False, stop=True)
            last.then_inc(*G("parts_ready").inc())

        @block.scalar
        def _(act):
            for e in range(2):
                act.wait_ge(*G("wu_ready").ge(e + 1))
                nc.scalar.mul(wu[:, e], bank[e], -1.0).then_inc(*G("wu_taken").inc())
            act.wait_ge(*G("parts_ready").ge(1))
            nc.scalar.copy(k.y[:, 4 + p, :], k.banks[3])

        @block.vector
        def _(dve):
            dve.wait_ge(*G("parts_ready").ge(1))
            nc.vector.tensor_tensor(query[:, p, :], k.banks[2], rho, ALU.add)
            for q in range(2):
                step, new = (k.banks[b + 2 * q][:, 0:ST * CH].rearrange("p (c k) -> p c k", c=ST) for b in (4, 5))
                for e in range(2):
                    nc.vector.tensor_tensor(step_T[half[e], p, q::2], step[half[e]], over_units(ident[half[e], half[e]]), ALU.add)
                nc.vector.tensor_tensor(gain[:, p, q::2], new, decay[:, p, q::2].unsqueeze(2).to_broadcast([P, ST, CH]), ALU.mult)


def rwkv_recurrence(k, state, step_T, gain, query, decay):
    nc, G = k.nc, k.counter
    half = [slice(0, CH), slice(CH, P)]
    bank = [b[:, 0:PAIRS * CH].rearrange("p (q v) -> p q v", q=PAIRS) for b in k.banks]
    with k.stage() as block:
        @block.sync
        def _(sp):
            sp.dma_start(k.x[:], k.xT).then_inc(k.small_landed, 16)
            k.small += 16
            sp.wait_ge(k.small_landed, k.small)

        @block.vector
        def _(dve):
            chain = Chain(dve, G("dve_step"))
            nc.vector.memset(state[:, 0], 0.0).then_inc(*G("state_ready").inc())
            for c in range(NCH - 1):
                dve.wait_ge(*G("stepped").ge(c + 1))
                chain(nc.vector.tensor_tensor(state[:, c + 1], bank[c % 2],
                                              decay[:, :, c].unsqueeze(2).to_broadcast([P, PAIRS, CH]), ALU.mult))
                nc.vector.tensor_tensor(state[:, c + 1], state[:, c + 1], gain[:, :, c, :],
                                        ALU.add).then_inc(*G("state_ready").inc())
            for p in range(PAIRS):
                dve.wait_ge(*G("output_ready").ge(p + 1))
                nc.vector.tensor_tensor(k.y[:, 4 + p, :], k.banks[2 + p], k.y[:, 4 + p, :], ALU.add)

        @block.tensor
        def _(pe):
            for c in range(NCH - 1):
                pe.wait_ge(*G("state_ready").ge(c + 1))
                for p in range(PAIRS):
                    for rows in half:
                        last = nc.tensor.matmul(bank[c % 2][rows, p, :], step_T[rows, p, c, :], state[rows, c, p, :],
                                                start=True, stop=True)
                last.then_inc(*G("stepped").inc())
            pe.wait_ge(*G("state_ready").ge(NCH))
            for p in range(PAIRS):
                for c in range(NCH):
                    for rows in half:
                        last = nc.tensor.matmul(k.banks[2 + p][rows, c * CH:(c + 1) * CH], state[rows, c, p, :],
                                                query[rows, p, c * CH:(c + 1) * CH], start=True, stop=True)
                last.then_inc(*G("output_ready").inc())


def rwkv_finish(k, rkv, gd, lora, scratch):
    nc, G = k.nc, k.counter
    t = [scratch[:, i, :] for i in range(PAIRS)]
    y = [k.y[:, 4 + p, :] for p in range(PAIRS)]
    with k.stage() as block:
        @block.tensor
        def _(pe):
            for p in range(PAIRS):
                nc.tensor.matmul(k.banks[p], k.const("ones_half"), y[p], start=True, stop=True).then_inc(*G("sums_ready").inc())
            for p in range(PAIRS):
                cols = slice(p * P, (p + 1) * P)
                nc.tensor.matmul(k.banks[4 + p], lora[:, 2, cols], gd[:, 0, :], start=True, stop=False)
                nc.tensor.matmul(k.banks[4 + p], lora[0:LORA_G - P, 3, cols], gd[0:LORA_G - P, 1, :], start=False,
                                 stop=True).then_inc(*G("gate_ready").inc())
                pe.wait_ge(*G("square_ready").ge(p + 1))
                nc.tensor.matmul(k.banks[p], k.const("ones_half"), t[p], start=True, stop=True).then_inc(*G("sums_ready").inc())

        @block.scalar
        def _(act):
            for p in range(PAIRS):
                act.wait_ge(*G("centred_ready").ge(p + 1))
                nc.scalar.activation(t[p], y[p], ACT.Square).then_inc(*G("square_ready").inc())
            for p in range(PAIRS):
                act.wait_ge(*G("var_ready").ge(p + 1))
                nc.scalar.activation(t[p], t[p], ACT.Sqrt).then_inc(*G("root_ready").inc())

        @block.vector
        def _(dve):
            chain = Chain(dve, G("dve_step"))
            for p in range(PAIRS):
                dve.wait_ge(*G("sums_ready").ge(p + 1))
                nc.vector.scalar_tensor_tensor(out=y[p], in0=k.banks[p], scalar=-1.0 / RHD, in1=y[p], op0=ALU.mult,
                                               op1=ALU.add).then_inc(*G("centred_ready").inc())
            for p in range(PAIRS):
                dve.wait_ge(*G("sums_ready").ge(PAIRS + p + 1))
                nc.vector.tensor_scalar(t[p], k.banks[p], 1.0 / RHD, GN_EPS, ALU.mult, ALU.add).then_inc(*G("var_ready").inc())
            for p in range(PAIRS):
                dve.wait_ge(*G("root_ready").ge(p + 1))
                chain(nc.vector.reciprocal(t[p], t[p]))
                chain(nc.vector.scalar_tensor_tensor(out=y[p], in0=y[p], scalar=k.vec("r_gn_g", p), in1=t[p],
                                                     op0=ALU.mult, op1=ALU.mult))
                chain(nc.vector.scalar_tensor_tensor(out=y[p], in0=y[p], scalar=k.vec("r_gn_b", p), in1=rkv[:, p, :],
                                                     op0=ALU.add, op1=ALU.add))
                dve.wait_ge(*G("gate_ready").ge(p + 1))
                nc.vector.tensor_tensor(y[p], k.banks[4 + p], y[p], ALU.mult)


def add_to_x(k, name, x, ktiles=DT, tiles=1, arriving=None, before=None, after=None):
    nc = k.nc
    project(k, [Job(name, feature_major(x, ktiles), "dve", lambda e, c, b, m=m: nc.vector.tensor_tensor(
        k.x[:, m, :], k.x[:, m, :], b, ALU.add), tiles) for m in range(DT)], arriving, before, after)


class Unit:

    def __init__(self, pairs, keys, value, width, out, row=0, mask=None):
        self.pairs, self.keys, self.value, self.width, self.out, self.row, self.mask = (
            pairs, keys, value, width, out, row, mask)


def attend(k, units, scale, background=Idle(), pace=0):
    nc, G = k.nc, k.counter
    n = len(units)
    scored, maxed, expd, scaled = G("score_ready"), G("max_ready"), G("exp_ready"), G("prob_ready")
    turned, copied, summed, taken = G("turned_ready"), G("turned_taken"), G("sum_ready"), G("out_taken")
    NS, NB = 4, 3
    with ExitStack() as ctx:
        s = k.sbuf(ctx, k.fresh("scores"), [P, NS, S])
        pT = k.sbuf(ctx, k.fresh("probT"), [P, 2, S])
        small = k.sbuf(ctx, k.fresh("row_stats"), [P, NS, 4])

        with k.stage() as block:
            @block.tensor
            def _(pe):
                for i in range(n + 3):
                    if i < n:
                        un = units[i]
                        if i >= NB:
                            pe.wait_ge(*expd.ge(i - NB + 1))
                        for j, (q, key) in enumerate(un.pairs):
                            last = nc.tensor.matmul(k.banks[i % NB][:, 0:un.keys], q, key, start=(j == 0),
                                                    stop=(j == len(un.pairs) - 1))
                        last.then_inc(*scored.inc())
                        background.pe(pe, pace)
                    if 0 <= i - 2 < n:
                        m, un = i - 2, units[i - 2]
                        pe.wait_ge(*scaled.ge(m + 1))
                        if m >= 2:
                            pe.wait_ge(*copied.ge(m - 1))
                        for c in range(0, un.keys, P):
                            last = nc.tensor.transpose(k.banks[3 + m % 2][:, c:c + P], s[:, m % NS, c:c + P], k.const("ident"))
                        last.then_inc(*turned.inc())
                    if 0 <= i - 3:
                        m, un = i - 3, units[i - 3]
                        pe.wait_ge(*copied.ge(m + 1))
                        if m >= 2:
                            pe.wait_ge(*taken.ge(m - 1))
                        rows = slice(un.row, un.row + un.width)
                        for part, (lo, value) in enumerate(un.value):
                            for c in range(0, un.keys, P):
                                last = nc.tensor.matmul(k.banks[5 + m % 2][rows, lo:lo + P], value(c // P),
                                                        pT[:, m % 2, c:c + P], start=(c == 0), stop=(c == un.keys - P))
                        last.then_inc(*summed.inc())

            @block.vector
            def _(dve):
                chain = Chain(dve, G("dve_step"))
                for i in range(n + 1):
                    if i < n:
                        un = units[i]
                        st = small[:, i % NS, :]
                        dve.wait_ge(*scored.ge(i + 1))
                        src = k.banks[i % NB][:, 0:un.keys]
                        if un.mask is not None:
                            if i >= NS:
                                dve.wait_ge(*turned.ge(i - NS + 1))
                            chain(nc.vector.scalar_tensor_tensor(out=s[:, i % NS, 0:un.keys], in0=src, scalar=scale,
                                                                 in1=un.mask, op0=ALU.mult, op1=ALU.add))
                            nc.vector.tensor_reduce(st[:, 1:2], s[:, i % NS, 0:un.keys], AX, ALU.max,
                                                    negate=True).then_inc(*maxed.inc())
                        else:
                            chain(nc.vector.tensor_reduce(st[:, 0:1], src, AX, ALU.max))
                            nc.vector.tensor_scalar(st[:, 1:2], st[:, 0:1], -scale, None, ALU.mult).then_inc(*maxed.inc())
                    if i:
                        m, un = i - 1, units[i - 1]
                        st = small[:, m % NS, :]
                        dve.wait_ge(*expd.ge(m + 1))
                        chain(nc.vector.reciprocal(st[:, 3:4], st[:, 2:3]))
                        nc.vector.tensor_scalar(s[:, m % NS, 0:un.keys], s[:, m % NS, 0:un.keys], st[:, 3:4], None,
                                                ALU.mult).then_inc(*scaled.inc())

            @block.scalar
            def _(act):
                for i in range(n + 3):
                    if i < n:
                        un = units[i]
                        act.wait_ge(*maxed.ge(i + 1))
                        if i >= NS:
                            act.wait_ge(*turned.ge(i - NS + 1))
                        src = s[:, i % NS, 0:un.keys] if un.mask is not None else k.banks[i % NB][:, 0:un.keys]
                        nc.scalar.activation(s[:, i % NS, 0:un.keys], src, ACT.Exp, bias=small[:, i % NS, 1:2],
                                             scale=1.0 if un.mask is not None else scale,
                                             accum_out=small[:, i % NS, 2:3]).then_inc(*expd.inc())
                        background.act(act, pace)
                    if 0 <= i - 2 < n:
                        m, un = i - 2, units[i - 2]
                        act.wait_ge(*turned.ge(m + 1))
                        if m >= 2:
                            act.wait_ge(*summed.ge(m - 1))
                        nc.scalar.copy(pT[:, m % 2, 0:un.keys], k.banks[3 + m % 2][:, 0:un.keys]).then_inc(*copied.inc())
                    if 0 <= i - 3:
                        m, un = i - 3, units[i - 3]
                        act.wait_ge(*summed.ge(m + 1))
                        rows = slice(un.row, un.row + un.width)
                        w = len(un.value) * P
                        nc.scalar.copy(un.out, k.banks[5 + m % 2][rows, 0:w] if w == P else
                                       k.banks[5 + m % 2][rows, 0:w].rearrange("p (a t) -> p a t", t=P)).then_inc(*taken.inc())

            @block.gpsimd
            def _(pool):
                k.split_low(pool, k.split_h)

            @block.sync
            def _(sp):
                k.prefetch_split(sp)


def memory_attention(k):
    nc = k.nc
    with ExitStack() as ctx:
        key = k.sbuf(ctx, "x_key", [P, DT, MEM])
        value = k.sbuf(ctx, "x_value", [P, MEM // P, D])
        q = k.sbuf(ctx, "x_query", [P, DT, S])
        o = k.sbuf(ctx, "x_out", [P, DT, S])
        raw = k.sbuf(ctx, "memory", [P, DT, MEM])
        with ExitStack() as h_ctx:
            h = halves(k, h_ctx, k.fresh("h"), [P, DT, S])
            normed = rms_norm(k, h_ctx, k.x, h, "norm_x")
            project(k, [Job("x_q", feature_major(h), "act",
                            lambda e, c, b, t=t: nc.scalar.copy(q[:, t, :], b)) for t in range(DT)], normed, before=lambda sp: k.load_small(sp, raw[:], k.memT))
        with ExitStack() as mem_ctx:
            mem, normed = normed_memory(k, mem_ctx, raw, "norm_mem")
            project(k, [Job("x_k", feature_major(mem, n=MEM), "act",
                            lambda e, c, b, t=t: nc.scalar.copy(key[:, t, :], b[:, 0:MEM])) for t in range(DT)], normed)
            for half in range(2):
                project_tokens(k, "x_v", mem, MEM, lambda act, t, b: nc.scalar.copy(value[:, t, half * 512:(half + 1) * 512], b))
        units = []
        for h in range(XH):
            for t in range(ST):
                tok = slice(t * P, (t + 1) * P)
                units.append(Unit([(q[:, 2 * h + j, tok], key[:, 2 * h + j, :]) for j in range(2)], MEM,
                                  [(P * j, lambda c, h=h, j=j: value[:, c, (2 * h + j) * P:(2 * h + j + 1) * P]) for j in range(2)],
                                  P, o[:, 2 * h:2 * h + 2, tok]))
        attend(k, units, XHD ** -0.5)
        oh = halves(k, ctx, "x_out_parts", [P, DT, S])
        add_to_x(k, "x_o", oh, arriving=Splitting(k, o, oh, DT))


def normed_memory(k, ctx, raw, gain):
    mem = halves(k, ctx, k.fresh("memory_normed"), [P, DT, MEM])
    return mem, rms_norm(k, ctx, raw, mem, gain, MEM, landed=lambda i: k.small_load())


def conv_glu(k):
    nc = k.nc
    with ExitStack() as ctx:
        act_t = halves(k, ctx, "ffn_act", [P, FT, S])
        with ExitStack() as h_ctx:
            h = halves(k, h_ctx, k.fresh("h"), [P, DT, S])
            gate = k.sbuf(h_ctx, "ffn_gate", [P, GATES, S])
            glu(k, h, rms_norm(k, h_ctx, k.x, h, "norm_ffn", room=gate), gate, act_t)
        add_to_x(k, "f_down", act_t, FT, 3)


def glu(k, h, arriving, gate, act_t):
    nc = k.nc
    conv_ready, silu_ready = k.counter("conv_ready"), k.counter("silu_ready")
    value_taken, high_made, low_made = k.counter("value_taken"), k.counter("high_made"), k.counter("low_made")
    first = k.used
    k.used += 2 * FT

    def times_value(dve, f):
        dve.wait_ge(*silu_ready.ge(f + 1))
        dve.wait_ge(k.tile_used, first + 2 * f + 2)
        nc.vector.tensor_tensor(gate[:, f % GATES, :], k.banks[2 * (f % 4) + 1], gate[:, f % GATES, :],
                                ALU.mult).then_inc(*value_taken.inc())

    def high(act, f):
        act.wait_ge(*value_taken.ge(f + 1))
        nc.scalar.copy(act_t.hi[:, f, :], gate[:, f % GATES, :]).then_inc(*high_made.inc())

    def low(pool, f):
        pool.wait_ge(*high_made.ge(f + 1))
        nc.gpsimd.tensor_tensor(act_t.lo[:, f, :], gate[:, f % GATES, :], act_t.hi[:, f, :].bitcast(F32),
                                ALU.subtract).then_inc(*low_made.inc())

    with k.stage() as block:
        @block.sync
        def _(sp):
            k.prefetch(sp, k.used)

        @block.tensor
        def _(pe):
            arriving.pe(pe)
            for f in range(FT):
                for half, taken in enumerate((conv_ready, value_taken)):
                    t = first + 2 * f + half
                    if f >= 4:
                        pe.wait_ge(*taken.ge(f - 3))
                    feature_major(h)(k, pe, t, k.banks[2 * (f % 4) + half], None if f or half else arriving)

        @block.vector
        def _(dve):
            arriving.dve(dve)
            chain = Chain(dve, k.counter("dve_step"))
            for f in range(FT):
                dve.wait_ge(k.tile_used, first + 2 * f + 1)
                if f >= GATES:
                    dve.wait_ge(*low_made.ge(f - GATES + 1))
                conv(k, dve, chain, k.banks[2 * (f % 4)], gate[:, f % GATES, :], "f_conv_w", "f_conv_b",
                     f, 3).then_inc(*conv_ready.inc())
                if f:
                    times_value(dve, f - 1)
            times_value(dve, FT - 1)

        @block.scalar
        def _(act):
            arriving.act(act)
            for f in range(FT):
                k.split_high(act, first + 2 * f + 1 + LEAD)
                if f:
                    high(act, f - 1)
                k.split_high(act, first + 2 * f + 2 + LEAD)
                act.wait_ge(*conv_ready.ge(f + 1))
                nc.scalar.activation(gate[:, f % GATES, :], gate[:, f % GATES, :], ACT.Silu).then_inc(*silu_ready.inc())
            high(act, FT - 1)

        @block.gpsimd
        def _(pool):
            arriving.pool(pool)
            for f in range(FT):
                k.split_low(pool, first + 2 * f + 2 + LEAD)
                if f:
                    low(pool, f - 1)
            low(pool, FT - 1)


def rope_tables(k, freq, cos, sin, spill=False):
    nc, G = k.nc, k.counter
    tables = [(freq, cos, sin)]
    magic = 1.5 * 2.0 ** 23
    c1 = 6.28125
    c2 = float(np.float32(2 * math.pi - c1))
    c2 = float((np.array([c2], np.float32).view(np.uint32) & 0xFFFFF000).view(np.float32)[0])
    c3 = 2 * math.pi - c1 - c2
    top = float(np.nextafter(np.float32(math.pi), np.float32(0)))
    with ExitStack() as ctx:
        raw = k.sbuf(ctx, k.fresh("pos_raw"), [P, S], I32)
        pos = k.sbuf(ctx, k.fresh("pos"), [P, S])
        turns = k.sbuf(ctx, k.fresh("pos_turns"), [P, S])
        with k.stage() as block:
            @block.sync
            def _(sp):
                sp.dma_start(raw[:], k.positions.to_broadcast([P, S])).then_inc(k.small_landed, 16)
                k.small += 16
                if spill:
                    sp.dma_start(k.x_spill, k.x[:]).then_inc(k.spilled, 16)
                    sp.wait_ge(k.spilled, 16)

            @block.vector
            def _(dve):
                chain = Chain(dve, G("dve_step"))
                dve.wait_ge(k.small_landed, k.small)
                chain(nc.vector.tensor_copy(pos[:], raw[:]))
                for i, (freq, cos, sin) in enumerate(tables):
                    chain(nc.vector.tensor_scalar(cos, pos[:], k.const(freq), None, ALU.mult))
                    chain(nc.vector.tensor_scalar(turns[:], cos, 1.0 / (2 * math.pi), magic, ALU.mult, ALU.add))
                    chain(nc.vector.tensor_scalar(turns[:], turns[:], -magic, None, ALU.add))
                    for part in (c1, c2, c3):
                        chain(nc.vector.scalar_tensor_tensor(out=cos, in0=turns[:], scalar=-part, in1=cos,
                                                             op0=ALU.mult, op1=ALU.add))
                    nc.vector.tensor_scalar(cos, cos, top, -top, ALU.min, ALU.max).then_inc(*G("angle_ready").inc())
                for i, (freq, cos, sin) in enumerate(tables):
                    dve.wait_ge(*G("abs_ready").ge(i + 1))
                    nc.vector.tensor_scalar(cos, cos, -1.0, math.pi / 2, ALU.mult, ALU.add).then_inc(*G("cos_arg_ready").inc())

            @block.scalar
            def _(act):
                for i, (freq, cos, sin) in enumerate(tables):
                    act.wait_ge(*G("angle_ready").ge(i + 1))
                    nc.scalar.activation(sin, cos, ACT.Sin)
                    nc.scalar.activation(cos, cos, ACT.Abs).then_inc(*G("abs_ready").inc())
                for i, (freq, cos, sin) in enumerate(tables):
                    act.wait_ge(*G("cos_arg_ready").ge(i + 1))
                    nc.scalar.activation(cos, cos, ACT.Sin)


def rotate_tiles(k, items, background):
    nc, G = k.nc, k.counter
    with ExitStack() as ctx:
        tmp = k.sbuf(ctx, k.fresh("turned_half"), [P, 2, S])
        with k.stage() as block:
            @block.tensor
            def _(pe):
                for i, (x, rows, matrix, cos, sin) in enumerate(items):
                    if i >= 2:
                        pe.wait_ge(*G("sin_taken").ge(i - 1))
                    nc.tensor.matmul(k.banks[i % 2][0:rows, :], matrix, x, start=True, stop=True).then_inc(*G("swapped").inc())
                    background.pe(pe, 1)

            @block.vector
            def _(dve):
                chain = Chain(dve, G("dve_step"))
                for i, (x, rows, matrix, cos, sin) in enumerate(items):
                    dve.wait_ge(*G("swapped").ge(i + 1))
                    nc.vector.tensor_tensor(tmp[0:rows, i % 2, :], k.banks[i % 2][0:rows, :], sin,
                                            ALU.mult).then_inc(*G("sin_taken").inc())
                    chain(nc.vector.tensor_tensor(x, x, cos, ALU.mult))
                    nc.vector.tensor_tensor(x, x, tmp[0:rows, i % 2, :], ALU.add)

            @block.scalar
            def _(act):
                background.act(act, len(items))

            @block.gpsimd
            def _(pool):
                k.split_low(pool, k.split_h)

            @block.sync
            def _(sp):
                k.prefetch_split(sp)


def choose_keys(k, qi, ki, wi, chosen, background):
    nc, G = k.nc, k.counter
    with ExitStack() as ctx:
        r = k.sbuf(ctx, "relu_dots", [P, 4, S])
        top = k.sbuf(ctx, "top8", [P, ST, 8])
        with k.stage() as block:
            @block.tensor
            def _(pe):
                for t in range(1, ST):
                    keys = (t + 1) * P
                    for h in range(AH):
                        i = (t - 1) * AH + h
                        rows = slice(64 * (h % 2), 64 * (h % 2) + 64)
                        if i >= 4:
                            pe.wait_ge(*G("relu_ready").ge(i - 3))
                        nc.tensor.matmul(k.banks[i % 4][:, 0:keys], qi[rows, h // 2, t * P:(t + 1) * P], ki[rows, 0:keys],
                                         start=True, stop=True).then_inc(*G("dots_ready").inc())
                background.pe(pe, CHOOSE_STEPS)

            @block.scalar
            def _(act):
                for t in range(1, ST):
                    keys = (t + 1) * P
                    for h in range(AH):
                        i = (t - 1) * AH + h
                        act.wait_ge(*G("dots_ready").ge(i + 1))
                        if i >= 4:
                            act.wait_ge(*G("dots_added").ge(i - 3))
                        nc.scalar.activation(r[:, i % 4, 0:keys], k.banks[i % 4][:, 0:keys], ACT.Relu,
                                             scale=AHD ** -0.5).then_inc(*G("relu_ready").inc())
                background.act(act, CHOOSE_STEPS)

            @block.vector
            def _(dve):
                chain = Chain(dve, G("dve_step"))
                chosen_step = [G(f"chosen_step_{t}") for t in range(ST)]
                chain(nc.vector.tensor_scalar(wi, wi, AH ** -0.5, None, ALU.mult))
                chain(nc.vector.tensor_copy(chosen[:, 0, 0:P], k.const("causal")[:, S - P:S]))
                for t in range(1, ST):
                    keys = (t + 1) * P
                    acc = chosen[:, t, 0:keys]
                    for h in range(AH):
                        i = (t - 1) * AH + h
                        dve.wait_ge(*G("relu_ready").ge(i + 1))
                        w = wi[:, t, h:h + 1]
                        if h == 0:
                            ins = nc.vector.tensor_scalar(acc, r[:, i % 4, 0:keys], w, None, ALU.mult)
                        else:
                            dve.wait_ge(*G("dots_added").ge(i))
                            ins = nc.vector.scalar_tensor_tensor(out=acc, in0=r[:, i % 4, 0:keys], scalar=w, in1=acc,
                                                                 op0=ALU.mult, op1=ALU.add)
                        ins.then_inc(*G("dots_added").inc())
                    dve.wait_ge(*G("dots_added").ge(t * AH))
                    nc.vector.tensor_tensor(acc, acc, k.const("causal")[:, S - keys:S], ALU.add).then_inc(*chosen_step[t].inc())

                def step(t, ins):
                    ins.then_inc(*chosen_step[t].inc())

                accs = [(t, chosen[:, t, 0:(t + 1) * P]) for t in range(ST - 1, 0, -1)]
                for r8 in range(TOPK // 8):
                    for t, acc in accs:
                        dve.wait_ge(*chosen_step[t].ge(2 * r8 + 1))
                        step(t, nc.vector.max(out=top[:, t], in_=acc))
                    for t, acc in accs:
                        dve.wait_ge(*chosen_step[t].ge(2 * r8 + 2))
                        step(t, nc.vector.match_replace(out=acc, in_to_replace=top[:, t], in_values=acc, imm_value=CHOSEN))
                for t, acc in accs:
                    dve.wait_ge(*chosen_step[t].all())
                    nc.vector.tensor_scalar(acc, acc, CHOSEN / 2, NEG, ALU.is_gt, ALU.mult)

            @block.gpsimd
            def _(pool):
                k.split_low(pool, k.split_h)

            @block.sync
            def _(sp):
                k.prefetch_split(sp)


def gates(k, name, z, sg):
    return Background(k, [(name, z[:, t, :]) for t in range(BW // P)] + [("gate", sg[:, m, :]) for m in range(DT)])


def close_branch(k, n, y, z, sg, merged, before=None):
    nc = k.nc

    def weigh(m):
        def take(dve, chain, bank):
            dve.wait_ge(*k.counter("gate_ready").ge(m + 1))
            if n == 0:
                return nc.vector.tensor_tensor(merged[:, m, :], bank, sg[:, m, :], ALU.mult)
            chain(nc.vector.tensor_tensor(sg[:, m, :], bank, sg[:, m, :], ALU.mult))
            return nc.vector.tensor_tensor(merged[:, m, :], merged[:, m, :], sg[:, m, :], ALU.add)
        return take

    with ExitStack() as ctx:
        yh = halves(k, ctx, k.fresh("gated"), [P, 4, S])
        project(k, [Job("branch", feature_major(yh, 4), "dve", weigh(m)) for m in range(DT)],
                Gating(k, y, z, sg, yh, 4), before)


def sparse_branch(k, merged):
    nc = k.nc
    with ExitStack() as ctx:
        y, z, sg = k.sbuf(ctx, "a_y", [P, 4, S]), k.sbuf(ctx, "a_z", [P, 4, S]), k.sbuf(ctx, "a_gate", [P, DT, S])
        with ExitStack() as at_ctx:
            qk = k.x
            v = k.sbuf(at_ctx, "a_v", [P, ST, AH * AHD])
            chosen = k.sbuf(at_ctx, "a_chosen", [P, ST, S])
            with ExitStack() as index_ctx:
                qi = k.sbuf(index_ctx, "a_qi", [P, 4, S])
                ki = k.sbuf(index_ctx, "a_ki", [P, S])
                wi = k.sbuf(index_ctx, "a_wi", [P, ST, AH])
                wiT = k.sbuf(index_ctx, "a_wiT", [AH, S])
                cos, sin = k.sbuf(index_ctx, "cos_a", [P, S]), k.sbuf(index_ctx, "sin_a", [P, S])
                rope_tables(k, "freq_a", cos[:], sin[:], spill=True)
                copy = lambda dst: (lambda e, c, b: nc.scalar.copy(dst, b[0:dst.shape[0], :]))
                jobs = [Job("a_qk", feature_major(k.h), "act", copy(qk[:, t, :])) for t in range(8)]
                jobs += [Job("a_qi", feature_major(k.h), "act", copy(qi[:, t, :])) for t in range(4)]

                def small(act, chain, bank):
                    for half in range(2):
                        nc.scalar.copy(ki[half * AHD:(half + 1) * AHD, :], bank[0:AHD, :])
                    nc.scalar.copy(wiT[:], bank[AHD:AHD + AH, :])
                    return nc.scalar.copy(k.rope_key, bank[P - BROPE:P, :])

                jobs.append(Job("a_small", feature_major(k.h), "act", small))
                project(k, jobs, rms_norm(k, index_ctx, k.x, k.h, "g_norm_2", room=sg))
                project_tokens(k, "a_v", k.h, S, lambda act, t, b: nc.scalar.copy(v[:, t, :], b))
                with k.stage() as block:
                    @block.tensor
                    def _(pe):
                        for t in range(ST):
                            last = nc.tensor.matmul(k.banks[0][:, t * AH:(t + 1) * AH], wiT[:, t * P:(t + 1) * P],
                                                    k.const("ident", AH)[:, 0:AH], start=True, stop=True)
                        last.then_inc(*k.counter("turned_ready").inc())

                    @block.vector
                    def _(dve):
                        dve.wait_ge(*k.counter("turned_ready").ge(1))
                        nc.vector.tensor_copy(wi[:].rearrange("p t h -> p (t h)"), k.banks[0][:, 0:ST * AH])
                background = gates(k, "a_z", z, sg)
                head_norms(k, [(qk[:, t, :], P, 2, AHD, "g_qn_a_2" if t < 4 else "g_kn_a_2") for t in range(8)],
                           room=sg)
                tiles = [qk[:, t, :] for t in range(8)] + [qi[:, t, :] for t in range(4)] + [ki[:]]
                rotate_tiles(k, [(x, P, k.const("rotate_a"), cos[:], sin[:]) for x in tiles], background)
                choose_keys(k, qi, ki, wi[:], chosen, background)
            units = []
            for h in range(AH):
                rows = slice(AHD * (h % 2), AHD * (h % 2) + AHD)
                for t in range(ST):
                    keys, tok = (t + 1) * P, slice(t * P, (t + 1) * P)
                    units.append(Unit([(qk[rows, h // 2, tok], qk[rows, 4 + h // 2, 0:keys])], keys,
                                      [(0, lambda c, h=h: v[:, c, h * AHD:(h + 1) * AHD])], AHD,
                                      y[rows, h // 2, tok], AHD * (h % 2), chosen[:, t, 0:keys]))
            attend(k, units, AHD ** -0.5, background, 1)
            background.finish()
        close_branch(k, 0, y, z, sg, merged)


def latent_branch(k, merged):
    nc = k.nc
    with ExitStack() as ctx:
        y, z, sg = k.sbuf(ctx, "b_y", [P, 4, S]), k.sbuf(ctx, "b_z", [P, 4, S]), k.sbuf(ctx, "b_gate", [P, DT, S])
        with ExitStack() as at_ctx:
            q = k.x
            key = k.sbuf(at_ctx, "b_k", [P, BH, S])
            v = k.sbuf(at_ctx, "b_v", [P, ST, BH * BV])
            rope = slice(BNOPE, BQK)
            with ExitStack() as c_ctx:
                ch = halves(k, c_ctx, "b_c", [P, 5, S])
                c = q

                jobs = [Job("b_c", feature_major(k.h), "act", lambda e, cc, b, t=t: nc.scalar.copy(c[:, t, :], b)) for t in range(5)]
                project(k, jobs)
                with ExitStack() as n_ctx:
                    normed = Norms(k, n_ctx, room=sg, groups=[(t * P, [(c[:, i, :], ch[:, i, :], P, k.vec(gain, i - at)) for i in range(at, at + t)])
                                              for gain, at, t in (("g_cq_2", 0, 3), ("g_ckv_2", 3, 2))])
                    project(k, [Job("b_uq", feature_major(ch, 3), "act",
                                    lambda e, cc, b, h=h: nc.scalar.copy(q[0:BQK, h, :], b[0:BQK, :])) for h in range(BH)], normed)
                t = k.used
                k.used += 1
                with k.stage() as block:
                    @block.sync
                    def _(sp):
                        k.prefetch(sp, k.used)

                    @block.tensor
                    def _(pe):
                        assert k.plan[t][0] == "b_uk"
                        pe.wait_ge(*k.tile_ready(t))
                        hi, lo = k.slot(t)
                        for pair in range(BH // 2):
                            for j in range(2):
                                cols = slice((2 * pair + j) * P, (2 * pair + j + 1) * P)
                                last = product(k, k.banks[pair], Halves(hi[:, cols], lo[:, cols]), ch[:, 3 + j, :], j == 0, j == 1)
                        last.then_inc(k.tile_used, 1)

                    @block.scalar
                    def _(act):
                        k.split_high(act, t + 1 + LEAD)
                        act.wait_ge(k.tile_used, t + 1)
                        for h in range(BH):
                            nc.scalar.copy(key[0:BNOPE, h, :], k.banks[h // 2][BNOPE * (h % 2):BNOPE * (h % 2) + BNOPE, :])

                    @block.gpsimd
                    def _(pool):
                        k.split_low(pool, k.used + LEAD)
                        pool.wait_ge(k.low_ready, k.split_l)
                        chain = Chain(pool, k.counter("pool_step"))
                        for h in range(BH):
                            chain(nc.gpsimd.tensor_copy(key[rope, h, :], k.rope_key))
                project_tokens(k, "b_uv", ch[:, 3:5, :], S, lambda act, t, b: nc.scalar.copy(v[:, t, :], b), ktiles=2)
            with ExitStack() as rope_ctx:
                cos, sin = k.sbuf(rope_ctx, "cos_b", [P, S]), k.sbuf(rope_ctx, "sin_b", [P, S])
                rope_tables(k, "freq_b", cos[:], sin[:])
                background = gates(k, "b_z", z, sg)
                head_norms(k, [(q[0:BQK, h, :], BQK, 1, BQK, "g_qn_b_2") for h in range(BH)] +
                           [(key[0:BQK, h, :], BQK, 1, BQK, "g_kn_b_2") for h in range(BH)],
                           room=sg)
                rotate_tiles(k, [(x[0:BQK, h, :], BQK, k.const("rotate_b", BQK), cos[0:BQK], sin[0:BQK])
                                 for x in (q, key) for h in range(BH)], background)
            units = []
            for h in range(BH):
                rows = slice(BV * (h % 2), BV * (h % 2) + BV)
                for t in range(ST):
                    keys, tok = (t + 1) * P, slice(t * P, (t + 1) * P)
                    units.append(Unit([(q[0:BQK, h, tok], key[0:BQK, h, 0:keys])], keys,
                                      [(0, lambda c, h=h: v[:, c, h * BV:(h + 1) * BV])], BV,
                                      y[rows, h // 2, tok], BV * (h % 2), k.const("causal")[:, S - keys:S]))
            attend(k, units, BQK ** -0.5, background, 1)
            background.finish()
        k.memory_rows = k.x[:, 0:DT * MEM // S, :].rearrange("p a (b n) -> p (a b) n", n=MEM)
        close_branch(k, 1, y, z, sg, merged, before=lambda sp: k.load_small(sp, k.memory_rows, k.mem2T))


def memory_branch(k, merged):
    nc = k.nc
    with ExitStack() as ctx:
        y, z, sg = k.sbuf(ctx, "m2_y", [P, 4, S]), k.sbuf(ctx, "m2_z", [P, 4, S]), k.sbuf(ctx, "m2_gate", [P, DT, S])
        with ExitStack() as at_ctx:
            key = k.sbuf(at_ctx, "m2_k", [P, 4, MEM])
            value = k.sbuf(at_ctx, "m2_v", [P, MEM // P, 512])
            q = k.sbuf(at_ctx, "m2_q", [P, 4, S])
            with ExitStack() as mem_ctx:
                mem, normed = normed_memory(k, mem_ctx, k.memory_rows, "g_mem_2")
                project(k, [Job("m2_k", feature_major(mem, n=MEM), "act",
                                lambda e, c, b, t=t: nc.scalar.copy(key[:, t, :], b[:, 0:MEM])) for t in range(4)], normed)
                project_tokens(k, "m2_v", mem, MEM, lambda act, t, b: nc.scalar.copy(value[:, t, :], b),
                               before=lambda sp: sp.dma_start(k.x[:], k.x_spill).then_inc(k.spilled, 16))
            project(k, [Job("m2_q", feature_major(k.h), "act",
                            lambda e, c, b, t=t: nc.scalar.copy(q[:, t, :], b)) for t in range(4)])
            background = gates(k, "m2_z", z, sg)
            head_norms(k, [(q[:, h, :], P, 1, P, "g_qn_m_2") for h in range(4)])
            head_norms(k, [(key[:, h, :], P, 1, P, "g_kn_m_2") for h in range(4)], MEM)
            units = []
            for h in range(4):
                for t in range(ST):
                    tok = slice(t * P, (t + 1) * P)
                    units.append(Unit([(q[:, h, tok], key[:, h, :])], MEM,
                                      [(0, lambda c, h=h: value[:, c, h * P:(h + 1) * P])], P, y[:, h, tok]))
            attend(k, units, P ** -0.5, background, 1)
            background.finish()
        close_branch(k, 2, y, z, sg, merged)


def second_block(k):
    nc = k.nc
    with ExitStack() as ctx:
        merged = k.sbuf(ctx, "merged", [P, DT, S])
        k.rope_key = k.const("chunk_start")[BNOPE:BQK, :]
        with ExitStack() as h_ctx:
            k.h = halves(k, h_ctx, k.fresh("h"), [P, DT, S])
            sparse_branch(k, merged)
            latent_branch(k, merged)
            memory_branch(k, merged)
        mh = halves(k, ctx, "merged_parts", [P, DT, S])
        def store(sp):
            for m in range(DT):
                sp.wait_ge(*k.counter("bank_taken_dve").ge(m + 1))
                sp.dma_start(k.out[:, m, :], k.x[:, m, :]).then_inc(k.stored, 16)
            sp.wait_ge(k.stored, 16 * DT)

        with k.stage() as block:
            @block.sync
            def _(sp):
                sp.wait_ge(k.spilled, 32)
        add_to_x(k, "w_out_2", mh, arriving=Splitting(k, merged, mh, DT), after=store)


def build(nc, weights, vectors, constants, xT, memT, mem2T, lora, positions, out, plan, const_at, n_vec):
    with ExitStack() as ctx:
        k = Kernel(nc, ctx)
        k.plan, k.weights, k.const_at, k.loaded, k.used, k.out = plan, weights, const_at, 0, 0, out
        k.ring = k.sbuf(ctx, "ring", [P, SLOTS, SLOT])
        k.consts = k.sbuf(ctx, "consts", [P, constants.shape[1]])
        k.vecs = k.sbuf(ctx, "vecs", [P, n_vec])
        k.x = k.sbuf(ctx, "x", [P, DT, S])
        k.parts = k.sbuf(ctx, "parts", [P, PARTS, 2, SLOT], F32R)
        psum = ctx.enter_context(nc.psum_tensor("banks", [P, 8, 512], F32))
        k.psum = psum
        k.banks = [psum[:, b, :] for b in range(8)]
        k.landed = [ctx.enter_context(nc.semaphore(f"slot{i}_landed")) for i in range(SLOTS)]
        k.high_ready = ctx.enter_context(nc.semaphore("high_ready"))
        k.low_ready = ctx.enter_context(nc.semaphore("low_ready"))
        k.spilled = ctx.enter_context(nc.semaphore("spilled"))
        k.x_spill = nc.dram_tensor("x_spill", (P, DT, S), F32, kind="Internal").ap()
        k.xT, k.split_h, k.split_l, k.used_before, k.split_at_end = xT, 0, 0, 0, 0
        k.tile_used = ctx.enter_context(nc.semaphore("tile_used"))
        x_landed = [ctx.enter_context(nc.semaphore(f"x_half{i}_landed")) for i in range(2)]
        tables_landed = ctx.enter_context(nc.semaphore("tables_landed"))
        k.background_taken, k.taken_in_background = ctx.enter_context(nc.semaphore("background_taken")), 0
        k.small_landed = ctx.enter_context(nc.semaphore("small_landed"))
        k.stored = ctx.enter_context(nc.semaphore("out_stored"))
        k.lora, k.memT, k.mem2T, k.positions = lora, memT, mem2T, positions
        def load_inputs(sp):
            for half, sem in enumerate(x_landed):
                part = slice(half * DT // 2, (half + 1) * DT // 2)
                sp.dma_start(k.x[:, part, :], xT[:, part, :]).then_inc(sem, 16)
                if half == 0:
                    sp.dma_start(k.consts[:], constants).then_inc(tables_landed, 16)
                    sp.dma_start(k.vecs[:], vectors).then_inc(tables_landed, 16)

        k.load_inputs = load_inputs
        k.inputs_landed = lambda i: (tables_landed, 32) if i is None else (x_landed[i * 2 // DT], 16)
        stages(k)


def stages(k):
    mixer(k)
    memory_attention(k)
    conv_glu(k)
    norm_stage(k, [(D, [(k.x[:, t, :], k.x[:, t, :], P, k.vec("norm_final", t)) for t in range(DT)])])
    second_block(k)


def kernel(**inputs):
    import concourse.bacc as _bacc
    from concourse.bass_utils import run_bass_kernel_spmd as _run

    plan = weight_plan()
    weights = np.zeros((len(plan), P, SLOT), np.float32)
    mats = {n: np.asarray(inputs[n][0]) for n in ("w_in", "w_out", "x_wq", "x_wkv", "x_wo", "f_up", "f_down",
                                      "w_in_2", "w_uq_2", "w_ukv_2", "w_mem_kv_2", "w_branch_2", "w_out_2")}
    mats["w_branch_2"] = mats["w_branch_2"].reshape(-1, D)
    for t, (_, blocks) in enumerate(plan):
        at = 0
        for mat, row, rows, col, cols in blocks:
            if mat:
                weights[t, :rows, at:at + cols] = mats[mat][row:row + rows, col:col + cols]
            at += cols

    def tiles(a):
        return np.ascontiguousarray(np.asarray(a).T.reshape(DT, P, -1).transpose(1, 0, 2))

    lora = np.zeros((P, 4, RW), np.float32)
    lora[:64, 0], lora[:64, 1] = inputs["r_w_up"][0], inputs["r_a_up"][0]
    lora[:, 2], lora[:LORA_G - P, 3] = inputs["r_g_up"][0, :P], inputs["r_g_up"][0, P:]
    vectors = vector_table(inputs)
    constants, const_at = constant_table()
    arrays = {
        "weights": weights, "vectors": vectors, "constants": constants, "xT": tiles(inputs["x"][0]),
        "memT": tiles(inputs["mem"][0]), "mem2T": tiles(inputs["mem_2"][0]), "lora": lora,
        "positions": np.ascontiguousarray(inputs["positions_2"]),
    }
    nc = _bacc.Bacc("TRN2", target_bir_lowering=False, num_devices=1)
    args = [nc.dram_tensor(n, a.shape, mybir.dt.from_np(a.dtype), kind="ExternalInput").ap() for n, a in arrays.items()]
    out = nc.dram_tensor("outT", (P, DT, S), F32, kind="ExternalOutput").ap()
    build(nc, *args, out, plan, const_at, vectors.shape[1])
    r = _run(nc, [arrays], core_ids=[0])
    got = np.asarray(r.results[0]["outT"])
    return np.ascontiguousarray(got.transpose(1, 0, 2).reshape(D, S).T)[None]
```
